# Optimizing a Trainium2 kernel written in Bass

```python
import jax, jax.numpy as jnp
from jax import lax
import numpy as np

D_MODEL = 1024
BATCH = 1
SEQ = 512
DEPTH = 2

RW_HEADS = 8
RW_HEAD_DIM = 64
RW_WIDTH = RW_HEADS * RW_HEAD_DIM
RW_DECAY_RANK = 64
RW_ICLR_RANK = 64
RW_GATE_RANK = 128
RW_COLS = 3 * RW_WIDTH + RW_DECAY_RANK + RW_ICLR_RANK + RW_GATE_RANK
RW_GN_EPS = 64e-5
RET_HEADS = 4
RET_QK_DIM = 64
RET_V_DIM = 128
RET_QK_WIDTH = RET_HEADS * RET_QK_DIM
RET_V_WIDTH = RET_HEADS * RET_V_DIM
RET_COLS = 2 * RET_QK_WIDTH + 2 * RET_V_WIDTH
RET_CHUNK = 128
ROPE_BASE = 10000.0
SG_GROUPS = 4
SG_CHUNK = 128
SG_WIDTH = 512
SG_GROUP_DIM = SG_WIDTH // SG_GROUPS
SG_COLS = 2 * SG_WIDTH
N_BRANCH = 3
BRANCH_WIDTH = 512
GATE_COLS = N_BRANCH * D_MODEL
IN_COLS = RW_COLS + RET_COLS + SG_COLS + GATE_COLS
D_FF = 2816
CONV_WIDTH = 3
EPS = 1e-6


def rmsnorm(x, g):
    xf = x.astype(jnp.float32)
    y = xf * lax.rsqrt(jnp.mean(xf * xf, axis=-1, keepdims=True) + EPS) * g.astype(jnp.float32)
    return y.astype(x.dtype)

def rwkv7_scan(r, w, k, v, kk, a):
    B, S, H, N = r.shape

    def step(state, inp):
        r_t, w_t, k_t, v_t, kk_t, a_t = inp
        sa = jnp.einsum('bhvk,bhk->bhv', state, -kk_t)
        state = (state * w_t[:, :, None, :]
                 + sa[..., None] * (kk_t * a_t)[:, :, None, :]
                 + v_t[..., None] * k_t[:, :, None, :])
        y = jnp.einsum('bhvk,bhk->bhv', state, r_t)
        return state, y

    xs = tuple(jnp.moveaxis(t.astype(jnp.float32), 1, 0) for t in (r, w, k, v, kk, a))
    s0 = jnp.zeros((B, H, N, N), jnp.float32)
    _, ys = lax.scan(step, s0, xs)
    return jnp.moveaxis(ys, 0, 1)

def rwkv7_branch(p, mu, w0, w_up, a0, a_up, g_up, k_k, k_a, r_k, lnx_g, lnx_b):
    B, S, _ = p.shape
    p_prev = jnp.pad(p, ((0, 0), (1, 0), (0, 0)))[:, :S]
    p = p + mu * (p_prev - p)
    cuts = [RW_WIDTH, 2 * RW_WIDTH, 3 * RW_WIDTH, 3 * RW_WIDTH + RW_DECAY_RANK,
            3 * RW_WIDTH + RW_DECAY_RANK + RW_ICLR_RANK]
    r, k, v, wd, ad, gd = jnp.split(p, cuts, axis=-1)
    w = -jax.nn.softplus(-(w0 + jnp.tanh(wd) @ w_up)) - 0.5
    decay = jnp.exp(-jnp.exp(w.astype(jnp.float32)))
    a = jax.nn.sigmoid(a0 + ad @ a_up)
    g = jax.nn.sigmoid(gd) @ g_up
    kk = (k * k_k).astype(jnp.float32)
    k = k * (1.0 + (a - 1.0) * k_a)

    def heads(t):
        return t.reshape(B, S, RW_HEADS, RW_HEAD_DIM)

    r, k, v, decay, a, kk = map(heads, (r, k, v, decay, a, kk))
    kk = kk / jnp.maximum(jnp.sqrt(jnp.sum(kk * kk, axis=-1, keepdims=True)), 1e-12)
    y = rwkv7_scan(r, decay, k, v, kk, a)
    mean = jnp.mean(y, axis=-1, keepdims=True)
    var = jnp.mean(jnp.square(y - mean), axis=-1, keepdims=True)
    y = (y - mean) * lax.rsqrt(var + RW_GN_EPS) * lnx_g + lnx_b
    y = y + jnp.sum(r * k * r_k, axis=-1, keepdims=True) * v
    return (y.reshape(B, S, RW_WIDTH) * g).astype(p.dtype)

def rotary(t, cos, sin):
    t1, t2 = jnp.split(t, 2, axis=-1)
    c = cos[None, :, None, :]
    s = sin[None, :, None, :]
    return jnp.concatenate([t1 * c - t2 * s, t2 * c + t1 * s], axis=-1)

def retention_branch(p, cos, sin):
    B, S, _ = p.shape
    nC = S // RET_CHUNK
    q, k, v, g = jnp.split(p, [RET_QK_WIDTH, 2 * RET_QK_WIDTH, 2 * RET_QK_WIDTH + RET_V_WIDTH], axis=-1)
    q = rotary(q.reshape(B, S, RET_HEADS, RET_QK_DIM), cos, sin)
    k = rotary(k.reshape(B, S, RET_HEADS, RET_QK_DIM), cos, sin) * (RET_QK_DIM ** -0.5)
    v = v.reshape(B, S, RET_HEADS, RET_V_DIM)

    def chunks(t):
        return t.reshape(B, nC, RET_CHUNK, RET_HEADS, t.shape[-1]).transpose(0, 3, 1, 2, 4)

    qc, kc, vc = chunks(q), chunks(k), chunks(v)
    log_gamma = jnp.log(1.0 - 2.0 ** (-5.0 - jnp.arange(RET_HEADS, dtype=jnp.float32)))
    pos = jnp.arange(RET_CHUNK, dtype=jnp.float32)
    diff = pos[:, None] - pos[None, :]
    decay_in = jnp.where(diff[None] >= 0,
                         jnp.exp(jnp.maximum(diff, 0.0)[None] * log_gamma[:, None, None]), 0.0)
    scores = jnp.einsum('bhnid,bhnjd->bhnij', qc, kc) * decay_in[:, None]
    inner = jnp.einsum('bhnij,bhnje->bhnie', scores, vc)
    k_dec = jnp.exp((RET_CHUNK - 1.0 - pos)[None] * log_gamma[:, None])
    kv = jnp.einsum('bhnjd,bhnje,hj->nbhde', kc, vc, k_dec).astype(jnp.float32)
    chunk_decay = jnp.exp(RET_CHUNK * log_gamma)[None, :, None, None]

    def step(R, kv_n):
        return R * chunk_decay + kv_n, R

    _, R_prev = lax.scan(step, jnp.zeros((B, RET_HEADS, RET_QK_DIM, RET_V_DIM), jnp.float32), kv)
    q_dec = jnp.exp((pos + 1.0)[None] * log_gamma[:, None])
    cross = jnp.einsum('bhnid,nbhde,hi->bhnie', qc, R_prev, q_dec)
    y = (inner + cross).transpose(0, 2, 3, 1, 4).reshape(B, S, RET_HEADS, RET_V_DIM)
    y = y * lax.rsqrt(jnp.mean(y * y, axis=-1, keepdims=True) + EPS)
    return (y.reshape(B, S, RET_V_WIDTH) * jax.nn.silu(g)).astype(p.dtype)

def sgu_branch(p, ln_g, ln_b, w_s, b_s):
    B, S, _ = p.shape
    nC = S // SG_CHUNK
    z = jax.nn.gelu(p, approximate=False)
    u, v = jnp.split(z, 2, axis=-1)
    vf = v.astype(jnp.float32)
    mean = jnp.mean(vf, axis=-1, keepdims=True)
    var = jnp.mean(jnp.square(vf - mean), axis=-1, keepdims=True)
    v = ((vf - mean) * lax.rsqrt(var + EPS) * ln_g + ln_b).astype(p.dtype)
    vc = v.reshape(B, nC, SG_CHUNK, SG_GROUPS, SG_GROUP_DIM)
    causal = jnp.tril(jnp.ones((SG_CHUNK, SG_CHUNK), dtype=bool))
    w = jnp.where(causal[None], w_s, 0.0)
    mixed = jnp.einsum('gij,bnjgd->bnigd', w, vc) + b_s.T[:, :, None]
    return u * mixed.reshape(B, S, SG_WIDTH)

def conv_ffn(h, w_up, conv_w, conv_b, w_down):
    S = h.shape[1]
    u = h @ w_up
    up = jnp.pad(u, ((0, 0), (CONV_WIDTH - 1, 0), (0, 0)))
    c = conv_b
    for j in range(CONV_WIDTH):
        c = c + conv_w[j] * up[:, j:j + S]
    gate, val = jnp.split(c, 2, axis=-1)
    return (jax.nn.silu(gate) * val) @ w_down

def _normal(k, shape, scale):
    return scale * jax.random.normal(k, shape, jnp.float32)

def first_inputs(seed: int = 0) -> dict:
    key = jax.random.key(seed)
    ks = jax.random.split(key, 32)
    L = DEPTH
    f32 = jnp.float32
    return {
        "x": jax.random.normal(ks[0], (BATCH, SEQ, D_MODEL), f32),
        "norm1_g": 1.0 + _normal(ks[1], (L, D_MODEL), 0.05),
        "w_in": _normal(ks[2], (L, D_MODEL, IN_COLS), D_MODEL ** -0.5),
        "rw_mu": jax.random.uniform(ks[3], (L, RW_COLS), f32),
        "rw_w0": jax.random.uniform(ks[4], (L, RW_WIDTH), f32, -6.0, 1.0),
        "rw_w_up": _normal(ks[5], (L, RW_DECAY_RANK, RW_WIDTH), 0.1 * RW_DECAY_RANK ** -0.5),
        "rw_a0": _normal(ks[6], (L, RW_WIDTH), 0.1),
        "rw_a_up": _normal(ks[7], (L, RW_ICLR_RANK, RW_WIDTH), 0.3 * RW_ICLR_RANK ** -0.5),
        "rw_g_up": _normal(ks[8], (L, RW_GATE_RANK, RW_WIDTH), RW_GATE_RANK ** -0.5),
        "rw_k_k": 0.85 + _normal(ks[9], (L, RW_WIDTH), 0.05),
        "rw_k_a": 1.0 + _normal(ks[10], (L, RW_WIDTH), 0.05),
        "rw_r_k": _normal(ks[11], (L, RW_HEADS, RW_HEAD_DIM), 0.1),
        "rw_lnx_g": 1.0 + _normal(ks[12], (L, RW_HEADS, RW_HEAD_DIM), 0.05),
        "rw_lnx_b": _normal(ks[13], (L, RW_HEADS, RW_HEAD_DIM), 0.02),
        "sg_ln_g": 1.0 + _normal(ks[14], (L, SG_WIDTH), 0.05),
        "sg_ln_b": _normal(ks[15], (L, SG_WIDTH), 0.02),
        "sg_w_s": _normal(ks[16], (L, SG_GROUPS, SG_CHUNK, SG_CHUNK), SG_CHUNK ** -0.5),
        "sg_b": 1.0 + _normal(ks[17], (L, SG_GROUPS, SG_CHUNK), 0.1),
        "w_branch": _normal(ks[18], (L, N_BRANCH, BRANCH_WIDTH, D_MODEL), BRANCH_WIDTH ** -0.5),
        "w_out": _normal(ks[19], (L, D_MODEL, D_MODEL), 0.5 * D_MODEL ** -0.5),
        "norm2_g": 1.0 + _normal(ks[20], (L, D_MODEL), 0.05),
        "ffn_w_up": _normal(ks[21], (L, D_MODEL, 2 * D_FF), D_MODEL ** -0.5),
        "ffn_conv_w": _normal(ks[22], (L, CONV_WIDTH, 2 * D_FF), CONV_WIDTH ** -0.5),
        "ffn_conv_b": _normal(ks[23], (L, 2 * D_FF), 0.02),
        "ffn_w_down": _normal(ks[24], (L, D_FF, D_MODEL), 0.5 * D_FF ** -0.5),
        "final_g": 1.0 + _normal(ks[25], (D_MODEL,), 0.05),
    }

def first_block(x, norm1_g, w_in, rw_mu, rw_w0, rw_w_up, rw_a0, rw_a_up, rw_g_up, rw_k_k, rw_k_a,
              rw_r_k, rw_lnx_g, rw_lnx_b, sg_ln_g, sg_ln_b, sg_w_s, sg_b, w_branch, w_out,
              norm2_g, ffn_w_up, ffn_conv_w, ffn_conv_b, ffn_w_down, final_g):
    B, S, _ = x.shape
    inv_freq = 1.0 / (ROPE_BASE ** jnp.linspace(0.0, 1.0, RET_QK_DIM // 2, dtype=jnp.float32))
    ang = jnp.arange(S, dtype=jnp.float32)[:, None] * inv_freq[None, :]
    cos, sin = jnp.cos(ang), jnp.sin(ang)
    in_cuts = [RW_COLS, RW_COLS + RET_COLS, RW_COLS + RET_COLS + SG_COLS]
    for l in range(DEPTH):
        h = rmsnorm(x, norm1_g[l])
        p = h @ w_in[l]
        p_rw, p_ret, p_sg, gate_logits = jnp.split(p, in_cuts, axis=-1)
        y_rw = rwkv7_branch(p_rw, rw_mu[l], rw_w0[l], rw_w_up[l], rw_a0[l], rw_a_up[l], rw_g_up[l],
                            rw_k_k[l], rw_k_a[l], rw_r_k[l], rw_lnx_g[l], rw_lnx_b[l])
        y_ret = retention_branch(p_ret, cos, sin)
        y_sg = sgu_branch(p_sg, sg_ln_g[l], sg_ln_b[l], sg_w_s[l], sg_b[l])
        branches = jnp.stack([y_rw, y_ret, y_sg], axis=2)
        proj = jnp.einsum('bsgc,gcd->bsgd', branches, w_branch[l])
        gates = jax.nn.sigmoid(gate_logits.reshape(B, S, N_BRANCH, D_MODEL))
        x = x + jnp.sum(gates * proj, axis=2) @ w_out[l]
        x = x + conv_ffn(rmsnorm(x, norm2_g[l]), ffn_w_up[l], ffn_conv_w[l], ffn_conv_b[l], ffn_w_down[l])
    return rmsnorm(x, final_g)


DEPTH_2 = 1

MEM_LEN = 256
HEAD_DIM = 64
CONV_CH = D_MODEL // 4
ATTN_HEADS = (3 * D_MODEL // 4) // HEAD_DIM
ATTN_WIDTH = ATTN_HEADS * HEAD_DIM
MIX_WIDTH = CONV_CH + ATTN_WIDTH
IN_WIDTH = 2 * CONV_CH + 3 * ATTN_WIDTH
CONV_KERNEL = 31
DILATED_BRANCHES = ((128, 1), (512, 4), (2048, 16))
ROPE_THETA = 10000.0
MEM_HEADS = 4
MEM_HEAD_DIM = D_MODEL // MEM_HEADS
N_GROUPS = 4
EXPERTS_PER_GROUP = 8
N_EXPERTS = N_GROUPS * EXPERTS_PER_GROUP
TOP_K = 2
EXPERT_FF = D_MODEL // 2
DISPATCH_BLOCK = 256
NORM_EPS = 1e-6
LN_EPS = 1e-5


def rms_norm(t, g):
    tf = t.astype(jnp.float32)
    y = tf * lax.rsqrt(jnp.mean(tf * tf, axis=-1, keepdims=True) + NORM_EPS)
    return (y * g.astype(jnp.float32)).astype(t.dtype)

def layer_norm(t, g, b):
    tf = t.astype(jnp.float32)
    mu = jnp.mean(tf, axis=-1, keepdims=True)
    var = jnp.mean(jnp.square(tf - mu), axis=-1, keepdims=True)
    y = (tf - mu) * lax.rsqrt(var + LN_EPS)
    return (y * g.astype(jnp.float32) + b.astype(jnp.float32)).astype(t.dtype)

def rotary_2(t, positions):
    half = t.shape[-1] // 2
    inv = 1.0 / (ROPE_THETA ** (jnp.arange(half, dtype=jnp.float32) * (2.0 / t.shape[-1])))
    ang = positions.astype(jnp.float32)[:, None] * inv[None, :]
    cos, sin = jnp.cos(ang), jnp.sin(ang)
    t1, t2 = t[..., :half], t[..., half:]
    return jnp.concatenate([t1 * cos - t2 * sin, t1 * sin + t2 * cos], axis=-1)

def conformer_conv(conv_in, dw_w, dw_b, ln_g, ln_b):
    a, gate = conv_in[..., :CONV_CH], conv_in[..., CONV_CH:]
    c = a * jax.nn.sigmoid(gate)
    pad = CONV_KERNEL // 2
    c = lax.conv_general_dilated(
        c, dw_w.reshape(CONV_KERNEL, 1, CONV_CH).astype(c.dtype),
        window_strides=(1,), padding=[(pad, pad)],
        dimension_numbers=('NWC', 'WIO', 'NWC'),
        feature_group_count=CONV_CH) + dw_b.astype(c.dtype)
    c = layer_norm(c, ln_g, ln_b)
    return jax.nn.silu(c)

def dilated_branch(q, k, v, window, dilation):
    B_, H, S_, Dh = q.shape
    half = window // (2 * dilation)
    blk = half
    L = S_ // dilation
    nb = -(-L // blk)
    Lp = nb * blk
    pad = Lp - L

    def to_sub(t):
        return t.reshape(B_, H, L, dilation, Dh).transpose(0, 1, 3, 2, 4)

    qs, ks, vs = to_sub(q), to_sub(k), to_sub(v)
    qs = jnp.pad(qs, ((0, 0), (0, 0), (0, 0), (0, pad), (0, 0)))
    kp = jnp.pad(ks, ((0, 0), (0, 0), (0, 0), (blk, pad + blk), (0, 0)))
    vp = jnp.pad(vs, ((0, 0), (0, 0), (0, 0), (blk, pad + blk), (0, 0)))
    qb = qs.reshape(B_, H, dilation, nb, blk, Dh)
    kb = kp.reshape(B_, H, dilation, nb + 2, blk, Dh)
    vb = vp.reshape(B_, H, dilation, nb + 2, blk, Dh)
    kw = jnp.concatenate([kb[:, :, :, :-2], kb[:, :, :, 1:-1], kb[:, :, :, 2:]], axis=-2)
    vw = jnp.concatenate([vb[:, :, :, :-2], vb[:, :, :, 1:-1], vb[:, :, :, 2:]], axis=-2)

    qi = np.arange(nb)[:, None] * blk + np.arange(blk)[None, :]
    ki = np.arange(nb)[:, None] * blk - blk + np.arange(3 * blk)[None, :]
    valid = ((np.abs(qi[:, :, None] - ki[:, None, :]) <= half)
             & (ki[:, None, :] >= 0) & (ki[:, None, :] < L))

    s = jnp.einsum('bhrnqd,bhrnkd->bhrnqk', qb, kw) * (HEAD_DIM ** -0.5)
    s = jnp.where(jnp.asarray(valid), s, -jnp.inf)
    m = jnp.max(s, axis=-1)
    p = jnp.exp(s - m[..., None])
    den = jnp.sum(p, axis=-1)
    num = jnp.einsum('bhrnqk,bhrnkd->bhrnqd', p, vw)

    def back(t):
        tail = tuple(t.shape[5:])
        t = t.reshape((B_, H, dilation, Lp) + tail)[:, :, :, :L]
        perm = (0, 1, 3, 2) + tuple(range(4, 4 + len(tail)))
        return t.transpose(perm).reshape((B_, H, S_) + tail)

    return back(num), back(m), back(den)

def dilated_attention(q, k, v, positions):
    B_, H, S_, Dh = q.shape
    out_dtype = q.dtype
    qf = rotary_2(q.astype(jnp.float32), positions)
    kf = rotary_2(k.astype(jnp.float32), positions)
    vf = v.astype(jnp.float32)
    num_acc = den_acc = m_acc = None
    for window, dilation in DILATED_BRANCHES:
        num, m, den = dilated_branch(qf, kf, vf, window, dilation)
        if m_acc is None:
            num_acc, den_acc, m_acc = num, den, m
        else:
            m_new = jnp.maximum(m_acc, m)
            a = jnp.exp(m_acc - m_new)
            b = jnp.exp(m - m_new)
            num_acc = num_acc * a[..., None] + num * b[..., None]
            den_acc = den_acc * a + den * b
            m_acc = m_new
    o = num_acc / den_acc[..., None]
    return o.transpose(0, 2, 1, 3).reshape(B_, S_, H * Dh).astype(out_dtype)

def memory_cross_attention(h, mem_n, w_q, w_k, w_v, w_o):
    B_, S_, D = h.shape
    q = (h @ w_q).reshape(B_, S_, MEM_HEADS, MEM_HEAD_DIM)
    k = (mem_n @ w_k).reshape(B_, -1, MEM_HEADS, MEM_HEAD_DIM)
    v = (mem_n @ w_v).reshape(B_, -1, MEM_HEADS, MEM_HEAD_DIM)
    s = jnp.einsum('bshd,bmhd->bhsm', q, k, preferred_element_type=jnp.float32) * (MEM_HEAD_DIM ** -0.5)
    p = jax.nn.softmax(s, axis=-1).astype(v.dtype)
    o = jnp.einsum('bhsm,bmhd->bshd', p, v).reshape(B_, S_, D)
    return o @ w_o

def hierarchical_moe(h, w_group, b_group, w_router, b_router, w1, w3, w2):
    B_, S_, D = h.shape
    T = B_ * S_
    hf = h.reshape(T, D)
    gl = (hf @ w_group + b_group).astype(jnp.float32)
    gp = jax.nn.softmax(gl, axis=-1)
    _, g_sel = lax.top_k(gl, 1)
    g_idx = g_sel[:, 0]
    tok_idx = jnp.arange(T, dtype=jnp.int32)
    p_g = gp[tok_idx, g_idx]
    el = (hf @ w_router + b_router).astype(jnp.float32).reshape(T, N_GROUPS, EXPERTS_PER_GROUP)
    el_sel = el[tok_idx, g_idx]
    top_v, top_i = lax.top_k(el_sel, TOP_K)
    gates = p_g[:, None] * jax.nn.softmax(top_v, axis=-1)
    expert_ids = g_idx[:, None] * EXPERTS_PER_GROUP + top_i

    A = T * TOP_K
    flat_e = expert_ids.reshape(A).astype(jnp.int32)
    flat_t = jnp.repeat(tok_idx, TOP_K)
    flat_g = gates.reshape(A)
    order = jnp.argsort(flat_e)
    se, st, sg = flat_e[order], flat_t[order], flat_g[order]
    counts = jnp.bincount(flat_e, length=N_EXPERTS).astype(jnp.int32)
    starts = jnp.cumsum(counts) - counts
    pcounts = (counts + DISPATCH_BLOCK - 1) // DISPATCH_BLOCK * DISPATCH_BLOCK
    pstarts = jnp.cumsum(pcounts) - pcounts
    dest = pstarts[se] + jnp.arange(A, dtype=jnp.int32) - starts[se]
    P = (-(-A // DISPATCH_BLOCK) + N_EXPERTS) * DISPATCH_BLOCK
    n_blk = P // DISPATCH_BLOCK
    row_tok = jnp.full((P,), T, dtype=jnp.int32).at[dest].set(st)
    row_gate = jnp.zeros((P,), jnp.float32).at[dest].set(sg)
    blk_e = jnp.minimum(
        jnp.searchsorted(pstarts + pcounts, jnp.arange(n_blk, dtype=jnp.int32) * DISPATCH_BLOCK,
                         side='right'),
        N_EXPERTS - 1).astype(jnp.int32)
    x_rows = jnp.concatenate([hf, jnp.zeros((1, D), hf.dtype)], axis=0)[row_tok]
    x_blocks = x_rows.reshape(n_blk, DISPATCH_BLOCK, D)

    def expert_block(args):
        xb, e = args
        return (jax.nn.silu(xb @ w1[e]) * (xb @ w3[e])) @ w2[e]

    y_rows = lax.map(expert_block, (x_blocks, blk_e)).reshape(P, D)
    y = jax.ops.segment_sum(y_rows * row_gate[:, None].astype(y_rows.dtype), row_tok,
                            num_segments=T + 1)[:T]
    return y.reshape(B_, S_, D)

def second_inputs(seed: int = 0) -> dict:
    key = jax.random.key(seed)
    ks = jax.random.split(key, 26)
    f32 = jnp.float32
    D = D_MODEL

    def nrm(k, shape, scale):
        return jax.random.normal(k, shape, f32) * scale

    def gain(k, shape):
        return 1.0 + 0.02 * jax.random.normal(k, shape, f32)

    return {
        'x': jax.random.normal(ks[0], (BATCH, SEQ, D), f32),
        'mem': jax.random.normal(ks[1], (BATCH, MEM_LEN, D), f32),
        'positions': jnp.arange(SEQ, dtype=jnp.int32),
        'mix_norm_g': gain(ks[2], (DEPTH_2, D)),
        'w_in': nrm(ks[3], (DEPTH_2, D, IN_WIDTH), D ** -0.5),
        'conv_dw_w': nrm(ks[4], (DEPTH_2, CONV_KERNEL, CONV_CH), CONV_KERNEL ** -0.5),
        'conv_dw_b': nrm(ks[5], (DEPTH_2, CONV_CH), 0.02),
        'conv_ln_g': gain(ks[6], (DEPTH_2, CONV_CH)),
        'conv_ln_b': nrm(ks[7], (DEPTH_2, CONV_CH), 0.02),
        'conv_out_g': gain(ks[8], (DEPTH_2, CONV_CH)),
        'attn_out_g': gain(ks[9], (DEPTH_2, ATTN_WIDTH)),
        'w_out': nrm(ks[10], (DEPTH_2, MIX_WIDTH, D), MIX_WIDTH ** -0.5),
        'xattn_norm_g': gain(ks[11], (DEPTH_2, D)),
        'mem_norm_g': gain(ks[12], (DEPTH_2, D)),
        'w_xq': nrm(ks[13], (DEPTH_2, D, D), D ** -0.5),
        'w_xk': nrm(ks[14], (DEPTH_2, D, D), D ** -0.5),
        'w_xv': nrm(ks[15], (DEPTH_2, D, D), D ** -0.5),
        'w_xo': nrm(ks[16], (DEPTH_2, D, D), D ** -0.5),
        'moe_norm_g': gain(ks[17], (DEPTH_2, D)),
        'w_group': nrm(ks[18], (DEPTH_2, D, N_GROUPS), D ** -0.5),
        'b_group': nrm(ks[19], (DEPTH_2, N_GROUPS), 0.01),
        'w_router': nrm(ks[20], (DEPTH_2, D, N_EXPERTS), D ** -0.5),
        'b_router': nrm(ks[21], (DEPTH_2, N_EXPERTS), 0.01),
        'w1': nrm(ks[22], (DEPTH_2, N_EXPERTS, D, EXPERT_FF), D ** -0.5),
        'w3': nrm(ks[23], (DEPTH_2, N_EXPERTS, D, EXPERT_FF), D ** -0.5),
        'w2': nrm(ks[24], (DEPTH_2, N_EXPERTS, EXPERT_FF, D), EXPERT_FF ** -0.5),
        'final_norm_g': gain(ks[25], (D,)),
    }

def second_block(x, mem, positions, mix_norm_g, w_in, conv_dw_w, conv_dw_b, conv_ln_g, conv_ln_b,
              conv_out_g, attn_out_g, w_out, xattn_norm_g, mem_norm_g, w_xq, w_xk, w_xv, w_xo,
              moe_norm_g, w_group, b_group, w_router, b_router, w1, w3, w2, final_norm_g):
    B_, S_, _ = x.shape
    for l in range(DEPTH_2):
        h = rms_norm(x, mix_norm_g[l])
        u = h @ w_in[l]
        conv_in = u[..., :2 * CONV_CH]
        qkv = u[..., 2 * CONV_CH:].reshape(B_, S_, 3, ATTN_HEADS, HEAD_DIM).transpose(2, 0, 3, 1, 4)
        c = conformer_conv(conv_in, conv_dw_w[l], conv_dw_b[l], conv_ln_g[l], conv_ln_b[l])
        a = dilated_attention(qkv[0], qkv[1], qkv[2], positions)
        mixed = jnp.concatenate([rms_norm(c, conv_out_g[l]), rms_norm(a, attn_out_g[l])], axis=-1)
        x = x + mixed @ w_out[l]
        h = rms_norm(x, xattn_norm_g[l])
        m = rms_norm(mem, mem_norm_g[l])
        x = x + memory_cross_attention(h, m, w_xq[l], w_xk[l], w_xv[l], w_xo[l])
        h = rms_norm(x, moe_norm_g[l])
        x = x + hierarchical_moe(h, w_group[l], b_group[l], w_router[l], b_router[l], w1[l], w3[l], w2[l])
    return rms_norm(x, final_norm_g)


def setup_inputs(seed=0):
    out = dict(first_inputs(seed))
    for name, value in second_inputs(seed + 1).items():
        if name != "x":
            out[name + "_2"] = value
    return out


def reference(
    x, norm1_g, w_in, rw_mu, rw_w0, rw_w_up, rw_a0, rw_a_up, rw_g_up, rw_k_k, rw_k_a, rw_r_k,
    rw_lnx_g, rw_lnx_b, sg_ln_g, sg_ln_b, sg_w_s, sg_b, w_branch, w_out, norm2_g, ffn_w_up,
    ffn_conv_w, ffn_conv_b, ffn_w_down, final_g, mem_2, positions_2, mix_norm_g_2, w_in_2,
    conv_dw_w_2, conv_dw_b_2, conv_ln_g_2, conv_ln_b_2, conv_out_g_2, attn_out_g_2, w_out_2,
    xattn_norm_g_2, mem_norm_g_2, w_xq_2, w_xk_2, w_xv_2, w_xo_2, moe_norm_g_2, w_group_2,
    b_group_2, w_router_2, b_router_2, w1_2, w3_2, w2_2, final_norm_g_2,
):
    x = first_block(
        x, norm1_g, w_in, rw_mu, rw_w0, rw_w_up, rw_a0, rw_a_up, rw_g_up, rw_k_k, rw_k_a,
        rw_r_k, rw_lnx_g, rw_lnx_b, sg_ln_g, sg_ln_b, sg_w_s, sg_b, w_branch, w_out, norm2_g,
        ffn_w_up, ffn_conv_w, ffn_conv_b, ffn_w_down, final_g,
    )
    return second_block(
        x, mem_2, positions_2, mix_norm_g_2, w_in_2, conv_dw_w_2, conv_dw_b_2, conv_ln_g_2,
        conv_ln_b_2, conv_out_g_2, attn_out_g_2, w_out_2, xattn_norm_g_2, mem_norm_g_2, w_xq_2,
        w_xk_2, w_xv_2, w_xo_2, moe_norm_g_2, w_group_2, b_group_2, w_router_2, b_router_2,
        w1_2, w3_2, w2_2, final_norm_g_2,
    )


_drawn_inputs = setup_inputs


def setup_inputs(seed=0):
    import zlib

    import numpy as np

    out = dict(_drawn_inputs(seed))
    spreads = {}
    factors = {'rw_w_up': 8.0,
     'rw_a0': 2.961,
     'rw_k_k': 3.79,
     'rw_k_a': 2.928,
     'rw_lnx_g': 2.936,
     'sg_ln_g': 3.261,
     'sg_ln_b': 5.347,
     'conv_ln_g_2': 3.464,
     'conv_ln_b_2': 4.935,
     'conv_out_g_2': 4.209,
     'xattn_norm_g_2': 8.0,
     'mem_norm_g_2': 8.0,
     'b_group_2': 26.408,
     'b_router_2': 58.08,
     'final_norm_g_2': 7.918,
     'moe_norm_g_2': 8.0}
    for name, (base, spread) in spreads.items():
        noise = np.random.default_rng([zlib.crc32(name.encode()), seed]).standard_normal(out[name].shape)
        drawn = base * np.exp(spread * noise) if base else spread * noise
        out[name] = __import__('jax').numpy.asarray(drawn.astype(out[name].dtype))
    for name, factor in factors.items():
        out[name] = (out[name] * factor).astype(out[name].dtype)
    return out
```

```python
from contextlib import ExitStack

import numpy as np

import concourse.bass as bass
from concourse import mybir

F32 = mybir.dt.float32
ALU = mybir.AluOpType
ACT = mybir.ActivationFunctionType
AX = mybir.AxisListType

P = 128
D = 1024
S = 512
KD = D // P
DEPTH = 2
RW_W = 512
RW_T = 14
PAIRS = RW_W // P
C = 64
NCH = S // C
LEVELS = 5
GN_EPS = 64e-5
LN_EPS = 1e-5
EPS = 1e-6
DECAY = float(np.exp(-0.5))
RET_HEADS = 4
SG_GROUPS = 4
D_FF = 2816
FT = D_FF // P
CONV_CH = 256
CONV_KERNEL = 31
HEAD_DIM = 64
ATT_W = 768
MEM_LEN = 256
N_GROUPS = 4
N_EXPERTS = 32
SLOTS = 64
MOE_ROUNDS = S // SLOTS
BIG = 16384.0
TWO_PI = (6.28125, 0.0019353032, 2 * np.pi - 6.28125 - 0.0019353032)
ds = bass.ds

LCOLS = {}
_n = 0
for _name, _k in (("norm1_g", 8), ("mu", 14), ("w0", 4), ("a0", 4), ("k_k", 4), ("k_a", 4), ("r_k", 4),
                  ("lnx_g", 4), ("lnx_b", 4), ("norm2_g", 8)):
    LCOLS[_name] = (_n, _n + _k)
    _n += _k
NLCOL = _n

GCOLS = {}
_n = 0
for _name, _k in (("final_g", 8), ("mix_norm_g_2", 8), ("conv_out_g_2", 2), ("attn_out_g_2", 6),
                  ("xattn_norm_g_2", 8), ("mem_norm_g_2", 8), ("moe_norm_g_2", 8), ("final_norm_g_2", 8)):
    GCOLS[_name] = (_n, _n + _k)
    _n += _k
NGCOL = _n


class Chain:

    def __init__(self, eng, sem):
        self.eng, self.sem, self.n = eng, sem, 0

    def __call__(self, ins):
        self.n += 1
        ins.then_inc(self.sem, 1)
        self.eng.wait_ge(self.sem, self.n)

    def restart(self):
        self.eng.sem_clear(self.sem)
        self.n = 0


def two_slots(eng, n):
    if n // 2:
        with eng.Fori(0, n // 2) as i:
            for s in (0, 1):
                yield i, s
    if n % 2:
        yield n // 2, 0


def flat(ap):
    return ap.rearrange("p a b -> p (a b)")


class Named:
    pass


def clear(sync, sems):
    for s in sems["all"]:
        sync.sem_clear(s)


def sem_set(nc, ctx, prefix, names):
    named, every = {}, []
    for n in names.split():
        n, _, k = n.partition("*")
        made = [ctx.enter_context(nc.semaphore(f"{prefix}_{n}{i if k else ''}")) for i in range(int(k or 1))]
        named[n] = made if k else made[0]
        every += made
    return {"all": every, **named}


def rsqrt(act, sem, before, out, sums, scale, eps):
    act.activation(out, sums, ACT.Ln, bias=eps, scale=scale).then_inc(sem, 1)
    act.wait_ge(sem, before + 1)
    act.activation(out, out, ACT.Exp, scale=-0.5).then_inc(sem, 1)


NORM_SEMS = "loaded squared summed rooted"


def norm_phase(nc, T, sems, stale, src, gain, dst, tiles=KD, width=S, eps=EPS, load=None, mean_of=None):
    n_feat = (mean_of or tiles * P)
    with nc.sbuf_tensor([P, tiles, width], F32) as sq, nc.sbuf_tensor([P, width], F32) as rstd, \
            nc.Block() as block:
        @block.sync
        def _(sync):
            clear(sync, stale)
            if load is not None:
                load(sync, sems["loaded"])

        @block.scalar
        def _(act):
            if load is not None:
                act.wait_ge(sems["loaded"], 16)
            for k in range(tiles):
                nc.scalar.activation(sq[:, k, :], src[:, k, :], ACT.Square).then_inc(sems["squared"], 1)
            act.wait_ge(sems["summed"], 1)
            rsqrt(act, sems["rooted"], 0, rstd[:, :], T.ps[0][:, 0:width], 1.0 / n_feat, T.eps(eps))

        @block.tensor
        def _(pe):
            for k in range(tiles):
                pe.wait_ge(sems["squared"], k + 1)
                mm = nc.tensor.matmul(T.ps[0][:, 0:width], T.ones[:, :], sq[:, k, :], start=(k == 0),
                                      stop=(k == tiles - 1))
            mm.then_inc(sems["summed"], 1)

        @block.vector
        def _(dve):
            if load is not None:
                dve.wait_ge(sems["loaded"], 16)
            dve.wait_ge(sems["rooted"], 2)
            for k in range(tiles):
                nc.vector.scalar_tensor_tensor(out=dst[:, k, :], in0=src[:, k, :], scalar=gain[:, k:k + 1],
                                               in1=rstd[:, :], op0=ALU.mult, op1=ALU.mult)


PROJECT_SEMS = "loaded w_full*2 act_took dve_took even_done odd_done"


def project_phase(nc, T, sems, stale, weights, chunks, rhs, write, kt=KD, width=S, load=None):
    with nc.Block() as block:
        @block.sync
        def _(sync):
            clear(sync, stale)
            if load is not None:
                load(sync, sems["loaded"])
            for i, s in two_slots(sync, chunks):
                sync.wait_ge(sems["dve_took"], 2 * i + s + 1)
                sync.dma_start(T.w[:, s, 0:kt * 256], weights(2 * i + s)).then_inc(sems["w_full"][s], 16)

        @block.tensor
        def _(pe):
            for i, s in two_slots(pe, chunks):
                pe.wait_ge(sems["w_full"][s], 16 * i + 16)
                for t in range(2):
                    pe.wait_ge((sems["act_took"], sems["dve_took"])[t], 2 * i + s + 1)
                    for k in range(kt):
                        mm = nc.tensor.matmul(T.ps[2 * s + t][:, 0:width],
                                              T.w[:, s, k * 256 + t * P:k * 256 + t * P + P], rhs[:, k, :],
                                              start=(k == 0), stop=(k == kt - 1))
                    mm.then_inc((sems["even_done"], sems["odd_done"])[t], 1)

        @block.scalar
        def _(act):
            act.sem_inc(sems["act_took"], 2)
            if load is not None:
                act.wait_ge(sems["loaded"], 16)
            for i, s in two_slots(act, chunks):
                act.wait_ge(sems["even_done"], 2 * i + s + 1)
                write(nc.scalar, 2 * i + s, 0, T.ps[2 * s][:, 0:width]).then_inc(sems["act_took"], 1)

        @block.vector
        def _(dve):
            dve.sem_inc(sems["dve_took"], 2)
            if load is not None:
                dve.wait_ge(sems["loaded"], 16)
            for i, s in two_slots(dve, chunks):
                dve.wait_ge(sems["odd_done"], 2 * i + s + 1)
                write(nc.vector, 2 * i + s, 1, T.ps[2 * s + 1][:, 0:width]).then_inc(sems["dve_took"], 1)


def token_project_phase(nc, T, sems, stale, weights, chunks, lhs, write, tiles=4):
    with nc.Block() as block:
        @block.sync
        def _(sync):
            clear(sync, stale)
            for i, s in two_slots(sync, chunks):
                sync.wait_ge(sems["dve_took"], 2 * i + s + 1)
                sync.dma_start(T.w[:, s, 0:KD * 256], weights(2 * i + s)).then_inc(sems["w_full"][s], 16)

        @block.tensor
        def _(pe):
            for i, s in two_slots(pe, chunks):
                pe.wait_ge(sems["w_full"][s], 16 * i + 16)
                pe.wait_ge(sems["act_took"], 2 * i + s + 1)
                pe.wait_ge(sems["dve_took"], 2 * i + s + 1)
                for m in range(tiles):
                    for k in range(KD):
                        mm = nc.tensor.matmul(T.ps[4 * s + m][:, 0:256], lhs[:, k, m * P:m * P + P],
                                              T.w[:, s, k * 256:k * 256 + 256], start=(k == 0), stop=(k == KD - 1))
                    mm.then_inc((sems["even_done"], sems["odd_done"])[m % 2], 1)

        @block.scalar
        def _(act):
            act.sem_inc(sems["act_took"], 2)
            for i, s in two_slots(act, chunks):
                for m in range(0, tiles, 2):
                    act.wait_ge(sems["even_done"], (2 * i + s) * (tiles // 2) + m // 2 + 1)
                    w = write(nc.scalar, 2 * i + s, m, T.ps[4 * s + m][:, 0:256])
                w.then_inc(sems["act_took"], 1)

        @block.vector
        def _(dve):
            dve.sem_inc(sems["dve_took"], 2)
            for i, s in two_slots(dve, chunks):
                for m in range(1, tiles, 2):
                    dve.wait_ge(sems["odd_done"], (2 * i + s) * (tiles // 2) + m // 2 + 1)
                    w = write(nc.vector, 2 * i + s, m, T.ps[4 * s + m][:, 0:256])
                w.then_inc(sems["dve_took"], 1)


def copied(eng, dst, src):
    return eng.copy(dst, src) if eng.engine == mybir.EngineType.Activation else eng.tensor_copy(dst, src)


def rwkv_prep_phase(nc, T, sems, stale, R):
    p = R.p
    col = lambda name, j: T.lc[:, LCOLS[name][0] + j:LCOLS[name][0] + j + 1]
    with nc.sbuf_tensor([P, 2, RW_W], F32) as up, nc.sbuf_tensor([P, 2, S], F32) as tmp, \
            nc.sbuf_tensor([P, PAIRS, S], F32) as w, nc.sbuf_tensor([P, PAIRS, S], F32) as a, \
            nc.sbuf_tensor([P, PAIRS, S], F32) as norm, \
            nc.sbuf_tensor([P, 2, S], F32) as sq, nc.sbuf_tensor([P, 2, S], F32) as rk, \
            nc.sbuf_tensor([P, 4], F32) as one_less_ka, nc.sbuf_tensor([P, S], F32) as chunk_start, \
            nc.Block() as block:
        @block.sync
        def _(sync):
            clear(sync, stale)
            sync.dma_start(up[:, :, :], R.up()).then_inc(sems["loaded"], 16)
            sync.dma_start(chunk_start[:, :], T.dram["chunk_start"]).then_inc(sems["loaded"], 16)

        @block.vector
        def _(dve):
            link = Chain(dve, sems["dve"])
            dve.wait_ge(sems["loaded"], 32)
            for n, t in enumerate((12, 13) + tuple(range(12))):
                d = tmp[:, n % 2, :]
                nc.vector.tensor_tensor(d[:, 1:S], p[:, t, 0:S - 1], p[:, t, 1:S], ALU.subtract)
                link(nc.vector.tensor_scalar(d[:, 0:1], p[:, t, 0:1], -1.0, None, ALU.mult))
                nc.vector.scalar_tensor_tensor(out=p[:, t, :], in0=d, scalar=col("mu", t), in1=p[:, t, :],
                                               op0=ALU.mult, op1=ALU.add).then_inc(sems["shifted"], 1)
            dve.wait_ge(sems["shifted"], 14)
            link(nc.vector.tensor_scalar(one_less_ka[:, :], T.lc[:, LCOLS["k_a"][0]:LCOLS["k_a"][1]], -1.0, 1.0,
                                         ALU.mult, ALU.add))
            for j in range(PAIRS):
                r, k, v = p[:, j, :], p[:, 4 + j, :], p[:, 8 + j, :]
                kk = R.alpha[:, j, :]
                link(nc.vector.tensor_scalar(kk, k, col("k_k", j), None, ALU.mult))
                if j >= 2:
                    dve.wait_ge(sems["kk_summed"], j - 1)
                nc.vector.tensor_tensor(sq[:, j % 2, :], kk, kk, ALU.mult).then_inc(sems["kk_squared"], 1)
                dve.wait_ge(sems["rate_ready"], j + 1)
                d = tmp[:, 0, :]
                link(nc.vector.tensor_scalar(d, a[:, j, :], col("k_a", j), one_less_ka[:, j:j + 1], ALU.mult,
                                             ALU.add))
                link(nc.vector.tensor_tensor(k, k, d, ALU.mult))
                if j >= 2:
                    dve.wait_ge(sems["rk_summed"], j - 1)
                nc.vector.scalar_tensor_tensor(out=rk[:, j % 2, :], in0=r, scalar=col("r_k", j), in1=k,
                                               op0=ALU.mult, op1=ALU.mult).then_inc(sems["rk_ready"], 1)
                dve.wait_ge(sems["kk_summed"], j + 1)
                nc.vector.tensor_scalar(norm[:, j, :], T.ps[4 + j % 2][:, :], 1e-24, None, ALU.max).then_inc(
                    sems["norm_guarded"], 1)
                dve.wait_ge(sems["decay_ready"], j + 1)
                nc.vector.tensor_tensor_scan(w[:, j, :], chunk_start[:, :], w[:, j, :], 0.0, ALU.mult,
                                             ALU.add).then_inc(sems["decay_scanned"], 1)
                dve.wait_ge(sems["norm_rooted"], 2 * j + 2)
                link(nc.vector.tensor_tensor(kk, kk, norm[:, j, :], ALU.mult))
                link(nc.vector.tensor_tensor(d, kk, a[:, j, :], ALU.mult))
                run = R.run[:, j, :]
                dve.wait_ge(sems["run_ready"], 2 * j + 2)
                nc.vector.tensor_tensor(R.beta[:, j, :], d, w[:, j, :], ALU.mult)
                nc.vector.tensor_tensor(R.kappa[:, j, :], k, w[:, j, :], ALU.mult)
                nc.vector.tensor_tensor(R.rho[:, j, :], r, run, ALU.mult)
                link(nc.vector.tensor_copy(tmp[:, 1, 0:S:C], kk[:, 0:S:C]))
                nc.vector.tensor_tensor(tmp[:, 0, 1:S], kk[:, 1:S], run[:, 0:S - 1], ALU.mult)
                link(nc.vector.tensor_copy(tmp[:, 0, 0:1], kk[:, 0:1]))
                link(nc.vector.tensor_copy(R.alpha[:, j, :], tmp[:, 0, :]))
                link(nc.vector.tensor_copy(R.alpha[:, j, 0:S:C], tmp[:, 1, 0:S:C]))
                dve.wait_ge(sems["rk_summed"], j + 1)
                nc.vector.tensor_tensor(R.bonus[:, j, :], T.ps[6 + j % 2][:, :], v, ALU.mult).then_inc(
                    sems["bonus_done"], 1)

        @block.scalar
        def _(act):
            act.wait_ge(sems["shifted"], 2)
            nc.scalar.activation(p[0:64, 12, :], p[0:64, 12, :], ACT.Tanh).then_inc(sems["low_ready"], 1)
            nc.scalar.activation(p[:, 13, :], p[:, 13, :], ACT.Sigmoid).then_inc(sems["low_ready"], 1)
            for j in range(PAIRS):
                act.wait_ge(sems["decay_summed"], j + 1)
                nc.scalar.activation(w[:, j, :], T.ps[0][:, :], ACT.Sigmoid, bias=col("w0", j)).then_inc(
                    sems["decay_ready"], 1)
                act.wait_ge(sems["rate_summed"], j + 1)
                nc.scalar.activation(a[:, j, :], T.ps[1][:, :], ACT.Sigmoid, bias=col("a0", j)).then_inc(
                    sems["rate_ready"], 1)
                act.wait_ge(sems["gate_summed"], j + 1)
                nc.scalar.copy(R.gate[:, j, :], T.ps[2][:, :]).then_inc(sems["gate_taken"], 1)
            for j in range(PAIRS):
                act.wait_ge(sems["norm_guarded"], j + 1)
                nc.scalar.activation(norm[:, j, :], norm[:, j, :], ACT.Ln, scale=2.0 ** 17).then_inc(
                    sems["norm_rooted"], 1)
                act.wait_ge(sems["norm_rooted"], 2 * j + 1)
                nc.scalar.activation(norm[:, j, :], norm[:, j, :], ACT.Exp, scale=-0.5,
                                     bias=T.half_17ln2[:, :]).then_inc(sems["norm_rooted"], 1)
                act.wait_ge(sems["decay_scanned"], j + 1)
                nc.scalar.activation(R.run[:, j, :], w[:, j, :], ACT.Exp, scale=-DECAY).then_inc(sems["run_ready"], 1)
                nc.scalar.activation(w[:, j, :], w[:, j, :], ACT.Exp, scale=DECAY).then_inc(sems["run_ready"], 1)

        @block.tensor
        def _(pe):
            pe.wait_ge(sems["loaded"], 32)
            pe.wait_ge(sems["low_ready"], 2)
            for j in range(PAIRS):
                if j:
                    pe.wait_ge(sems["decay_ready"], j)
                    pe.wait_ge(sems["rate_ready"], j)
                    pe.wait_ge(sems["gate_taken"], j)
                o = slice(j * P, j * P + P)
                nc.tensor.matmul(T.ps[0][:, :], up[0:64, 0, o], p[0:64, 12, :], start=True, stop=True).then_inc(
                    sems["decay_summed"], 1)
                nc.tensor.matmul(T.ps[1][:, :], up[64:128, 0, o], p[64:128, 12, :], start=True,
                                 stop=True).then_inc(sems["rate_summed"], 1)
                nc.tensor.matmul(T.ps[2][:, :], up[:, 1, o], p[:, 13, :], start=True, stop=True).then_inc(
                    sems["gate_summed"], 1)
            for j in range(PAIRS):
                if j >= 2:
                    pe.wait_ge(sems["bonus_done"], j - 1)
                pe.wait_ge(sems["kk_squared"], j + 1)
                nc.tensor.matmul(T.ps[4 + j % 2][:, :], T.head_ones[:, :], sq[:, j % 2, :], start=True,
                                 stop=True).then_inc(sems["kk_summed"], 1)
                pe.wait_ge(sems["rk_ready"], j + 1)
                nc.tensor.matmul(T.ps[6 + j % 2][:, :], T.head_ones[:, :], rk[:, j % 2, :], start=True,
                                 stop=True).then_inc(sems["rk_summed"], 1)


RWKV_PREP_SEMS = ("loaded shifted dve low_ready norm_guarded norm_rooted decay_scanned run_ready decay_summed rate_summed gate_summed rate_ready gate_taken "
                  "decay_ready kk_squared kk_summed rk_ready rk_summed bonus_done")


def rwkv_chunk_phases(nc, T, pre, rec, R):
    with ExitStack() as ctx:
        def sb(name, *shape):
            return ctx.enter_context(nc.sbuf_tensor(f"rec_{name}", [P, *shape], F32))

        aB, bB, kB, vB, M, LT, AkT, X, XT, T1, bT, kT, vT, Rs, Un = (
            sb(n, PAIRS, P) for n in "aB bB kB vB M LT AkT X XT T1 bT kT vT Rs Un".split())
        rho, BT, ArT, PC = sb("rho", PAIRS, C), sb("BT", 2, PAIRS * P), sb("ArT", 2, PAIRS, C), sb("PC", PAIRS, 1)
        rmask = sb("masks", LEVELS + 4, S)
        ps = T.ps

        def pair(j):
            return slice(j * P, j * P + P)

        with nc.Block() as block:
            @block.sync
            def _(sync):
                clear(sync, rec["stale"])
                sync.dma_start(rmask[:, :, :], T.dram["rmask"]).then_inc(rec["masks_loaded"], 16)
                sync.wait_ge(rec["masks_loaded"], 16)

            @block.gpsimd
            def _(pool):
                for t in (aB, bB, kB, vB, M):
                    nc.gpsimd.memset(t[:, :, :], 0.0)

        with nc.Fori(0, NCH) as c:
            with nc.Block() as block:
                @block.sync
                def _(sync):
                    clear(sync, rec)

                @block.scalar
                def _(act):
                    now = ds(c * C, C)
                    for h in range(2):
                        q = slice(64 * h, 64 * h + 64)
                        nc.scalar.copy(aB[q, :, 64 * h:64 * h + 64], R.alpha[q, :, now]).then_inc(pre["blocks_act"], 1)
                        nc.scalar.copy(kB[q, :, 64 * h:64 * h + 64], R.kappa[q, :, now]).then_inc(pre["blocks_act"], 1)
                    nc.scalar.copy(PC[:, :, :], R.run[:, :, ds(c * C + C - 1, 1)])
                    for n, t in enumerate((bT, kT, vT)):
                        act.wait_ge(pre["turned"], n + 1)
                        nc.scalar.copy(flat(t[:, :, :]), ps[4 + n][:, :])
                    for lev in range(LEVELS):
                        act.wait_ge(pre["t1_done"], lev + 1)
                        nc.scalar.copy(flat(T1[:, :, :]), ps[0][:, :]).then_inc(pre["t1_taken"], 1)

                @block.gpsimd
                def _(pool):
                    pool.wait_ge(pre["lt_ready"], 1)
                    for lev in range(LEVELS):
                        if lev >= 2:
                            pool.wait_ge(pre["t1_done"], lev - 1)
                        nc.gpsimd.tensor_tensor(BT[:, lev % 2, :], flat(LT[:, :, :]), rmask[:, 3 + lev, :],
                                                ALU.mult).then_inc(pre["bt_ready"], 1)

                @block.vector
                def _(dve):
                    link = Chain(dve, pre["dve"])
                    now = ds(c * C, C)
                    for h in range(2):
                        q = slice(64 * h, 64 * h + 64)
                        nc.vector.tensor_copy(bB[q, :, 64 * h:64 * h + 64], R.beta[q, :, now]).then_inc(
                            pre["blocks_dve"], 1)
                        nc.vector.tensor_copy(vB[q, :, 64 * h:64 * h + 64], R.p[q, 8:12, now]).then_inc(
                            pre["blocks_dve"], 1)
                    nc.vector.tensor_copy(rho[:, :, :], R.rho[:, :, now]).then_inc(pre["blocks_dve"], 1)
                    dve.wait_ge(pre["products"], 1)
                    link(nc.vector.tensor_tensor(flat(LT[:, :, :]), ps[0][:, :], rmask[:, 0, :], ALU.mult))
                    dve.sem_inc(pre["lt_ready"], 1)
                    link(nc.vector.tensor_tensor(flat(XT[:, :, :]), flat(LT[:, :, :]), rmask[:, 2, :], ALU.mult))
                    link(nc.vector.tensor_tensor(flat(XT[:, :, :]), T.ident4[:, :], flat(XT[:, :, :]), ALU.subtract))
                    dve.wait_ge(pre["products"], 2)
                    link(nc.vector.tensor_tensor(flat(X[:, :, :]), ps[1][:, :], rmask[:, 8, :], ALU.mult))
                    nc.vector.tensor_tensor(flat(X[:, :, :]), T.ident4[:, :], flat(X[:, :, :]),
                                            ALU.subtract).then_inc(pre["x_ready"], 1)
                    dve.wait_ge(pre["products"], 3)
                    nc.vector.tensor_tensor(flat(AkT[:, :, :]), ps[2][:, :], rmask[:, 0, :], ALU.mult)
                    dve.wait_ge(pre["products"], 4)
                    nc.vector.tensor_tensor(ArT[:, :, :, :].rearrange("p a b c -> p (a b c)"), ps[3][:, :],
                                            rmask[:, 1, :], ALU.mult)
                    for lev in range(LEVELS):
                        dve.wait_ge(pre["xt_done"], lev + 1)
                        if lev < LEVELS - 1:
                            nc.vector.tensor_tensor(flat(X[:, :, :]), flat(X[:, :, :]), ps[1][:, :], ALU.subtract)
                        nc.vector.tensor_tensor(flat(XT[:, :, :]), flat(XT[:, :, :]), ps[7][:, :],
                                                ALU.subtract).then_inc(pre["x_ready"], 1)

                @block.tensor
                def _(pe):
                    pe.wait_ge(pre["blocks_act"], 4)
                    pe.wait_ge(pre["blocks_dve"], 5)
                    for bank, lhs, rhs in ((0, bB, aB), (1, aB, bB), (2, kB, aB)):
                        for j in range(PAIRS):
                            mm = nc.tensor.matmul(ps[bank][:, pair(j)], lhs[:, j, :], rhs[:, j, :], start=True,
                                                  stop=True)
                        mm.then_inc(pre["products"], 1)
                    for n, lhs in enumerate((bB, kB)):
                        for j in range(PAIRS):
                            mm = nc.tensor.matmul(ps[3][:, (4 * n + j) * C:(4 * n + j + 1) * C], lhs[:, j, :],
                                                  rho[:, j, :], start=True, stop=True)
                    mm.then_inc(pre["products"], 1)
                    for n, src in enumerate((bB, kB, vB)):
                        for j in range(PAIRS):
                            mm = nc.tensor.transpose(ps[4 + n][:, pair(j)], src[:, j, :], T.ident[:, :])
                        mm.then_inc(pre["turned"], 1)
                    for lev in range(LEVELS):
                        pe.wait_ge(pre["bt_ready"], lev + 1)
                        pe.wait_ge(pre["x_ready"], lev + 1)
                        for j in range(PAIRS):
                            mm = nc.tensor.matmul(ps[0][:, pair(j)], BT[:, lev % 2, pair(j)], X[:, j, :],
                                                  start=True, stop=True)
                        mm.then_inc(pre["t1_done"], 1)
                        pe.wait_ge(pre["t1_taken"], lev + 1)
                        for bank, lhs, rhs in ((1, XT, T1), (7, T1, XT)):
                            if bank == 1 and lev == LEVELS - 1:
                                continue
                            for j in range(PAIRS):
                                mm = nc.tensor.matmul(ps[bank][:, pair(j)], lhs[:, j, :], rhs[:, j, :],
                                                      start=True, stop=True)
                        mm.then_inc(pre["xt_done"], 1)

            with nc.Block() as block:
                @block.sync
                def _(sync):
                    clear(sync, pre)

                @block.tensor
                def _(pe):
                    for j in range(PAIRS):
                        nc.tensor.matmul(ps[0][:, pair(j)], aB[:, j, :], M[:, j, :], start=True, stop=False)
                        mm = nc.tensor.matmul(ps[0][:, pair(j)], AkT[:, j, :], vT[:, j, :], start=False, stop=True)
                    mm.then_inc(rec["right_done"], 1)
                    pe.wait_ge(rec["right_taken"], 1)
                    for j in range(PAIRS):
                        mm = nc.tensor.matmul(ps[1][:, pair(j)], XT[:, j, :], Rs[:, j, :], start=True, stop=True)
                    mm.then_inc(rec["u_done"], 1)
                    pe.wait_ge(rec["u_taken"], 1)
                    for j in range(PAIRS):
                        nc.tensor.matmul(ps[2][:, pair(j)], kT[:, j, :], vT[:, j, :], start=True, stop=False)
                        mm = nc.tensor.matmul(ps[2][:, pair(j)], bT[:, j, :], Un[:, j, :], start=False, stop=True)
                    mm.then_inc(rec["change_done"], 1)
                    for j in range(PAIRS):
                        o = slice(j * C, j * C + C)
                        nc.tensor.matmul(ps[3][:, o], M[:, j, :], rho[:, j, :], start=True, stop=False)
                        nc.tensor.matmul(ps[3][:, o], vT[:, j, :], ArT[:, 1, j, :], start=False, stop=False)
                        mm = nc.tensor.matmul(ps[3][:, o], Un[:, j, :], ArT[:, 0, j, :], start=False, stop=True)
                    mm.then_inc(rec["y_done"], 1)

                @block.scalar
                def _(act):
                    act.wait_ge(rec["right_done"], 1)
                    nc.scalar.copy(flat(Rs[:, :, :]), ps[0][:, :]).then_inc(rec["right_taken"], 1)
                    act.wait_ge(rec["u_done"], 1)
                    nc.scalar.mul(flat(Un[:, :, :]), ps[1][:, :], -1.0).then_inc(rec["u_taken"], 1)
                    act.wait_ge(rec["y_done"], 1)
                    nc.scalar.copy(R.y[:, :, ds(c * C, C)], ps[3][:, 0:PAIRS * C].rearrange(
                        "p (j t) -> p j t", j=PAIRS))

                @block.vector
                def _(dve):
                    dve.wait_ge(rec["y_done"], 1)
                    nc.vector.tensor_tensor(flat(M[:, :, :]), flat(M[:, :, :]), ps[2][:, :], ALU.add).then_inc(
                        rec["dve"], 1)
                    dve.wait_ge(rec["dve"], 1)
                    nc.vector.tensor_tensor(M[:, :, :], M[:, :, :], PC[:, :, :].to_broadcast([P, PAIRS, P]),
                                            ALU.mult)


RWKV_PRE_SEMS = ("blocks_act blocks_dve turned t1_done t1_taken lt_ready bt_ready dve products x_ready xt_done")
RWKV_REC_SEMS = "masks_loaded right_done right_taken u_done u_taken change_done y_done dve"


def rwkv_out_phase(nc, T, sems, stale, R, out):
    col = lambda name, j: T.lc[:, LCOLS[name][0] + j:LCOLS[name][0] + j + 1]
    with nc.sbuf_tensor([P, 2, S], F32) as sq, nc.sbuf_tensor([P, PAIRS, S], F32) as rstd, nc.Block() as block:
        @block.sync
        def _(sync):
            clear(sync, stale)

        @block.scalar
        def _(act):
            for j in range(PAIRS):
                act.wait_ge(sems["var_done"], j + 1)
                rsqrt(act, sems["rooted"], 2 * j, rstd[:, j, :], T.ps[4 + j][:, :], 1.0 / 64, T.eps(GN_EPS))

        @block.tensor
        def _(pe):
            for j in range(PAIRS):
                nc.tensor.matmul(T.ps[j][:, :], T.head_ones[:, :], R.y[:, j, :], start=True, stop=True).then_inc(
                    sems["mean_done"], 1)
            for j in range(PAIRS):
                pe.wait_ge(sems["squared"], j + 1)
                nc.tensor.matmul(T.ps[4 + j][:, :], T.head_ones[:, :], sq[:, j % 2, :], start=True,
                                 stop=True).then_inc(sems["var_done"], 1)

        @block.vector
        def _(dve):
            link = Chain(dve, sems["dve"])
            for j in range(PAIRS):
                y = R.y[:, j, :]
                dve.wait_ge(sems["mean_done"], j + 1)
                link(nc.vector.scalar_tensor_tensor(out=y, in0=T.ps[j][:, :], scalar=-1.0 / 64, in1=y,
                                                    op0=ALU.mult, op1=ALU.add))
                if j >= 2:
                    dve.wait_ge(sems["var_done"], j - 1)
                nc.vector.tensor_tensor(sq[:, j % 2, :], y, y, ALU.mult).then_inc(sems["squared"], 1)
            for j in range(PAIRS):
                y, rs = R.y[:, j, :], rstd[:, j, :]
                dve.wait_ge(sems["rooted"], 2 * j + 2)
                link(nc.vector.scalar_tensor_tensor(out=y, in0=y, scalar=col("lnx_g", j), in1=rs,
                                                    op0=ALU.mult, op1=ALU.mult))
                link(nc.vector.scalar_tensor_tensor(out=y, in0=y, scalar=col("lnx_b", j), in1=R.bonus[:, j, :],
                                                    op0=ALU.add, op1=ALU.add))
                nc.vector.tensor_tensor(out[:, j, :], y, R.gate[:, j, :], ALU.mult)


RWKV_OUT_SEMS = "mean_done squared var_done rooted dve"


RET_SEMS = ("loaded rotated rot_summed taken scored decayed summed squared sq_summed rooted done silu dve")


def retention_phase(nc, T, sems, stale, qk, vt, g, out):
    with nc.sbuf_tensor([P, RET_HEADS, S], F32) as decay, nc.sbuf_tensor([P, 2, S], F32) as cossin, \
            nc.sbuf_tensor([P, P], F32) as rot, nc.sbuf_tensor([P, 2, S], F32) as tmp, \
            nc.sbuf_tensor([P, 4, S], F32) as sc, nc.sbuf_tensor([P, S], F32) as rstd, nc.Block() as block:
        @block.sync
        def _(sync):
            clear(sync, stale)
            sync.dma_start(cossin[:, :, :], T.dram["ret_cossin"]).then_inc(sems["loaded"], 16)
            sync.dma_start(rot[:, :], T.dram["rot"]).then_inc(sems["loaded"], 16)
            sync.dma_start(decay[:, :, :], T.dram["ret_decay"]).then_inc(sems["loaded"], 16)

        @block.tensor
        def _(pe):
            pe.wait_ge(sems["loaded"], 48)
            for t in range(4):
                nc.tensor.matmul(T.ps[t][:, :], rot[:, :], qk[:, t, :], start=True, stop=True).then_inc(
                    sems["rot_summed"], 1)
            pe.wait_ge(sems["rotated"], 4)
            for h in range(RET_HEADS):
                q = slice(64 * (h % 2), 64 * (h % 2) + 64)
                for jc in range(4):
                    if h:
                        pe.wait_ge(sems["decayed"], 4 * (h - 1) + jc + 1)
                    nc.tensor.matmul(T.ps[jc][:, 0:S - jc * P], qk[q, 2 + h // 2, jc * P:jc * P + P],
                                     qk[q, h // 2, jc * P:S], start=True, stop=True).then_inc(sems["scored"], 1)
                for jc in range(4):
                    pe.wait_ge(sems["decayed"], 4 * h + jc + 1)
                    if h >= 2 and jc == 0:
                        pe.wait_ge(sems["done"], h - 1)
                    mm = nc.tensor.matmul(T.ps[4 + h % 2][:, jc * P:S], vt[:, jc, h * P:h * P + P],
                                          sc[:, jc, 0:S - jc * P], start=(jc == 0), stop=(jc == 3),
                                          skip_group_check=True)
                mm.then_inc(sems["summed"], 1)
                pe.wait_ge(sems["squared"], h + 1)
                nc.tensor.matmul(T.ps[6][:, :], T.ones[:, :], tmp[:, 1, :], start=True, stop=True).then_inc(
                    sems["sq_summed"], 1)

        @block.scalar
        def _(act):
            for h in range(RET_HEADS):
                nc.scalar.activation(g[:, h, :], g[:, h, :], ACT.Silu).then_inc(sems["silu"], 1)
            act.wait_ge(sems["rotated"], 4)
            for h in range(RET_HEADS):
                act.wait_ge(sems["summed"], h + 1)
                nc.scalar.activation(tmp[:, 1, :], T.ps[4 + h % 2][:, :], ACT.Square).then_inc(sems["squared"], 1)
                act.wait_ge(sems["sq_summed"], h + 1)
                if h:
                    act.wait_ge(sems["done"], h)
                rsqrt(act, sems["rooted"], 2 * h, rstd[:, :], T.ps[6][:, :], 1.0 / P, T.eps(EPS))

        @block.vector
        def _(dve):
            link = Chain(dve, sems["dve"])
            dve.wait_ge(sems["loaded"], 48)
            for t in range(4):
                dve.wait_ge(sems["rot_summed"], t + 1)
                if t:
                    dve.wait_ge(sems["rotated"], t)
                nc.vector.tensor_tensor(tmp[:, 0, :], T.ps[t][:, :], cossin[:, 1, :], ALU.mult)
                link(nc.vector.tensor_tensor(tmp[:, 1, :], qk[:, t, :], cossin[:, 0, :], ALU.mult))
                nc.vector.tensor_tensor(qk[:, t, :], tmp[:, 0, :], tmp[:, 1, :], ALU.add).then_inc(sems["rotated"], 1)
            dve.wait_ge(sems["silu"], 4)
            for h in range(RET_HEADS):
                if h:
                    dve.wait_ge(sems["summed"], h)
                for jc in range(4):
                    dve.wait_ge(sems["scored"], 4 * h + jc + 1)
                    n = S - jc * P
                    nc.vector.tensor_tensor(sc[:, jc, 0:n], T.ps[jc][:, 0:n], decay[:, h, 0:n], ALU.mult).then_inc(
                        sems["decayed"], 1)
                dve.wait_ge(sems["rooted"], 2 * h + 2)
                if h:
                    dve.wait_ge(sems["done"], h)
                link(nc.vector.tensor_tensor(tmp[:, 0, :], T.ps[4 + h % 2][:, :], rstd[:, :], ALU.mult))
                nc.vector.tensor_tensor(out[:, h, :], tmp[:, 0, :], g[:, h, :], ALU.mult).then_inc(sems["done"], 1)


SGU_SEMS = "loaded gelu_v gelu_u normed rooted stats mixed w_masked dve"


def sgu_phase(nc, T, sems, stale, u, vt, layer, out):
    with nc.sbuf_tensor([P, S], F32) as wsT, nc.sbuf_tensor([P, S], F32) as causal, nc.sbuf_tensor([P, 3, S], F32) as rows, \
            nc.sbuf_tensor([P, 4, 6], F32) as stats, nc.sbuf_tensor([P, 4, 2], F32) as mv, \
            nc.sbuf_tensor([P, 4], F32) as rstd, nc.sbuf_tensor([P, 2, S], F32) as tmp, nc.Block() as block:
        @block.sync
        def _(sync):
            clear(sync, stale)
            sync.dma_start(wsT[:, :], T.dram["sg_wT"][ds(layer, 1)].rearrange("l p c -> p (l c)")).then_inc(
                sems["loaded"], 16)
            sync.dma_start(causal[:, :], T.dram["causal"]).then_inc(sems["loaded"], 16)
            sync.dma_start(rows[:, :, :].rearrange("p a b -> p (a b)"),
                           T.dram["sg_rows"][ds(layer, 1), :].to_broadcast([P, 3 * S])).then_inc(sems["loaded"], 16)

        @block.scalar
        def _(act):
            for m in range(4):
                nc.scalar.activation(vt[:, m, :], vt[:, m, :], ACT.Gelu).then_inc(sems["gelu_v"], 1)
            for t in range(4):
                nc.scalar.activation(u[:, t, :], u[:, t, :], ACT.Gelu).then_inc(sems["gelu_u"], 1)
            act.wait_ge(sems["stats"], 4)
            rsqrt(act, sems["rooted"], 0, rstd[:, :], mv[:, :, 1:2].rearrange("p m a -> p (m a)"), 1.0, T.eps(EPS))

        @block.vector
        def _(dve):
            link = Chain(dve, sems["dve"])
            dve.wait_ge(sems["loaded"], 48)
            nc.vector.tensor_tensor(wsT[:, :], wsT[:, :], causal[:, :], ALU.mult).then_inc(sems["w_masked"], 1)
            for m in range(4):
                dve.wait_ge(sems["gelu_v"], m + 1)
                link(nc.vector.bn_stats(stats[:, m, :], vt[:, m, :]))
                nc.vector.bn_aggr(mv[:, m, :], stats[:, m, :]).then_inc(sems["stats"], 1)
            dve.wait_ge(sems["rooted"], 2)
            for m in range(4):
                v = vt[:, m, :]
                link(nc.vector.tensor_scalar(v, v, mv[:, m, 0:1], rstd[:, m:m + 1], ALU.subtract, ALU.mult))
                link(nc.vector.tensor_tensor(v, v, rows[:, 0, :], ALU.mult))
                nc.vector.tensor_tensor(v, v, rows[:, 1, :], ALU.add).then_inc(sems["normed"], 1)
            dve.wait_ge(sems["gelu_u"], 4)
            for g in range(SG_GROUPS):
                dve.wait_ge(sems["mixed"], g + 1)
                bias = rows[:, 2, g * P:g * P + P].unsqueeze(1).to_broadcast([P, 4, P])
                link(nc.vector.tensor_tensor(tmp[:, g % 2, :].rearrange("p (m i) -> p m i", m=4),
                                             T.ps[g][:, :].rearrange("p (m i) -> p m i", m=4), bias, ALU.add))
                link(nc.vector.tensor_tensor(out[:, g, :], tmp[:, g % 2, :], u[:, g, :], ALU.mult))

        @block.tensor
        def _(pe):
            pe.wait_ge(sems["w_masked"], 1)
            pe.wait_ge(sems["normed"], 4)
            for g in range(SG_GROUPS):
                for m in range(4):
                    mm = nc.tensor.matmul(T.ps[g][:, m * P:m * P + P], vt[:, m, g * P:g * P + P],
                                          wsT[:, g * P:g * P + P], start=True, stop=True)
                mm.then_inc(sems["mixed"], 1)


MERGE_SEMS = "w_full*2 logits_done proj_done sig_done added zeroed dve"


def merge_phase(nc, T, sems, stale, weights, hT, branches, merged):
    with nc.sbuf_tensor([P, 4, S], F32) as sig, nc.Block() as block:
        @block.sync
        def _(sync):
            clear(sync, stale)
            with sync.Fori(0, 6) as i:
                for s in range(2):
                    sync.wait_ge(sems["added"], 4 * i + 2 * s + 2)
                    sync.dma_start(T.w[:, s, 0:12 * 256], weights(2 * i + s)).then_inc(sems["w_full"][s], 16)

        @block.tensor
        def _(pe):
            for b in range(3):
                with pe.Fori(0, 2) as i:
                    for s in range(2):
                        pe.wait_ge(sems["w_full"][s], 16 * i + 32 * b + 16)
                        for t in range(2):
                            n = 2 * s + t
                            pe.wait_ge(sems["added"], 4 * i + 8 * b + n + 1)
                            for k in range(KD):
                                c = k * 256 + t * P
                                mm = nc.tensor.matmul(T.ps[2 * n][:, :], T.w[:, s, c:c + P], hT[:, k, :],
                                                      start=(k == 0), stop=(k == KD - 1))
                            mm.then_inc(sems["logits_done"], 1)
                            for k in range(4):
                                c = (KD + k) * 256 + t * P
                                mm = nc.tensor.matmul(T.ps[2 * n + 1][:, :], T.w[:, s, c:c + P],
                                                      branches[b][:, k, :], start=(k == 0), stop=(k == 3))
                            mm.then_inc(sems["proj_done"], 1)

        @block.scalar
        def _(act):
            with act.Fori(0, 6) as i:
                for n in range(4):
                    act.wait_ge(sems["logits_done"], 4 * i + n + 1)
                    act.wait_ge(sems["added"], 4 * i + n + 1)
                    nc.scalar.activation(sig[:, n, :], T.ps[2 * n][:, :], ACT.Sigmoid).then_inc(sems["sig_done"], 1)

        @block.vector
        def _(dve):
            link = Chain(dve, sems["dve"])
            for k in range(KD):
                ms = nc.vector.memset(merged[:, k, :], 0.0)
            ms.then_inc(sems["zeroed"], 1)
            dve.wait_ge(sems["zeroed"], 1)
            dve.sem_inc(sems["added"], 4)
            for b in range(3):
                with dve.Fori(0, 2) as i:
                    for n in range(4):
                        dve.wait_ge(sems["sig_done"], 4 * i + 8 * b + n + 1)
                        dve.wait_ge(sems["proj_done"], 4 * i + 8 * b + n + 1)
                        link(nc.vector.tensor_tensor(sig[:, n, :], sig[:, n, :], T.ps[2 * n + 1][:, :], ALU.mult))
                        m = merged[:, ds(4 * i + n, 1), :].rearrange("p a t -> p (a t)")
                        nc.vector.tensor_tensor(m, m, sig[:, n, :], ALU.add).then_inc(sems["added"], 1)
                    link.restart()


FFN_UP_SEMS = "loaded w_full*2 gate_done val_done gate_taken val_taken conv_done silu_done made dve"


def ffn_up_phase(nc, T, sems, stale, weights, layer, hT, made):
    with nc.sbuf_tensor([P, FT, 8], F32) as cw, nc.sbuf_tensor([P, 4, S], F32) as conv, nc.Block() as block:
        @block.sync
        def _(sync):
            clear(sync, stale)
            sync.dma_start(cw[:, :, :], T.dram["ffn_conv"][ds(layer, 1)].rearrange(
                "l p j c -> p (l j) c")).then_inc(sems["loaded"], 16)
            for i, s in two_slots(sync, FT):
                sync.wait_ge(sems["made"], 2 * i + s + 1)
                sync.dma_start(T.w[:, s, 0:KD * 256], weights(2 * i + s)).then_inc(sems["w_full"][s], 16)

        @block.tensor
        def _(pe):
            for i, s in two_slots(pe, FT):
                pe.wait_ge(sems["w_full"][s], 16 * i + 16)
                pe.wait_ge(sems["made"], 2 * i + s + 1)
                for t in range(2):
                    for k in range(KD):
                        mm = nc.tensor.matmul(T.ps[2 * s + t][:, :], T.w[:, s, k * 256 + t * P:k * 256 + t * P + P],
                                              hT[:, k, :], start=(k == 0), stop=(k == KD - 1))
                    mm.then_inc((sems["gate_done"], sems["val_done"])[t], 1)

        @block.scalar
        def _(act):
            act.wait_ge(sems["loaded"], 16)
            for i, s in two_slots(act, FT):
                j = 2 * i + s
                act.wait_ge(sems["made"], j + 1)
                for t in range(2):
                    act.wait_ge((sems["gate_done"], sems["val_done"])[t], j + 1)
                    w2 = cw[:, ds(j, 1), 4 * t + 2:4 * t + 3].rearrange("p a b -> p (a b)")
                    b = cw[:, ds(j, 1), 4 * t + 3:4 * t + 4].rearrange("p a b -> p (a b)")
                    nc.scalar.activation(conv[:, 2 * s + t, :], T.ps[2 * s + t][:, :], ACT.Identity, bias=b,
                                         scale=w2).then_inc((sems["gate_taken"], sems["val_taken"])[t], 1)
                act.wait_ge(sems["conv_done"], j + 1)
                nc.scalar.activation(conv[:, 2 * s, :], conv[:, 2 * s, :], ACT.Silu).then_inc(sems["silu_done"], 1)

        @block.vector
        def _(dve):
            link = Chain(dve, sems["dve"])
            dve.sem_inc(sems["made"], 2)
            dve.wait_ge(sems["loaded"], 16)
            for i, s in two_slots(dve, FT):
                j = 2 * i + s
                for t in range(2):
                    c, u = conv[:, 2 * s + t, :], T.ps[2 * s + t]
                    tap = lambda q: cw[:, ds(j, 1), 4 * t + q:4 * t + q + 1].rearrange("p a b -> p (a b)")
                    dve.wait_ge((sems["gate_taken"], sems["val_taken"])[t], j + 1)
                    link(nc.vector.scalar_tensor_tensor(out=c[:, 1:S], in0=u[:, 0:S - 1], scalar=tap(1),
                                                        in1=c[:, 1:S], op0=ALU.mult, op1=ALU.add))
                    st = nc.vector.scalar_tensor_tensor(out=c[:, 2:S], in0=u[:, 0:S - 2], scalar=tap(0),
                                                        in1=c[:, 2:S], op0=ALU.mult, op1=ALU.add)
                    if t == 0:
                        st.then_inc(sems["conv_done"], 1)
                    else:
                        link(st)
                dve.wait_ge(sems["silu_done"], j + 1)
                nc.vector.tensor_tensor(made[:, ds(j, 1), :].rearrange("p a t -> p (a t)"), conv[:, 2 * s, :],
                                        conv[:, 2 * s + 1, :], ALU.mult).then_inc(sems["made"], 1)
                if s == 1:
                    link.restart()


DOWN_SEMS = "w_full*2 tile_done added"


def down_phase(nc, T, sems, stale, weights, kt, rhs, xT):
    with nc.Block() as block:
        @block.sync
        def _(sync):
            clear(sync, stale)
            for i, s in two_slots(sync, KD):
                sync.wait_ge(sems["added"], 2 * i + s + 1)
                sync.dma_start(T.w[:, s, 0:kt * P], weights(2 * i + s)).then_inc(sems["w_full"][s], 16)

        @block.tensor
        def _(pe):
            for i, s in two_slots(pe, KD):
                pe.wait_ge(sems["w_full"][s], 16 * i + 16)
                pe.wait_ge(sems["added"], 2 * i + s + 1)
                for k in range(kt):
                    mm = nc.tensor.matmul(T.ps[s][:, :], T.w[:, s, k * P:k * P + P], rhs[:, k, :],
                                          start=(k == 0), stop=(k == kt - 1))
                mm.then_inc(sems["tile_done"], 1)

        @block.vector
        def _(dve):
            dve.sem_inc(sems["added"], 2)
            for i, s in two_slots(dve, KD):
                dve.wait_ge(sems["tile_done"], 2 * i + s + 1)
                x = xT[:, ds(2 * i + s, 1), :].rearrange("p a t -> p (a t)")
                nc.vector.tensor_tensor(x, x, T.ps[s][:, :], ALU.add).then_inc(sems["added"], 1)


def put(dst):
    def write(eng, c, t, psum):
        return copied(eng, dst[:, ds(2 * c + t, 1), :].rearrange("p a t -> p (a t)"), psum)
    return write


def put_tokens(dst):
    def write(eng, c, m, psum):
        return copied(eng, dst[:, m, ds(256 * c, 256)], psum)
    return write


def pick(dram, *index):
    ap = dram
    names = "abcdef"[:len(index)]
    ap = ap[tuple(ds(i, 1) for i in index)]
    return ap.rearrange(f"{' '.join(names)} p c -> p ({' '.join(names)} c)")


def shared(nc, ctx, dram):
    def sb(name, *shape):
        return ctx.enter_context(nc.sbuf_tensor(name, [P, *shape], F32))

    T = Named()
    T.dram = dram
    T.xT, T.hT = sb("xT", KD, S), sb("hT", KD, S)
    T.w = sb("w", 2, 12 * 256)
    T.ident4, T.head_ones, T.ones = sb("ident4", 4 * P), sb("head_ones", P), sb("ones", P)
    T.lc, T.scalars = sb("layer_cols", NLCOL), sb("scalars", 4)
    T.ident = T.ident4[:, 0:P]
    T.eps = lambda e: T.scalars[:, (EPS, GN_EPS, LN_EPS).index(e):][:, 0:1]
    T.half_17ln2 = T.scalars[:, 3:4]
    T.ps = [ctx.enter_context(nc.psum_tensor(f"bank{i}", [P, 512], F32)) for i in range(8)]
    return T


def pick4(dram, i):
    return dram[ds(i, 1)].rearrange("l p a c -> p (l a) c")


def shared_sems(nc, ctx):
    return {name: sem_set(nc, ctx, name, names) for name, names in (
        ("start", "loaded"), ("stored", "done"), ("head", "loaded"), ("norm", NORM_SEMS), ("norm2", NORM_SEMS), ("pa", PROJECT_SEMS),
        ("pb", PROJECT_SEMS), ("down", DOWN_SEMS))}


def block_one(nc, T):
    with ExitStack() as ctx:
        layers(nc, ctx, T)


def layers(nc, ctx, T):
    ss = lambda prefix, names: sem_set(nc, ctx, prefix, names)
    head, norm, pa, pb, down = (T.sems[n] for n in ("head", "norm", "pa", "pb", "down"))
    prep, pre, rec, rout = (ss("prep", RWKV_PREP_SEMS), ss("pre", RWKV_PRE_SEMS), ss("rec", RWKV_REC_SEMS),
                            ss("rout", RWKV_OUT_SEMS))
    ret, sgu, merge, up = (ss("ret", RET_SEMS), ss("sgu", SGU_SEMS), ss("merge", MERGE_SEMS),
                           ss("up", FFN_UP_SEMS))
    rec["stale"] = prep
    d = T.dram
    xT = T.xT

    with nc.Fori(0, DEPTH) as layer:
        with nc.Block() as block:
            @block.sync
            def _(sync):
                clear(sync, T.sems["start"])
                clear(sync, down)
                sync.dma_start(T.lc[:, :], pick(d["layer_cols"], layer)).then_inc(head["loaded"], 16)
                sync.wait_ge(head["loaded"], 16)
        hT = T.hT
        gain = lambda name: T.lc[:, LCOLS[name][0]:LCOLS[name][1]]
        w_in = lambda first: (lambda c: pick(d["w_in"], layer, c + first))
        norm_phase(nc, T, norm, head, xT, gain("norm1_g"), hT)
        with ExitStack() as branch:
            def keep_branch(name, *shape):
                return branch.enter_context(nc.sbuf_tensor(name, [P, *shape], F32))

            y_rw = keep_branch("y_rw", 4, S)
            with ExitStack() as rw:
                R = Named()
                R.up = lambda: pick4(d["rw_up"], layer)
                R.beta, R.kappa, R.alpha, R.rho, R.run, R.gate, R.bonus = (
                    rw.enter_context(nc.sbuf_tensor("rw_" + n, [P, PAIRS, S], F32))
                    for n in ("beta", "kappa", "alpha", "rho", "run", "gate", "bonus"))
                R.p = rw.enter_context(nc.sbuf_tensor("rw_p", [P, RW_T, S], F32))
                R.y = y_rw
                project_phase(nc, T, pa, norm, w_in(0), 7, hT, put(R.p))
                rwkv_prep_phase(nc, T, prep, pa, R)
                rwkv_chunk_phases(nc, T, pre, rec, R)
                rwkv_out_phase(nc, T, rout, rec, R, y_rw)
            y_ret, y_sg = keep_branch("y_ret", 4, S), keep_branch("y_sg", 4, S)
            with nc.sbuf_tensor([P, 4, S], F32) as qk, nc.sbuf_tensor([P, 4, S], F32) as vt, \
                    nc.sbuf_tensor([P, 4, S], F32) as g:
                project_phase(nc, T, pa, rout, w_in(7), 2, hT, put(qk))
                token_project_phase(nc, T, pb, pa, w_in(9), 2, hT, put_tokens(vt))
                project_phase(nc, T, pa, pb, w_in(11), 2, hT, put(g))
                retention_phase(nc, T, ret, pa, qk, vt, g, y_ret)
            with nc.sbuf_tensor([P, 4, S], F32) as u, nc.sbuf_tensor([P, 4, S], F32) as vt:
                project_phase(nc, T, pa, ret, w_in(13), 2, hT, put(u))
                token_project_phase(nc, T, pb, pa, w_in(15), 2, hT, put_tokens(vt))
                sgu_phase(nc, T, sgu, pb, u, vt, layer, y_sg)
            with nc.sbuf_tensor([P, KD, S], F32) as merged:
                merge_phase(nc, T, merge, sgu, lambda c: pick(d["w_merge"], layer, c), hT, (y_rw, y_ret, y_sg),
                            merged)
                down_phase(nc, T, down, merge, lambda c: pick(d["w_out"], layer, c), KD, merged, xT)
        norm_phase(nc, T, norm, down, xT, gain("norm2_g"), hT)
        with nc.sbuf_tensor([P, FT, S], F32) as made:
            ffn_up_phase(nc, T, up, norm, lambda c: pick(d["ffn_up"], layer, c), layer, hT, made)
            down_phase(nc, T, down, up, lambda c: pick(d["ffn_down"], layer, c), FT, made, xT)


CONV_SEMS = "loaded sig sums_done squared sq_done rooted half dve silu"


def conv_phase(nc, T, sems, stale, ag, out):
    half = CONV_KERNEL // 2
    with nc.sbuf_tensor([P, 2, S + 2 * half], F32) as padded, nc.sbuf_tensor([P, 2, S], F32) as acc, \
            nc.sbuf_tensor([P, 2, CONV_KERNEL + 3], F32) as par, nc.sbuf_tensor([P, 2, S], F32) as sq, \
            nc.sbuf_tensor([P, S], F32) as rstd, nc.Block() as block:
        @block.sync
        def _(sync):
            clear(sync, stale)
            sync.dma_start(par[:, :, :], T.dram["conv_par"]).then_inc(sems["loaded"], 16)

        @block.scalar
        def _(act):
            for t in range(2):
                nc.scalar.activation(ag[:, 2 + t, :], ag[:, 2 + t, :], ACT.Sigmoid).then_inc(sems["sig"], 1)
            act.wait_ge(sems["sq_done"], 1)
            rsqrt(act, sems["rooted"], 0, rstd[:, :], T.ps[1][:, :], 1.0 / CONV_CH, T.eps(LN_EPS))
            for t in range(2):
                act.wait_ge(sems["half"], 3 + t)
                nc.scalar.activation(out[:, t, :], acc[:, t, :], ACT.Silu)

        @block.vector
        def _(dve):
            link = Chain(dve, sems["dve"])
            link(nc.vector.memset(padded[:, :, :], 0.0))
            dve.wait_ge(sems["loaded"], 16)
            dve.wait_ge(sems["sig"], 2)
            for t in range(2):
                link(nc.vector.tensor_tensor(padded[:, t, half:half + S], ag[:, t, :], ag[:, 2 + t, :], ALU.mult))
            for t in range(2):
                nc.vector.tensor_scalar(acc[:, t, :], padded[:, t, 0:S], par[:, t, 0:1],
                                        par[:, t, CONV_KERNEL:CONV_KERNEL + 1], ALU.mult, ALU.add).then_inc(
                    sems["dve"], 1)
            for j in range(1, CONV_KERNEL):
                for t in range(2):
                    dve.wait_ge(sems["dve"], link.n + 1)
                    nc.vector.scalar_tensor_tensor(out=acc[:, t, :], in0=padded[:, t, j:j + S],
                                                   scalar=par[:, t, j:j + 1], in1=acc[:, t, :], op0=ALU.mult,
                                                   op1=ALU.add).then_inc(sems["dve"], 1)
                    link.n += 1
            dve.wait_ge(sems["dve"], link.n + 2)
            link.n += 2
            dve.sem_inc(sems["half"], 1)
            dve.wait_ge(sems["sums_done"], 1)
            for t in range(2):
                link(nc.vector.scalar_tensor_tensor(out=acc[:, t, :], in0=T.ps[0][:, :], scalar=-1.0 / CONV_CH,
                                                    in1=acc[:, t, :], op0=ALU.mult, op1=ALU.add))
                nc.vector.tensor_tensor(sq[:, t, :], acc[:, t, :], acc[:, t, :], ALU.mult).then_inc(sems["squared"], 1)
            dve.wait_ge(sems["rooted"], 2)
            dve.sem_inc(sems["half"], 1)
            for t in range(2):
                link(nc.vector.scalar_tensor_tensor(out=acc[:, t, :], in0=acc[:, t, :],
                                                    scalar=par[:, t, CONV_KERNEL + 1:CONV_KERNEL + 2],
                                                    in1=rstd[:, :], op0=ALU.mult, op1=ALU.mult))
                nc.vector.tensor_scalar(acc[:, t, :], acc[:, t, :], par[:, t, CONV_KERNEL + 2:CONV_KERNEL + 3],
                                        None, ALU.add).then_inc(sems["half"], 1)

        @block.tensor
        def _(pe):
            pe.wait_ge(sems["half"], 1)
            for t in range(2):
                mm = nc.tensor.matmul(T.ps[0][:, :], T.ones[:, :], acc[:, t, :], start=(t == 0), stop=(t == 1))
            mm.then_inc(sems["sums_done"], 1)
            for t in range(2):
                pe.wait_ge(sems["squared"], t + 1)
                mm = nc.tensor.matmul(T.ps[1][:, :], T.ones[:, :], sq[:, t, :], start=(t == 0), stop=(t == 1))
            mm.then_inc(sems["sq_done"], 1)


ROPE_SEMS = "loaded dve reduced tables turned half_done pool done"


def rope_phase(nc, T, sems, stale, qk, tiles):
    with nc.sbuf_tensor([P, S], mybir.dt.int32) as pos_i, nc.sbuf_tensor([P, 1], F32) as inv, \
            nc.sbuf_tensor([P, S], F32) as ang, nc.sbuf_tensor([P, S], F32) as turns, \
            nc.sbuf_tensor([P, 2, S], F32) as table, nc.sbuf_tensor([P, P], F32) as rot, \
            nc.sbuf_tensor([P, 4, S], F32) as tmp, nc.Block() as block:
        @block.sync
        def _(sync):
            clear(sync, stale)
            sync.dma_start(pos_i[:, :], T.dram["positions"].to_broadcast([P, S])).then_inc(sems["loaded"], 16)
            sync.dma_start(inv[:, :], T.dram["rope_inv"]).then_inc(sems["loaded"], 16)
            sync.dma_start(rot[:, :], T.dram["rot"]).then_inc(sems["loaded"], 16)

        @block.vector
        def _(dve):
            link = Chain(dve, sems["dve"])
            dve.wait_ge(sems["loaded"], 48)
            link(nc.vector.tensor_copy(ang[:, :], pos_i[:, :]))
            link(nc.vector.tensor_scalar(ang[:, :], ang[:, :], inv[:, 0:1], None, ALU.mult))
            for n, shift in enumerate((np.pi / 2, 0.0)):
                r = table[:, n, :]
                link(nc.vector.tensor_scalar(turns[:, :], ang[:, :], float(shift), float(1 / (2 * np.pi)), ALU.add,
                                             ALU.mult))
                link(nc.vector.tensor_scalar(turns[:, :], turns[:, :], 12582912.0, None, ALU.add))
                link(nc.vector.tensor_scalar(turns[:, :], turns[:, :], -12582912.0, None, ALU.add))
                link(nc.vector.scalar_tensor_tensor(out=r, in0=turns[:, :], scalar=-TWO_PI[0], in1=ang[:, :],
                                                    op0=ALU.mult, op1=ALU.add))
                for part in TWO_PI[1:]:
                    link(nc.vector.scalar_tensor_tensor(out=r, in0=turns[:, :], scalar=-part, in1=r,
                                                        op0=ALU.mult, op1=ALU.add))
                link(nc.vector.tensor_scalar(r, r, float(shift), None, ALU.add))
                link(nc.vector.tensor_scalar(r, r, 3.1415925, -3.1415925, ALU.min, ALU.max))
            dve.sem_inc(sems["reduced"], 1)
            dve.wait_ge(sems["tables"], 2)
            with dve.Fori(0, tiles // 4) as i:
                for b in range(4):
                    dve.wait_ge(sems["turned"], 4 * i + b + 1)
                    nc.vector.tensor_tensor(tmp[:, b, :], T.ps[b][:, :], table[:, 1, :], ALU.mult).then_inc(
                        sems["half_done"], 1)
                for b in range(4):
                    x = qk[:, ds(4 * i + b, 1), :].rearrange("p a t -> p (a t)")
                    dve.wait_ge(sems["half_done"], 4 * i + b + 1)
                    dve.wait_ge(sems["pool"], 4 * i + b + 1)
                    nc.vector.tensor_tensor(x, x, tmp[:, b, :], ALU.add).then_inc(sems["done"], 1)
                dve.wait_ge(sems["done"], 4 * i + 4)

        @block.gpsimd
        def _(pool):
            pool.wait_ge(sems["tables"], 2)
            with pool.Fori(0, tiles // 4) as i:
                for b in range(4):
                    x = qk[:, ds(4 * i + b, 1), :].rearrange("p a t -> p (a t)")
                    pool.wait_ge(sems["turned"], 4 * i + b + 1)
                    nc.gpsimd.tensor_tensor(x, x, table[:, 0, :], ALU.mult).then_inc(sems["pool"], 1)

        @block.scalar
        def _(act):
            act.wait_ge(sems["reduced"], 1)
            for n in range(2):
                nc.scalar.activation(table[:, n, :], table[:, n, :], ACT.Sin).then_inc(sems["tables"], 1)

        @block.tensor
        def _(pe):
            pe.wait_ge(sems["loaded"], 48)
            with pe.Fori(0, tiles // 4) as i:
                for b in range(4):
                    x = qk[:, ds(4 * i + b, 1), :].rearrange("p a t -> p (a t)")
                    nc.tensor.matmul(T.ps[b][:, :], rot[:, :], x, start=True, stop=True).then_inc(sems["turned"], 1)
                pe.wait_ge(sems["half_done"], 4 * i + 4)


ATT_SEMS = ("loaded staged scored scaled maxed exped normed dve turned act_took dve_took summed put")


def attention_phase(nc, T, sems, stale, q, k, k_first, v, out, groups, q_tiles, keys, scale, mask=None):
    kt = keys // P
    vc = q_tiles * P
    wide = q_tiles > 1
    with nc.sbuf_tensor([P, q_tiles, S], F32) as qs, nc.sbuf_tensor([P, kt, vc], F32) as vs, \
            nc.sbuf_tensor([P, q_tiles, keys], F32) as ks, \
            nc.sbuf_tensor([P, 2, 4, keys], F32) as sc, nc.sbuf_tensor([P, kt, S], F32) as pT, \
            nc.sbuf_tensor([P, 2, 3, 4], F32) as st, nc.Block() as block:
        @block.sync
        def _(sync):
            clear(sync, stale)

        @block.gpsimd
        def _(pool):
            with pool.Fori(0, groups) as g:
                pool.wait_ge(sems["put"], 2 * g + 1)
                nc.gpsimd.tensor_copy(qs[:, :, :], q[:, ds(q_tiles * g, q_tiles), :]).then_inc(sems["staged"], 1)
                nc.gpsimd.tensor_copy(ks[:, :, :], k[:, ds(q_tiles * g + k_first, q_tiles), :]).then_inc(
                    sems["staged"], 1)
                nc.gpsimd.tensor_copy(vs[:, :, :], v[:, :, ds(vc * g, vc)]).then_inc(sems["staged"], 1)

        def rows(u):
            return slice(0, P) if wide else slice(64 * u, 64 * u + 64)

        @block.tensor
        def _(pe):
            with pe.Fori(0, groups) as g:
                pe.wait_ge(sems["staged"], 3 * g + 3)
                for u in range(2):
                    for m in range(4):
                        pe.wait_ge(sems["scaled"], 8 * g + 4 * u + m + 1)
                        tiles = (2 * u, 2 * u + 1) if wide else (0,)
                        for n in tiles:
                            mm = nc.tensor.matmul(T.ps[m % 2][:, 0:keys], qs[rows(u), n, m * P:m * P + P],
                                                  ks[rows(u), n, :], start=(n == tiles[0]), stop=(n == tiles[-1]))
                        mm.then_inc(sems["scored"], 1)
                for u in range(2):
                    pe.wait_ge(sems["normed"], 2 * g + u + 1)
                    pe.wait_ge(sems["act_took"], 2 * g + u + 1)
                    pe.wait_ge(sems["dve_took"], 2 * g + u + 1)
                    for j in range(kt):
                        for m in range(4):
                            mm = nc.tensor.transpose(T.ps[2 + j][:, m * P:m * P + P], sc[:, u, m, j * P:j * P + P],
                                                     T.ident[:, :])
                    mm.then_inc(sems["turned"], 1)
                    pe.wait_ge(sems["act_took"], 2 * g + u + 2)
                    pe.wait_ge(sems["dve_took"], 2 * g + u + 2)
                    pe.wait_ge(sems["put"], 2 * g + u + 1)
                    for e in range(2 if wide else 1):
                        o = T.ps[6 + e][:, :] if wide else T.ps[6 + u][rows(u), :]
                        c = (2 * u + e) * P if wide else 64 * u
                        n = P if wide else 64
                        for j in range(kt):
                            mm = nc.tensor.matmul(o, vs[:, j, c:c + n], pT[:, j, :], start=(j == 0),
                                                  stop=(j == kt - 1))
                    mm.then_inc(sems["summed"], 1)

        @block.vector
        def _(dve):
            link = Chain(dve, sems["dve"])
            dve.sem_inc(sems["scaled"], 2)
            dve.sem_inc(sems["dve_took"], 1)
            with dve.Fori(0, groups) as g:
                for u in range(2):
                    for m in range(4):
                        dve.wait_ge(sems["scored"], 8 * g + 4 * u + m + 1)
                        s = sc[:, u, m, :]
                        if mask is None:
                            ins = nc.vector.tensor_scalar(s, T.ps[m % 2][:, 0:keys], scale, None, ALU.mult)
                        else:
                            ins = nc.vector.scalar_tensor_tensor(out=s, in0=T.ps[m % 2][:, 0:keys], scalar=scale,
                                                                 in1=mask[:, m, :], op0=ALU.mult, op1=ALU.add)
                        ins.then_inc(sems["scaled"], 1)
                        dve.wait_ge(sems["scaled"], 8 * g + 4 * u + m + 3)
                        link(nc.vector.reduce_max(st[:, u, 0, m:m + 1], s, AX.X))
                    nc.vector.tensor_scalar(st[:, u, 0, :], st[:, u, 0, :], -1.0, None, ALU.mult).then_inc(
                        sems["maxed"], 1)
                for u in range(2):
                    dve.wait_ge(sems["exped"], 8 * g + 4 * u + 4)
                    link(nc.vector.reciprocal(st[:, u, 2, :], st[:, u, 1, :]))
                    for m in range(4):
                        s = sc[:, u, m, :]
                        ins = nc.vector.tensor_scalar(s, s, st[:, u, 2, m:m + 1], None, ALU.mult)
                        if m < 3:
                            link(ins)
                    ins.then_inc(sems["normed"], 1)
                    dve.wait_ge(sems["turned"], 2 * g + u + 1)
                    for j in range(1, kt, 2):
                        ins = nc.vector.tensor_copy(pT[:, j, :], T.ps[2 + j][:, :])
                        if j < kt - 1:
                            link(ins)
                    ins.then_inc(sems["dve_took"], 1)
                link.restart()

        @block.scalar
        def _(act):
            act.sem_inc(sems["act_took"], 1)
            act.sem_inc(sems["put"], 1)
            with act.Fori(0, groups) as g:
                for u in range(2):
                    act.wait_ge(sems["maxed"], 2 * g + u + 1)
                    for m in range(4):
                        s = sc[:, u, m, :]
                        nc.scalar.activation(s, s, ACT.Exp, bias=st[:, u, 0, m:m + 1],
                                             accum_out=st[:, u, 1, m:m + 1]).then_inc(sems["exped"], 1)
                for u in range(2):
                    act.wait_ge(sems["turned"], 2 * g + u + 1)
                    act.wait_ge(sems["put"], 2 * g + u + 1)
                    for j in range(0, kt, 2):
                        ins = nc.scalar.copy(pT[:, j, :], T.ps[2 + j][:, :])
                        if j < kt - 2:
                            ins.then_inc(sems["loaded"], 1)
                    if kt > 2:
                        act.wait_ge(sems["loaded"], 2 * g + u + 1)
                    ins.then_inc(sems["act_took"], 1)
                    act.wait_ge(sems["summed"], 2 * g + u + 1)
                    if wide:
                        for e in range(2):
                            o = out[:, ds(4 * g + 2 * u + e, 1), :].rearrange("p a t -> p (a t)")
                            ins = nc.scalar.copy(o, T.ps[6 + e][:, :])
                            if e == 0:
                                ins.then_inc(sems["loaded"], 1)
                                act.wait_ge(sems["loaded"], 2 * g + u + 1)
                    else:
                        o = out[rows(u), ds(g, 1), :].rearrange("p a t -> p (a t)")
                        ins = nc.scalar.copy(o, T.ps[6 + u][rows(u), :])
                    ins.then_inc(sems["put"], 1)


ROUTE_SEMS = "loaded turned act_took dve_took logits dve exp_in exped ranks counted ready"


def route_phase(nc, T, sems, stale, hT, M):
    E, G = N_EXPERTS, N_GROUPS
    W = G + E
    with ExitStack() as ctx:
        def sb(name, *shape):
            return ctx.enter_context(nc.sbuf_tensor(f"route_{name}", [P, *shape], F32))

        wr, bias, lg, iota = sb("w", KD, W), sb("bias", W), sb("logits", 4, W), sb("iota", E)
        before = sb("before", P)
        ge, gt, goh, pg = sb("gexp", 4, G), sb("gtie", 4, G), sb("ghot", 4, G), sb("pg", 4, 1)
        em, tie, oh1, oh2 = sb("em", 4, E), sb("tie", 4, E), sb("hot1", 4, E), sb("hot2", 4, E)
        m0, m1, m2, t1, t2, g1, g2 = (sb(n, 4, 1) for n in "m0 m1 m2 t1 t2 g1 g2".split())
        chosen, pm, many = sb("chosen", 4, E), sb("pairmax", E // 2), sb("many", MOE_ROUNDS - 1, E // 2)
        block = ctx.enter_context(nc.Block())

        @block.sync
        def _(sync):
            clear(sync, stale)
            sync.dma_start(wr[:, :, :], T.dram["router_w"]).then_inc(sems["loaded"], 16)
            sync.dma_start(bias[:, :], T.dram["router_b"].to_broadcast([P, W])).then_inc(sems["loaded"], 16)
            sync.dma_start(iota[:, :], T.dram["iota"][:, 0:E]).then_inc(sems["loaded"], 16)
            sync.dma_start(before[:, :], T.dram["before"]).then_inc(sems["loaded"], 16)
            sync.dma_start(M.slots[:, :], T.dram["iota"]).then_inc(sems["loaded"], 16)

        @block.tensor
        def _(pe):
            pe.wait_ge(sems["loaded"], 80)
            for m in range(4):
                for k in range(KD):
                    mm = nc.tensor.matmul(T.ps[7][:, m * W:m * W + W], hT[:, k, m * P:m * P + P], wr[:, k, :],
                                          start=(k == 0), stop=(k == KD - 1))
            mm.then_inc(sems["logits"], 1)
            for m in range(4):
                for half in range(2):
                    if m >= 2:
                        pe.wait_ge((sems["act_took"], sems["dve_took"])[half], m - 1)
                    for k in range(4):
                        mm = nc.tensor.transpose(T.ps[2 * (m % 2) + half][:, k * P:k * P + P],
                                                 hT[:, 4 * half + k, m * P:m * P + P], T.ident[:, :])
                    mm.then_inc(sems["turned"], 1)
            pe.wait_ge(sems["ready"], 1)
            for m in range(4):
                for n in range(m + 1):
                    mm = nc.tensor.matmul(T.ps[5][:, m * E:m * E + E], (before if n == m else T.ones)[:, :],
                                          chosen[:, n, :], start=(n == 0), stop=(n == m))
            mm.then_inc(sems["ranks"], 1)
            for n in range(4):
                mm = nc.tensor.matmul(T.ps[6][:, 0:E], T.ones[:, :], chosen[:, n, :], start=(n == 0), stop=(n == 3))
            mm.then_inc(sems["counted"], 1)

        @block.scalar
        def _(act):
            act.wait_ge(sems["exp_in"], 1)
            nc.scalar.activation(ge[:, :, :], ge[:, :, :], ACT.Exp).then_inc(sems["exped"], 1)
            for m in range(4):
                act.wait_ge(sems["turned"], 2 * m + 1)
                nc.scalar.copy(M.h_tok[:, m, 0:512], T.ps[2 * (m % 2)][:, :]).then_inc(sems["act_took"], 1)
            act.wait_ge(sems["exp_in"], 2)
            nc.scalar.activation(t1[:, :, :], t1[:, :, :], ACT.Exp).then_inc(sems["exped"], 1)

        @block.vector
        def _(dve):
            link = Chain(dve, sems["dve"])
            v = nc.vector
            dve.wait_ge(sems["loaded"], 80)
            dve.wait_ge(sems["logits"], 1)
            link(v.tensor_tensor(lg[:, :, :], T.ps[7][:, 0:4 * W].rearrange("p (m w) -> p m w", m=4),
                                 bias[:, :].unsqueeze(1).to_broadcast([P, 4, W]), ALU.add))
            gl, el = lg[:, :, 0:G], lg[:, :, G:W]

            def first_max(x, width, best, tie_, hot):
                link(v.tensor_reduce(best[:, :, :], x, AX.X, ALU.max))
                link(v.tensor_tensor(tie_[:, :, :], x, best[:, :, :].to_broadcast([P, 4, width]), ALU.is_equal))
                link(v.tensor_scalar(tie_[:, :, :], tie_[:, :, :], -100.0, None, ALU.mult))
                link(v.tensor_tensor(tie_[:, :, :], tie_[:, :, :],
                                     iota[:, 0:width].unsqueeze(1).to_broadcast([P, 4, width]), ALU.add))
                link(v.tensor_reduce(t2[:, :, :], tie_[:, :, :], AX.X, ALU.min))
                link(v.tensor_tensor(hot[:, :, :], tie_[:, :, :], t2[:, :, :].to_broadcast([P, 4, width]),
                                     ALU.is_equal))

            first_max(gl, G, m0, gt, goh)
            v.tensor_tensor(ge[:, :, :], gl, m0[:, :, :].to_broadcast([P, 4, G]), ALU.subtract).then_inc(
                sems["exp_in"], 1)
            link(v.tensor_scalar(gt[:, :, :], goh[:, :, :], 1e30, -1e30, ALU.mult, ALU.add))
            for g in range(G):
                q = slice(8 * g, 8 * g + 8)
                link(v.tensor_tensor(em[:, :, q], el[:, :, q], gt[:, :, g:g + 1].to_broadcast([P, 4, 8]), ALU.add))
            first_max(em[:, :, :], E, m1, tie, oh1)
            link(v.tensor_scalar(tie[:, :, :], oh1[:, :, :], -2e30, None, ALU.mult))
            link(v.tensor_tensor(em[:, :, :], em[:, :, :], tie[:, :, :], ALU.add))
            first_max(em[:, :, :], E, m2, tie, oh2)
            v.tensor_tensor(t1[:, :, :], m2[:, :, :], m1[:, :, :], ALU.subtract).then_inc(sems["exp_in"], 1)
            v.tensor_tensor(chosen[:, :, :], oh1[:, :, :], oh2[:, :, :], ALU.add).then_inc(sems["ready"], 1)
            for m in range(4):
                dve.wait_ge(sems["turned"], 2 * m + 2)
                v.tensor_copy(M.h_tok[:, m, 512:1024], T.ps[2 * (m % 2) + 1][:, :]).then_inc(sems["dve_took"], 1)
            dve.wait_ge(sems["exped"], 2)
            link(v.tensor_reduce(pg[:, :, :], ge[:, :, :], AX.X, ALU.add))
            link(v.reciprocal(pg[:, :, :], pg[:, :, :]))
            link(v.tensor_scalar(g1[:, :, :], t1[:, :, :], 1.0, None, ALU.add))
            link(v.reciprocal(g1[:, :, :], g1[:, :, :]))
            link(v.tensor_tensor(g1[:, :, :], g1[:, :, :], pg[:, :, :], ALU.mult))
            link(v.tensor_tensor(g2[:, :, :], g1[:, :, :], t1[:, :, :], ALU.mult))
            link(v.tensor_tensor(oh1[:, :, :], oh1[:, :, :], g1[:, :, :].to_broadcast([P, 4, E]), ALU.mult))
            link(v.tensor_tensor(oh2[:, :, :], oh2[:, :, :], g2[:, :, :].to_broadcast([P, 4, E]), ALU.mult))
            link(v.tensor_tensor(M.gates[:, :, :], oh1[:, :, :], oh2[:, :, :], ALU.add))
            link(v.tensor_scalar(tie[:, :, :], chosen[:, :, :], -BIG, BIG, ALU.mult, ALU.add))
            dve.wait_ge(sems["ranks"], 1)
            link(v.tensor_tensor(M.place[:, :, :], T.ps[5][:, 0:4 * E].rearrange("p (m e) -> p m e", m=4),
                                 tie[:, :, :], ALU.add))
            dve.wait_ge(sems["counted"], 1)
            link(v.tensor_reduce(pm[:, :], T.ps[6][:, 0:E].rearrange("p (g u) -> p g u", u=2), AX.X, ALU.max))
            for r in range(1, MOE_ROUNDS):
                link(v.tensor_scalar(many[:, r - 1, :], pm[:, :], float(SLOTS * r), None, ALU.is_gt))
            link(v.tensor_copy(M.again[:, 1:], flat(many[:, :, :])))
            link(v.tensor_reduce(t2[:, 0, :], many[:, 0, :], AX.X, ALU.max))
            link(v.tensor_copy(M.again[:, 0:1], t2[:, 0, :]))


MOE_SEMS = ("w1_full*2 w3_full*2 w2_full*2 sel_ready selT_done selT_taken gathered act_took dve_took up_done "
            "silu_done made down_done yT_act yT_dve y_turned y_act y_dve scattered added dve pool")


def experts_phase(nc, T, sems, stale, M, pairs, first_pair):
    D1, F1 = 8 * 512, 4 * 1024
    with ExitStack() as ctx:
        def sb(name, *shape):
            return ctx.enter_context(nc.sbuf_tensor(f"moe_{name}_{nc.next_id()}", [P, *shape], F32))

        w1, w3, w2 = sb("w1", 2, D1), sb("w3", 2, D1), sb("w2", 2, F1)
        sel, selg, selT = sb("sel", 4, P), sb("selg", 4, P), sb("selT", S)
        hg, sil, mid, yT, y = sb("hg", KD, P), sb("silu", 2, 256), sb("mid", 2, 256), sb("yT", KD, P), sb("y", D)
        place, gate = sb("pair_place", 4, 2), sb("pair_gate", 4, 2)
        block = ctx.enter_context(nc.Block())
        single = pairs == 1
        ps = T.ps

        def turns(eng):
            if single:
                yield 0
            else:
                with eng.Fori(0, pairs) as g:
                    yield g

        @block.sync
        def _(sync):
            clear(sync, stale)
            for g in turns(sync):
                for u in range(2):
                    e = 2 * g + u + 2 * first_pair
                    if not single:
                        sync.wait_ge(sems["made"], 2 * g + u + 1)
                    sync.dma_start(w1[:, u, :], pick(T.dram["moe_w1"], e)).then_inc(sems["w1_full"][u], 16)
                    sync.dma_start(w3[:, u, :], pick(T.dram["moe_w3"], e)).then_inc(sems["w3_full"][u], 16)
                    if not single:
                        sync.wait_ge(sems["down_done"], 2 * g + u + 1)
                    sync.dma_start(w2[:, u, :], pick(T.dram["moe_w2"], e)).then_inc(sems["w2_full"][u], 16)

        @block.gpsimd
        def _(pool):
            for g in turns(pool):
                if not single:
                    pool.wait_ge(sems["gathered"], 2 * g + 1)
                    pool.wait_ge(sems["selT_done"], g + 1)
                two = ds(2 * g + 2 * first_pair, 2)
                nc.gpsimd.tensor_copy(place[:, :, :], M.place[:, :, two]).then_inc(sems["pool"], 1)
                nc.gpsimd.tensor_copy(gate[:, :, :], M.gates[:, :, two]).then_inc(sems["pool"], 1)
                pool.wait_ge(sems["pool"], 2)
                pool.sem_clear(sems["pool"])
                for m in range(4):
                    for u in range(2):
                        c = slice(SLOTS * u, SLOTS * u + SLOTS)
                        nc.gpsimd.tensor_scalar(sel[:, m, c], M.slots[:, :], place[:, m, u:u + 1], None,
                                                ALU.is_equal)
                        ins = nc.gpsimd.tensor_scalar(selg[:, m, c], M.slots[:, :], place[:, m, u:u + 1],
                                                      gate[:, m, u:u + 1], ALU.is_equal, ALU.mult)
                ins.then_inc(sems["sel_ready"], 1)

        @block.tensor
        def _(pe):
            if not single:
                pe.sem_inc(sems["gathered"], 1)
                pe.sem_inc(sems["selT_done"], 1)
                pe.sem_inc(sems["down_done"], 2)
            credit = 0 if single else 1
            for g in turns(pe):
                pe.wait_ge(sems["sel_ready"], g + 1)
                if not single:
                    pe.wait_ge(sems["added"], KD * g + KD)
                for k in range(KD):
                    for m in range(4):
                        mm = nc.tensor.matmul(ps[k // 4][:, (k % 4) * P:(k % 4) * P + P],
                                              M.h_tok[:, m, k * P:k * P + P], sel[:, m, :], start=(m == 0),
                                              stop=(m == 3))
                    if k % 4 == 3:
                        mm.then_inc(sems["gathered"], 1)
                if not single:
                    pe.wait_ge(sems["y_act"], g + 1)
                for m in range(4):
                    mm = nc.tensor.transpose(ps[6][:, m * P:m * P + P], selg[:, m, :], T.ident[:, :])
                mm.then_inc(sems["selT_done"], 1)
                pe.wait_ge(sems["act_took"], g + 1)
                pe.wait_ge(sems["dve_took"], g + 1)
                for u in range(2):
                    c = slice(SLOTS * u, SLOTS * u + SLOTS)
                    pe.wait_ge(sems["w1_full"][u], 16 * g + 16)
                    pe.wait_ge(sems["w3_full"][u], 16 * g + 16)
                    if not single:
                        pe.wait_ge(sems["made"], 2 * g + u + 1)
                    for half, w in ((0, w1), (1, w3)):
                        for f in range(4):
                            o = half * 256 + f * SLOTS
                            for k in range(KD):
                                mm = nc.tensor.matmul(ps[2 + u][:, o:o + SLOTS],
                                                      w[:, u, k * 512 + f * P:k * 512 + f * P + P], hg[:, k, c],
                                                      start=(k == 0), stop=(k == KD - 1))
                    mm.then_inc(sems["up_done"], 1)
                if not single:
                    pe.wait_ge(sems["yT_act"], g + 1)
                    pe.wait_ge(sems["yT_dve"], g + 1)
                for u in range(2):
                    pe.wait_ge(sems["w2_full"][u], 16 * g + 16)
                    pe.wait_ge(sems["made"], 2 * g + u + 1 + (0 if single else 2))
                    for k in range(KD):
                        o = (k % 4) * P + SLOTS * u
                        for f in range(4):
                            mm = nc.tensor.matmul(ps[4 + k // 4][:, o:o + SLOTS],
                                                  w2[:, u, f * D + k * P:f * D + k * P + P],
                                                  mid[:, u, f * SLOTS:f * SLOTS + SLOTS], start=(f == 0),
                                                  stop=(f == 3))
                    mm.then_inc(sems["down_done"], 1)
                pe.wait_ge(sems["yT_act"], g + 1 + credit)
                pe.wait_ge(sems["yT_dve"], g + 1 + credit)
                pe.wait_ge(sems["selT_taken"], g + 1)
                if not single:
                    pe.wait_ge(sems["y_dve"], g + 1)
                for k in range(KD):
                    mm = nc.tensor.transpose(ps[6 + k // 4][:, (k % 4) * P:(k % 4) * P + P], yT[:, k, :],
                                             T.ident[:, :])
                mm.then_inc(sems["y_turned"], 1)
                pe.wait_ge(sems["y_act"], g + 1 + credit)
                pe.wait_ge(sems["y_dve"], g + 1 + credit)
                for k in range(KD):
                    if k >= 2:
                        pe.wait_ge(sems["added"], KD * g + k - 1 + (0 if single else KD))
                    nc.tensor.matmul(ps[k % 2][:, :], y[:, k * P:k * P + P], selT[:, :], start=True,
                                     stop=True).then_inc(sems["scattered"], 1)

        @block.scalar
        def _(act):
            if not single:
                act.sem_inc(sems["yT_act"], 1)
                act.sem_inc(sems["y_act"], 1)
            for g in turns(act):
                act.wait_ge(sems["gathered"], 2 * g + 1 + (0 if single else 1))
                nc.scalar.copy(flat(hg[:, 0:4, :]), ps[0][:, :]).then_inc(sems["act_took"], 1)
                act.wait_ge(sems["selT_done"], g + 1 + (0 if single else 1))
                if not single:
                    act.wait_ge(sems["added"], KD * g + KD)
                nc.scalar.copy(selT[:, :], ps[6][:, :]).then_inc(sems["selT_taken"], 1)
                for u in range(2):
                    act.wait_ge(sems["up_done"], 2 * g + u + 1)
                    nc.scalar.activation(sil[:, u, :], ps[2 + u][:, 0:256], ACT.Silu).then_inc(sems["silu_done"], 1)
                act.wait_ge(sems["down_done"], 2 * g + 2 + (0 if single else 2))
                nc.scalar.copy(flat(yT[:, 0:4, :]), ps[4][:, :]).then_inc(sems["yT_act"], 1)
                act.wait_ge(sems["y_turned"], g + 1)
                nc.scalar.copy(y[:, 0:512], ps[6][:, :]).then_inc(sems["y_act"], 1)

        @block.vector
        def _(dve):
            if not single:
                dve.sem_inc(sems["yT_dve"], 1)
                dve.sem_inc(sems["y_dve"], 1)
                dve.sem_inc(sems["made"], 2)
                dve.sem_inc(sems["added"], KD)
            for g in turns(dve):
                dve.wait_ge(sems["gathered"], 2 * g + 2 + (0 if single else 1))
                nc.vector.tensor_copy(flat(hg[:, 4:8, :]), ps[1][:, :]).then_inc(sems["dve_took"], 1)
                for u in range(2):
                    dve.wait_ge(sems["silu_done"], 2 * g + u + 1)
                    nc.vector.tensor_tensor(mid[:, u, :], sil[:, u, :], ps[2 + u][:, 256:512], ALU.mult).then_inc(
                        sems["made"], 1)
                dve.wait_ge(sems["down_done"], 2 * g + 2 + (0 if single else 2))
                nc.vector.tensor_copy(flat(yT[:, 4:8, :]), ps[5][:, :]).then_inc(sems["yT_dve"], 1)
                dve.wait_ge(sems["y_turned"], g + 1)
                nc.vector.tensor_copy(y[:, 512:1024], ps[7][:, :]).then_inc(sems["y_dve"], 1)
                for k in range(KD):
                    dve.wait_ge(sems["scattered"], KD * g + k + 1)
                    nc.vector.tensor_tensor(T.xT[:, k, :], T.xT[:, k, :], ps[k % 2][:, :], ALU.add).then_inc(
                        sems["added"], 1)


def gains_phase(nc, sems, stale, dst, src):
    with nc.Block() as block:
        @block.sync
        def _(sync):
            clear(sync, stale)
            sync.dma_start(dst, src).then_inc(sems["loaded"], 16)
            sync.wait_ge(sems["loaded"], 16)


def next_places_phase(nc, stale, M):
    with nc.Block() as block:
        @block.sync
        def _(sync):
            clear(sync, stale)

        @block.vector
        def _(dve):
            nc.vector.tensor_scalar(M.place[:, :, :], M.place[:, :, :], float(-SLOTS), None, ALU.add)


def block_two(nc, T):
    sems, d, xT, hT = T.sems, T.dram, T.xT, T.hT
    norm, norm2, pa, pb, down, head = (sems[n] for n in ("norm", "norm2", "pa", "pb", "down", "head"))
    gain = lambda name: T.g2[:, GCOLS[name][0]:GCOLS[name][1]]
    with ExitStack() as ctx:
        conv, rope, att = (sem_set(nc, ctx, n, names) for n, names in (("conv", CONV_SEMS), ("rope", ROPE_SEMS),
                                                                      ("att", ATT_SEMS)))
        T.g2 = ctx.enter_context(nc.sbuf_tensor("gains2", [P, NGCOL], F32))
        gains_phase(nc, head, down, T.g2[:, :], d["gains2"])
        norm_phase(nc, T, norm, head, xT, gain("final_g"), xT)
        norm_phase(nc, T, norm2, norm, xT, gain("mix_norm_g_2"), hT)
        with nc.sbuf_tensor([P, KD, S], F32) as mixed:
            with nc.sbuf_tensor([P, 6, S], F32) as att_out, nc.sbuf_tensor([P, 2, S], F32) as conv_out:
                with nc.sbuf_tensor([P, 4, S], F32) as ag:
                    project_phase(nc, T, pa, norm2, lambda c: pick(d["w_in_2"], c), 2, hT, put(ag))
                    conv_phase(nc, T, conv, pa, ag, conv_out)
                with nc.sbuf_tensor([P, 12, S], F32) as qk, nc.sbuf_tensor([P, 4, 768], F32) as vt, \
                        nc.sbuf_tensor([P, 4, S], F32) as mask:
                    project_phase(nc, T, pa, conv, lambda c: pick(d["w_in_2"], c + 2), 6, hT, put(qk),
                                  load=lambda sync, sem: sync.dma_start(mask[:, :, :], d["att_mask"]).then_inc(
                                      sem, 16))
                    token_project_phase(nc, T, pb, pa, lambda c: pick(d["w_in_2"], c + 8), 3, hT, put_tokens(vt))
                    rope_phase(nc, T, rope, pb, qk, 12)
                    attention_phase(nc, T, att, rope, qk, qk, 6, vt, att_out, 6, 1, S, HEAD_DIM ** -0.5, mask)
                norm_phase(nc, T, norm, att, conv_out, gain("conv_out_g_2"), mixed[:, 0:2, :], tiles=2)
                norm_phase(nc, T, norm2, norm, att_out, gain("attn_out_g_2"), mixed[:, 2:8, :], tiles=6)
            down_phase(nc, T, down, norm2, lambda c: pick(d["w_out_2"], c), KD, mixed, xT)
        norm_phase(nc, T, norm, down, xT, gain("xattn_norm_g_2"), hT)
        with nc.sbuf_tensor([P, KD, MEM_LEN], F32) as mem, nc.sbuf_tensor([P, KD, MEM_LEN], F32) as mem_k, \
                nc.sbuf_tensor([P, 2, D], F32) as mem_v, nc.sbuf_tensor([P, KD, S], F32) as ox:
            norm_phase(nc, T, norm2, norm, mem, gain("mem_norm_g_2"), mem, width=MEM_LEN, eps=EPS,
                       load=lambda sync, sem: sync.dma_start(mem[:, :, :], d["memT"]).then_inc(sem, 16))
            project_phase(nc, T, pa, norm2, lambda c: pick(d["w_xk_2"], c), 4, mem, put(mem_k), width=MEM_LEN)
            token_project_phase(nc, T, pb, pa, lambda c: pick(d["w_xv_2"], c), 4, mem, put_tokens(mem_v), tiles=2)
            with nc.sbuf_tensor([P, KD, S], F32) as q:
                project_phase(nc, T, pa, pb, lambda c: pick(d["w_xq_2"], c), 4, hT, put(q))
                attention_phase(nc, T, att, pa, q, mem_k, 0, mem_v, ox, 2, 4, MEM_LEN, 256 ** -0.5)
            down_phase(nc, T, down, att, lambda c: pick(d["w_xo_2"], c), KD, ox, xT)
        norm_phase(nc, T, norm, down, xT, gain("moe_norm_g_2"), hT)
    with ExitStack() as ctx:
        route, moe = sem_set(nc, ctx, "route", ROUTE_SEMS), sem_set(nc, ctx, "moe", MOE_SEMS)
        T.g2 = ctx.enter_context(nc.sbuf_tensor("gains2b", [P, NGCOL], F32))

        def sb(name, *shape, dt=F32):
            return ctx.enter_context(nc.sbuf_tensor("moe_" + name, [P, *shape], dt))

        M = Named()
        M.h_tok = sb("h", 4, D)
        M.gates, M.place = sb("gates", 4, N_EXPERTS), sb("place", 4, N_EXPERTS)
        M.slots = sb("slots", SLOTS)
        M.again = sb("again", 1 + (MOE_ROUNDS - 1) * N_EXPERTS // 2, dt=mybir.dt.int32)
        route_phase(nc, T, route, norm, hT, M)
        experts_phase(nc, T, moe, route, M, N_EXPERTS // 2, 0)
        gains_phase(nc, head, moe, T.g2[:, :], d["gains2"])
        again = nc.values_load(M.again[0:1, 0:1], min_val=0, max_val=1)
        with nc.If(again > 0):
            with nc.Fori(0, MOE_ROUNDS - 1) as r:
                next_places_phase(nc, head, M)
                with nc.Fori(0, N_EXPERTS // 2) as pair:
                    needed = nc.values_load(M.again[0:1, ds(1 + N_EXPERTS // 2 * r + pair, 1)], min_val=0,
                                            max_val=1)
                    with nc.If(needed > 0):
                        experts_phase(nc, T, moe, head, M, 1, pair)
                        with nc.Block() as block:
                            @block.sync
                            def _(sync):
                                clear(sync, moe)
        norm_phase(nc, T, norm2, head, xT, gain("final_norm_g_2"), hT)


def two_blocks(nc, dram, out):
    with ExitStack() as ctx:
        T = shared(nc, ctx, dram)
        T.sems = shared_sems(nc, ctx)
        start = T.sems["start"]
        with nc.Block() as block:
            @block.sync
            def _(sync):
                loads = [(T.xT[:, :, :], dram["xT"]), (T.ident4[:, :], dram["ident4"]),
                         (T.head_ones[:, :], dram["head_ones"]), (T.scalars[:, :], dram["scalars"])]
                for dst, src in loads:
                    sync.dma_start(dst, src).then_inc(start["loaded"], 16)
                sync.wait_ge(start["loaded"], 16 * len(loads))

            @block.gpsimd
            def _(pool):
                nc.gpsimd.memset(T.ones[:, :], 1.0)

        block_one(nc, T)
        block_two(nc, T)
        with nc.Block() as block:
            @block.sync
            def _(sync):
                clear(sync, T.sems["norm2"])
                sync.dma_start(out, T.hT[:, :, :]).then_inc(T.sems["stored"]["done"], 16)
                sync.wait_ge(T.sems["stored"]["done"], 16)


def by_feature(v):
    v = np.asarray(v)
    return np.ascontiguousarray(np.swapaxes(v.reshape(v.shape[:-1] + (v.shape[-1] // P, P)), -1, -2))


def weight_chunks(w, cols):
    w = np.asarray(w)
    lead, (k, n) = w.shape[:-2], w.shape[-2:]
    w = w.reshape(lead + (k // P, P, n // cols, cols))
    m = len(lead)
    w = w.transpose(tuple(range(m)) + (m + 2, m + 1, m, m + 3))
    return np.ascontiguousarray(w).reshape(lead + (n // cols, P, k // P * cols))


def shape_constants():
    f4 = np.float32
    s = np.arange(P)
    head, tok = s // C, s % C
    same = head[:, None] == head[None, :]
    strict = (same & (tok[:, None] < tok[None, :])).astype(f4)
    upto = (tok[:, None] <= np.arange(C)[None, :]).astype(f4)
    masks = [np.tile(strict, (1, PAIRS)), np.tile(upto, (1, 2 * PAIRS))]
    for size in [1 << n for n in range(LEVELS + 1)]:
        m = same & (tok[:, None] // (2 * size) == tok[None, :] // (2 * size)) & \
            (tok[:, None] // size % 2 == 0) & (tok[None, :] // size % 2 == 1)
        masks.append(np.tile(m.astype(f4), (1, PAIRS)))
        if size == 1:
            first = m.astype(f4)
    masks.append(np.tile(first.T, (1, PAIRS)))
    return {
        "ident4": np.tile(np.eye(P, dtype=f4), (1, 4)),
        "head_ones": same.astype(f4),
        "chunk_start": np.tile((np.arange(S) % C != 0).astype(f4), (P, 1)),
        "scalars": np.tile(np.array([[EPS, GN_EPS, LN_EPS, 8.5 * np.log(2.0)]], f4), (P, 1)),
        "rmask": np.stack(masks, 1).astype(f4),
    }


def ret_tables():
    f4 = np.float32
    inv = 1.0 / (f4(10000.0) ** np.linspace(0.0, 1.0, 32, dtype=f4))
    ang = (np.arange(S, dtype=f4)[:, None] * inv[None, :]).astype(f4)
    rep = lambda t: np.tile(t.T, (4, 1))
    rot = np.zeros((P, P), f4)
    for q in range(P):
        if q % 64 < 32:
            rot[q + 32, q] = -1.0
        else:
            rot[q - 32, q] = 1.0
    gamma = np.log(f4(1.0) - f4(2.0) ** (f4(-5.0) - np.arange(RET_HEADS, dtype=f4))).astype(np.float64)
    diff = np.arange(S)[None, :] - np.arange(P)[:, None]
    decay = np.where(diff[:, None, :] >= 0, np.exp(np.maximum(diff, 0)[:, None, :] * gamma[None, :, None]), 0.0)
    return {"ret_cossin": np.stack([rep(np.cos(ang)), rep(np.sin(ang))], 1).astype(f4), "rot": rot,
            "ret_decay": (decay * 64 ** -0.5).astype(f4)}


def layout(a):
    a = {k: np.asarray(v) for k, v in a.items()}
    L = DEPTH
    flat2 = lambda n: a[n].reshape(L, -1)
    out = shape_constants()
    out["layer_cols"] = np.concatenate(
        [by_feature(flat2(n)) for n in ("norm1_g", "rw_mu", "rw_w0", "rw_a0", "rw_k_k", "rw_k_a", "rw_r_k",
                                        "rw_lnx_g", "rw_lnx_b", "norm2_g")], axis=-1)
    low = np.concatenate([a["rw_w_up"], a["rw_a_up"]], axis=1)
    out.update(ret_tables())
    x = a["x"][0]
    out["xT"] = np.ascontiguousarray(x.reshape(S, KD, P).transpose(2, 1, 0))
    w_in = weight_chunks(a["w_in"], 256)
    first_gate = (RW_T * P + 1536 + 1024) // 256
    gates = w_in[:, first_gate:]
    out["w_in"] = w_in[:, :first_gate]
    out["w_merge"] = np.concatenate([gates, weight_chunks(a["w_branch"], 256).reshape(L, 12, P, -1)], axis=-1)
    out["w_out"] = weight_chunks(a["w_out"], P)
    up = a["ffn_w_up"]
    gate, val = (weight_chunks(up[:, :, o:o + D_FF], P).reshape(L, FT, P, KD, P) for o in (0, D_FF))
    out["ffn_up"] = np.concatenate([gate, val], axis=-1).reshape(L, FT, P, KD * 256)
    out["ffn_down"] = weight_chunks(a["ffn_w_down"], P)
    taps = np.concatenate([a["ffn_conv_w"], a["ffn_conv_b"][:, None]], axis=1)
    taps = taps.reshape(L, 4, 2, FT, P).transpose(0, 4, 3, 2, 1)
    out["ffn_conv"] = np.ascontiguousarray(taps).reshape(L, P, FT, 8)
    out["sg_wT"] = np.ascontiguousarray(a["sg_w_s"].transpose(0, 3, 1, 2)).reshape(L, P, S)
    out["sg_rows"] = np.concatenate([a["sg_ln_g"], a["sg_ln_b"], a["sg_b"].reshape(L, -1)], axis=-1)
    out["causal"] = np.tile((np.arange(P)[:, None] <= np.arange(P)[None, :]).astype(np.float32), (1, 4))
    out["gains2"] = np.concatenate([by_feature(a[n].reshape(-1)) for n in GCOLS], axis=-1)
    out["w_in_2"] = weight_chunks(a["w_in_2"][0], 256)
    for n in ("w_xq_2", "w_xk_2", "w_xv_2"):
        out[n] = weight_chunks(a[n][0], 256)
    for n in ("w_out_2", "w_xo_2"):
        out[n] = weight_chunks(a[n][0], P)
    par = np.concatenate([a["conv_dw_w_2"][0], a["conv_dw_b_2"], a["conv_ln_g_2"], a["conv_ln_b_2"]], axis=0)
    out["conv_par"] = np.ascontiguousarray(par.reshape(CONV_KERNEL + 3, 2, P).transpose(2, 1, 0))
    out["positions"] = a["positions_2"].reshape(1, S)
    out["memT"] = np.ascontiguousarray(a["mem_2"][0].reshape(MEM_LEN, KD, P).transpose(2, 1, 0))
    inv = 1.0 / (np.float32(10000.0) ** (np.arange(32, dtype=np.float32) * np.float32(2.0 / 64)))
    out["rope_inv"] = np.tile(inv.astype(np.float32), 4)[:, None]
    off = np.abs(np.arange(S)[:, None] - np.arange(S)[None, :])
    seen = (off <= 64).astype(int) + ((off <= 256) & (off % 4 == 0)) + (off % 16 == 0)
    mask = np.where(seen > 0, np.log(np.maximum(seen, 1)), -1e30).astype(np.float32)
    out["att_mask"] = np.ascontiguousarray(mask.reshape(4, P, S).transpose(1, 0, 2))
    out["router_w"] = np.ascontiguousarray(np.concatenate([a["w_group_2"][0], a["w_router_2"][0]], axis=-1).reshape(
        KD, P, -1).transpose(1, 0, 2))
    out["router_b"] = np.concatenate([a["b_group_2"], a["b_router_2"]], axis=-1)
    out["iota"] = np.tile(np.arange(SLOTS, dtype=np.float32), (P, 1))
    out["before"] = (np.arange(P)[:, None] < np.arange(P)[None, :]).astype(np.float32)
    for n in ("w1_2", "w3_2", "w2_2"):
        w = a[n][0]
        out["moe_" + n[:2]] = np.ascontiguousarray(w.reshape(N_EXPERTS, -1, P, w.shape[-1]).transpose(
            0, 2, 1, 3)).reshape(N_EXPERTS, P, -1)
    out["rw_up"] = np.stack([low, a["rw_g_up"]], axis=2)
    return out


def kernel(**inputs):
    import concourse.bacc as bacc
    from concourse.bass_utils import run_bass_kernel_spmd

    nc = bacc.Bacc("TRN2", target_bir_lowering=False, num_devices=1)
    arrays = {f"in_{name}": a for name, a in layout(inputs).items()}
    dram = {name[3:]: nc.dram_tensor(name, a.shape, mybir.dt.from_np(a.dtype), kind="ExternalInput").ap()
            for name, a in arrays.items()}
    out = nc.dram_tensor("out", (P, KD, S), F32, kind="ExternalOutput").ap()
    two_blocks(nc, dram, out)
    got = run_bass_kernel_spmd(nc, [arrays], core_ids=[0]).results[0]["out"]
    return np.ascontiguousarray(got.transpose(2, 1, 0)).reshape(1, S, D)
```

```python
from contextlib import ExitStack

import numpy as np

import concourse.bass as bass
from concourse import mybir

F32 = mybir.dt.float32
F32R = mybir.dt.float32r
ALU = mybir.AluOpType
ACT = mybir.ActivationFunctionType
AX = mybir.AxisListType

P = 128
D = 1024
S = 512
KD = D // P
DEPTH = 2
RW_W = 512
RW_T = 14
PAIRS = RW_W // P
C = 64
NCH = S // C
LEVELS = 5
GN_EPS = 64e-5
LN_EPS = 1e-5
EPS = 1e-6
DECAY = float(np.exp(-0.5))
RET_HEADS = 4
SG_GROUPS = 4
D_FF = 2816
FT = D_FF // P
CONV_CH = 256
CONV_KERNEL = 31
HEAD_DIM = 64
ATT_W = 768
MEM_LEN = 256
N_GROUPS = 4
N_EXPERTS = 32
SLOTS = 64
MOE_ROUNDS = S // SLOTS
BIG = 16384.0
TWO_PI = (6.28125, 0.0019353032, 2 * np.pi - 6.28125 - 0.0019353032)
ds = bass.ds

LCOLS = {}
_n = 0
for _name, _k in (("norm1_g", 8), ("mu", 14), ("w0", 4), ("a0", 4), ("k_k", 4), ("k_a", 4), ("r_k", 4),
                  ("lnx_g", 4), ("lnx_b", 4), ("norm2_g", 8)):
    LCOLS[_name] = (_n, _n + _k)
    _n += _k
NLCOL = _n

GCOLS = {}
_n = 0
for _name, _k in (("final_g", 8), ("mix_norm_g_2", 8), ("conv_out_g_2", 2), ("attn_out_g_2", 6),
                  ("xattn_norm_g_2", 8), ("mem_norm_g_2", 8), ("moe_norm_g_2", 8), ("final_norm_g_2", 8)):
    GCOLS[_name] = (_n, _n + _k)
    _n += _k
NGCOL = _n


class Chain:

    def __init__(self, eng, sem):
        self.eng, self.sem, self.n = eng, sem, 0

    def __call__(self, ins):
        self.n += 1
        ins.then_inc(self.sem, 1)
        self.eng.wait_ge(self.sem, self.n)

    def restart(self):
        self.eng.sem_clear(self.sem)
        self.n = 0


def two_slots(eng, n):
    if n // 2:
        with eng.Fori(0, n // 2) as i:
            for s in (0, 1):
                yield i, s
    if n % 2:
        yield n // 2, 0


def flat(ap):
    return ap.rearrange("p a b -> p (a b)")


class Named:
    pass


def clear(sync, sems):
    for s in sems["all"]:
        sync.sem_clear(s)


def sem_set(nc, ctx, prefix, names):
    named, every = {}, []
    for n in names.split():
        n, _, k = n.partition("*")
        made = [ctx.enter_context(nc.semaphore(f"{prefix}_{n}{i if k else ''}")) for i in range(int(k or 1))]
        named[n] = made if k else made[0]
        every += made
    return {"all": every, **named}


def rsqrt(act, sem, before, out, sums, scale, eps):
    act.activation(out, sums, ACT.Ln, bias=eps, scale=scale).then_inc(sem, 1)
    act.wait_ge(sem, before + 1)
    act.activation(out, out, ACT.Exp, scale=-0.5).then_inc(sem, 1)


NORM_SEMS = "loaded squared summed rooted"


def norm_phase(nc, T, sems, stale, src, gain, dst, tiles=KD, width=S, eps=EPS, load=None, mean_of=None):
    n_feat = (mean_of or tiles * P)
    with nc.sbuf_tensor([P, tiles, width], F32) as sq, nc.sbuf_tensor([P, width], F32) as rstd, \
            nc.Block() as block:
        @block.sync
        def _(sync):
            clear(sync, stale)
            if load is not None:
                load(sync, sems["loaded"])

        @block.scalar
        def _(act):
            if load is not None:
                act.wait_ge(sems["loaded"], 16)
            for k in range(tiles):
                nc.scalar.activation(sq[:, k, :], src[:, k, :], ACT.Square).then_inc(sems["squared"], 1)
            act.wait_ge(sems["summed"], 1)
            rsqrt(act, sems["rooted"], 0, rstd[:, :], T.ps[0][:, 0:width], 1.0 / n_feat, T.eps(eps))

        @block.tensor
        def _(pe):
            for k in range(tiles):
                pe.wait_ge(sems["squared"], k + 1)
                mm = nc.tensor.matmul(T.ps[0][:, 0:width], T.ones[:, :], sq[:, k, :], start=(k == 0),
                                      stop=(k == tiles - 1))
            mm.then_inc(sems["summed"], 1)

        @block.vector
        def _(dve):
            if load is not None:
                dve.wait_ge(sems["loaded"], 16)
            dve.wait_ge(sems["rooted"], 2)
            for k in range(tiles):
                nc.vector.scalar_tensor_tensor(out=dst[:, k, :], in0=src[:, k, :], scalar=gain[:, k:k + 1],
                                               in1=rstd[:, :], op0=ALU.mult, op1=ALU.mult)


SPLIT_SEMS = "w_full*2 w_hi w_lo rhs_hi rhs_lo"


class Split:

    def __init__(self, nc, ctx, T, sems, kt, rhs_hi=None, rhs_lo=None, width=S):
        self.nc, self.T, self.sems, self.kt, self.rhs_tiles = nc, T, sems, kt, 0
        n = nc.next_id()

        def part(name, *shape):
            return ctx.enter_context(nc.sbuf_tensor(f"{name}_{n}", [P, *shape], F32R))

        self.w_hi, self.w_lo = part("w_hi", 2, kt, P), part("w_lo", 2, kt, P)
        self.rhs_hi, self.rhs_lo = rhs_hi, rhs_lo
        if rhs_hi is None:
            self.rhs_hi, self.rhs_lo = part("rhs_hi", kt, width), part("rhs_lo", kt, width)
            self.rhs_tiles = kt

    def raw(self, s, c, cols):
        return self.T.w[:, s, 0:self.kt * cols].rearrange("p (k c) -> p k c", k=self.kt)[:, :, c:c + P]

    def high(self, raw, t):
        self.nc.scalar.copy(self.w_hi[:, t, :, :], raw).then_inc(self.sems["w_hi"], 1)

    def low(self, pool, n, raw, t):
        pool.wait_ge(self.sems["w_hi"], n + 1)
        self.nc.gpsimd.tensor_tensor(self.w_lo[:, t, :, :], raw, self.w_hi[:, t, :, :].bitcast(F32),
                                     ALU.subtract).then_inc(self.sems["w_lo"], 1)

    def rhs(self, dve, rhs):
        for k in range(self.kt):
            self.nc.vector.tensor_copy(self.rhs_hi[:, k, :], rhs[:, k, :]).then_inc(self.sems["rhs_hi"], 1)
        dve.wait_ge(self.sems["rhs_hi"], self.kt)
        for k in range(self.kt):
            self.nc.vector.tensor_tensor(self.rhs_lo[:, k, :], rhs[:, k, :], self.rhs_hi[:, k, :].bitcast(F32),
                                         ALU.subtract).then_inc(self.sems["rhs_lo"], 1)

    def products(self, pe, bank, n, lows, t):
        hi, lo, kt = self.w_hi, self.w_lo, self.kt
        pe.wait_ge(self.sems["w_hi"], n + 1)
        for k in range(kt):
            self.nc.tensor.matmul(bank, hi[:, t, k, :], self.rhs_hi[:, k, :], start=(k == 0), stop=False)
        if self.rhs_tiles:
            pe.wait_ge(self.sems["rhs_lo"], self.rhs_tiles)
        for k in range(kt):
            self.nc.tensor.matmul(bank, hi[:, t, k, :], self.rhs_lo[:, k, :], start=False, stop=False)
        pe.wait_ge(self.sems["w_lo"], lows)
        for k in range(kt):
            mm = self.nc.tensor.matmul(bank, lo[:, t, k, :], self.rhs_hi[:, k, :], start=False, stop=(k == kt - 1))
        return mm


def with_next(eng, n):
    last = (n - 1) // 2
    if last:
        with eng.Fori(0, last) as i:
            yield (i, 0), (i, 1)
            yield (i, 1), (i + 1, 0)
    if n % 2 == 0:
        yield (last, 0), (last, 1)
    yield (last, (n - 1) % 2), None


PROJECT_SEMS = SPLIT_SEMS + " loaded act_took dve_took even_done odd_done"


def project_phase(nc, T, sems, stale, weights, chunks, rhs, write, kt=KD, width=S, load=None):
    done = (sems["even_done"], sems["odd_done"])
    with ExitStack() as ctx:
        split = Split(nc, ctx, T, sems, kt, width=width)
        block = ctx.enter_context(nc.Block())

        @block.sync
        def _(sync):
            clear(sync, stale)
            if load is not None:
                load(sync, sems["loaded"])
            for i, s in two_slots(sync, chunks):
                sync.wait_ge(sems["w_lo"], 4 * i + 2 * s + 2)
                sync.dma_start(T.w[:, s, 0:kt * 256], weights(2 * i + s)).then_inc(sems["w_full"][s], 16)

        @block.gpsimd
        def _(pool):
            pool.sem_inc(sems["w_lo"], 4)
            for i, s in two_slots(pool, chunks):
                for t in range(2):
                    split.low(pool, 4 * i + 2 * s + t, split.raw(s, t * P, 256), t)

        @block.tensor
        def _(pe):
            pe.sem_inc(done[0], 1)
            pe.sem_inc(done[1], 1)
            pe.wait_ge(sems["rhs_hi"], kt)
            for i, s in two_slots(pe, chunks):
                for t in range(2):
                    pe.wait_ge((sems["act_took"], sems["dve_took"])[t], 2 * i + s + 1)
                    n = 4 * i + 2 * s + t
                    split.products(pe, T.ps[2 * s + t][:, 0:width], n, n + 5, t).then_inc(done[t], 1)

        @block.scalar
        def _(act):
            act.sem_inc(sems["act_took"], 2)
            if load is not None:
                act.wait_ge(sems["loaded"], 16)

            def high(i, s, t):
                act.wait_ge(sems["w_full"][s], 16 * i + 16)
                act.wait_ge(done[t], 2 * i + s + 1)
                split.high(split.raw(s, t * P, 256), t)

            high(0, 0, 0)
            high(0, 0, 1)
            for (i, s), behind in with_next(act, chunks):
                if behind:
                    high(*behind, 0)
                act.wait_ge(done[0], 2 * i + s + 2)
                write(nc.scalar, 2 * i + s, 0, T.ps[2 * s][:, 0:width]).then_inc(sems["act_took"], 1)
                if behind:
                    high(*behind, 1)

        @block.vector
        def _(dve):
            dve.sem_inc(sems["dve_took"], 2)
            split.rhs(dve, rhs)
            if load is not None:
                dve.wait_ge(sems["loaded"], 16)
            for i, s in two_slots(dve, chunks):
                dve.wait_ge(done[1], 2 * i + s + 2)
                write(nc.vector, 2 * i + s, 1, T.ps[2 * s + 1][:, 0:width]).then_inc(sems["dve_took"], 1)


def token_project_phase(nc, T, sems, stale, weights, chunks, lhs, write, tiles=4):
    with nc.Block() as block:
        @block.sync
        def _(sync):
            clear(sync, stale)
            for i, s in two_slots(sync, chunks):
                sync.wait_ge(sems["dve_took"], 2 * i + s + 1)
                sync.dma_start(T.w[:, s, 0:KD * 256], weights(2 * i + s)).then_inc(sems["w_full"][s], 16)

        @block.tensor
        def _(pe):
            for i, s in two_slots(pe, chunks):
                pe.wait_ge(sems["w_full"][s], 16 * i + 16)
                pe.wait_ge(sems["act_took"], 2 * i + s + 1)
                pe.wait_ge(sems["dve_took"], 2 * i + s + 1)
                for m in range(tiles):
                    for k in range(KD):
                        mm = nc.tensor.matmul(T.ps[4 * s + m][:, 0:256], lhs[:, k, m * P:m * P + P],
                                              T.w[:, s, k * 256:k * 256 + 256], start=(k == 0), stop=(k == KD - 1))
                    mm.then_inc((sems["even_done"], sems["odd_done"])[m % 2], 1)

        @block.scalar
        def _(act):
            act.sem_inc(sems["act_took"], 2)
            for i, s in two_slots(act, chunks):
                for m in range(0, tiles, 2):
                    act.wait_ge(sems["even_done"], (2 * i + s) * (tiles // 2) + m // 2 + 1)
                    w = write(nc.scalar, 2 * i + s, m, T.ps[4 * s + m][:, 0:256])
                w.then_inc(sems["act_took"], 1)

        @block.vector
        def _(dve):
            dve.sem_inc(sems["dve_took"], 2)
            for i, s in two_slots(dve, chunks):
                for m in range(1, tiles, 2):
                    dve.wait_ge(sems["odd_done"], (2 * i + s) * (tiles // 2) + m // 2 + 1)
                    w = write(nc.vector, 2 * i + s, m, T.ps[4 * s + m][:, 0:256])
                w.then_inc(sems["dve_took"], 1)


def copied(eng, dst, src):
    return eng.copy(dst, src) if eng.engine == mybir.EngineType.Activation else eng.tensor_copy(dst, src)


def rwkv_prep_phase(nc, T, sems, stale, R):
    p = R.p
    col = lambda name, j: T.lc[:, LCOLS[name][0] + j:LCOLS[name][0] + j + 1]
    with nc.sbuf_tensor([P, 2, RW_W], F32) as up, nc.sbuf_tensor([P, 2, S], F32) as tmp, \
            nc.sbuf_tensor([P, PAIRS, S], F32) as w, nc.sbuf_tensor([P, PAIRS, S], F32) as a, \
            nc.sbuf_tensor([P, PAIRS, S], F32) as norm, \
            nc.sbuf_tensor([P, 2, S], F32) as sq, nc.sbuf_tensor([P, 2, S], F32) as rk, \
            nc.sbuf_tensor([P, 4], F32) as one_less_ka, nc.sbuf_tensor([P, S], F32) as chunk_start, \
            nc.Block() as block:
        @block.sync
        def _(sync):
            clear(sync, stale)
            sync.dma_start(up[:, :, :], R.up()).then_inc(sems["loaded"], 16)
            sync.dma_start(chunk_start[:, :], T.dram["chunk_start"]).then_inc(sems["loaded"], 16)

        @block.vector
        def _(dve):
            link = Chain(dve, sems["dve"])
            dve.wait_ge(sems["loaded"], 32)
            for n, t in enumerate((12, 13) + tuple(range(12))):
                d = tmp[:, n % 2, :]
                nc.vector.tensor_tensor(d[:, 1:S], p[:, t, 0:S - 1], p[:, t, 1:S], ALU.subtract)
                link(nc.vector.tensor_scalar(d[:, 0:1], p[:, t, 0:1], -1.0, None, ALU.mult))
                nc.vector.scalar_tensor_tensor(out=p[:, t, :], in0=d, scalar=col("mu", t), in1=p[:, t, :],
                                               op0=ALU.mult, op1=ALU.add).then_inc(sems["shifted"], 1)
            dve.wait_ge(sems["shifted"], 14)
            link(nc.vector.tensor_scalar(one_less_ka[:, :], T.lc[:, LCOLS["k_a"][0]:LCOLS["k_a"][1]], -1.0, 1.0,
                                         ALU.mult, ALU.add))
            for j in range(PAIRS):
                r, k, v = p[:, j, :], p[:, 4 + j, :], p[:, 8 + j, :]
                kk = R.alpha[:, j, :]
                link(nc.vector.tensor_scalar(kk, k, col("k_k", j), None, ALU.mult))
                if j >= 2:
                    dve.wait_ge(sems["kk_summed"], j - 1)
                nc.vector.tensor_tensor(sq[:, j % 2, :], kk, kk, ALU.mult).then_inc(sems["kk_squared"], 1)
                dve.wait_ge(sems["rate_ready"], j + 1)
                d = tmp[:, 0, :]
                link(nc.vector.tensor_scalar(d, a[:, j, :], col("k_a", j), one_less_ka[:, j:j + 1], ALU.mult,
                                             ALU.add))
                link(nc.vector.tensor_tensor(k, k, d, ALU.mult))
                if j >= 2:
                    dve.wait_ge(sems["rk_summed"], j - 1)
                nc.vector.scalar_tensor_tensor(out=rk[:, j % 2, :], in0=r, scalar=col("r_k", j), in1=k,
                                               op0=ALU.mult, op1=ALU.mult).then_inc(sems["rk_ready"], 1)
                dve.wait_ge(sems["kk_summed"], j + 1)
                nc.vector.tensor_scalar(norm[:, j, :], T.ps[4 + j % 2][:, :], 1e-24, None, ALU.max).then_inc(
                    sems["norm_guarded"], 1)
                dve.wait_ge(sems["decay_ready"], j + 1)
                nc.vector.tensor_tensor_scan(w[:, j, :], chunk_start[:, :], w[:, j, :], 0.0, ALU.mult,
                                             ALU.add).then_inc(sems["decay_scanned"], 1)
                dve.wait_ge(sems["norm_rooted"], 2 * j + 2)
                link(nc.vector.tensor_tensor(kk, kk, norm[:, j, :], ALU.mult))
                link(nc.vector.tensor_tensor(d, kk, a[:, j, :], ALU.mult))
                run = R.run[:, j, :]
                dve.wait_ge(sems["run_ready"], 2 * j + 2)
                nc.vector.tensor_tensor(R.beta[:, j, :], d, w[:, j, :], ALU.mult)
                nc.vector.tensor_tensor(R.kappa[:, j, :], k, w[:, j, :], ALU.mult)
                nc.vector.tensor_tensor(R.rho[:, j, :], r, run, ALU.mult)
                link(nc.vector.tensor_copy(tmp[:, 1, 0:S:C], kk[:, 0:S:C]))
                nc.vector.tensor_tensor(tmp[:, 0, 1:S], kk[:, 1:S], run[:, 0:S - 1], ALU.mult)
                link(nc.vector.tensor_copy(tmp[:, 0, 0:1], kk[:, 0:1]))
                link(nc.vector.tensor_copy(R.alpha[:, j, :], tmp[:, 0, :]))
                link(nc.vector.tensor_copy(R.alpha[:, j, 0:S:C], tmp[:, 1, 0:S:C]))
                dve.wait_ge(sems["rk_summed"], j + 1)
                nc.vector.tensor_tensor(R.bonus[:, j, :], T.ps[6 + j % 2][:, :], v, ALU.mult).then_inc(
                    sems["bonus_done"], 1)

        @block.scalar
        def _(act):
            act.wait_ge(sems["shifted"], 2)
            nc.scalar.activation(p[0:64, 12, :], p[0:64, 12, :], ACT.Tanh).then_inc(sems["low_ready"], 1)
            nc.scalar.activation(p[:, 13, :], p[:, 13, :], ACT.Sigmoid).then_inc(sems["low_ready"], 1)
            for j in range(PAIRS):
                act.wait_ge(sems["decay_summed"], j + 1)
                nc.scalar.activation(w[:, j, :], T.ps[0][:, :], ACT.Sigmoid, bias=col("w0", j)).then_inc(
                    sems["decay_ready"], 1)
                act.wait_ge(sems["rate_summed"], j + 1)
                nc.scalar.activation(a[:, j, :], T.ps[1][:, :], ACT.Sigmoid, bias=col("a0", j)).then_inc(
                    sems["rate_ready"], 1)
                act.wait_ge(sems["gate_summed"], j + 1)
                nc.scalar.copy(R.gate[:, j, :], T.ps[2][:, :]).then_inc(sems["gate_taken"], 1)
            for j in range(PAIRS):
                act.wait_ge(sems["norm_guarded"], j + 1)
                nc.scalar.activation(norm[:, j, :], norm[:, j, :], ACT.Ln, scale=2.0 ** 17).then_inc(
                    sems["norm_rooted"], 1)
                act.wait_ge(sems["norm_rooted"], 2 * j + 1)
                nc.scalar.activation(norm[:, j, :], norm[:, j, :], ACT.Exp, scale=-0.5,
                                     bias=T.half_17ln2[:, :]).then_inc(sems["norm_rooted"], 1)
                act.wait_ge(sems["decay_scanned"], j + 1)
                nc.scalar.activation(R.run[:, j, :], w[:, j, :], ACT.Exp, scale=-DECAY).then_inc(sems["run_ready"], 1)
                nc.scalar.activation(w[:, j, :], w[:, j, :], ACT.Exp, scale=DECAY).then_inc(sems["run_ready"], 1)

        @block.tensor
        def _(pe):
            pe.wait_ge(sems["loaded"], 32)
            pe.wait_ge(sems["low_ready"], 2)
            for j in range(PAIRS):
                if j:
                    pe.wait_ge(sems["decay_ready"], j)
                    pe.wait_ge(sems["rate_ready"], j)
                    pe.wait_ge(sems["gate_taken"], j)
                o = slice(j * P, j * P + P)
                nc.tensor.matmul(T.ps[0][:, :], up[0:64, 0, o], p[0:64, 12, :], start=True, stop=True).then_inc(
                    sems["decay_summed"], 1)
                nc.tensor.matmul(T.ps[1][:, :], up[64:128, 0, o], p[64:128, 12, :], start=True,
                                 stop=True).then_inc(sems["rate_summed"], 1)
                nc.tensor.matmul(T.ps[2][:, :], up[:, 1, o], p[:, 13, :], start=True, stop=True).then_inc(
                    sems["gate_summed"], 1)
            for j in range(PAIRS):
                if j >= 2:
                    pe.wait_ge(sems["bonus_done"], j - 1)
                pe.wait_ge(sems["kk_squared"], j + 1)
                nc.tensor.matmul(T.ps[4 + j % 2][:, :], T.head_ones[:, :], sq[:, j % 2, :], start=True,
                                 stop=True).then_inc(sems["kk_summed"], 1)
                pe.wait_ge(sems["rk_ready"], j + 1)
                nc.tensor.matmul(T.ps[6 + j % 2][:, :], T.head_ones[:, :], rk[:, j % 2, :], start=True,
                                 stop=True).then_inc(sems["rk_summed"], 1)


RWKV_PREP_SEMS = ("loaded shifted dve low_ready norm_guarded norm_rooted decay_scanned run_ready decay_summed rate_summed gate_summed rate_ready gate_taken "
                  "decay_ready kk_squared kk_summed rk_ready rk_summed bonus_done")


def rwkv_chunk_phases(nc, T, pre, rec, R):
    with ExitStack() as ctx:
        def sb(name, *shape):
            return ctx.enter_context(nc.sbuf_tensor(f"rec_{name}", [P, *shape], F32))

        aB, bB, kB, vB, M, LT, AkT, X, XT, T1, bT, kT, vT, Rs, Un = (
            sb(n, PAIRS, P) for n in "aB bB kB vB M LT AkT X XT T1 bT kT vT Rs Un".split())
        rho, BT, ArT, PC = sb("rho", PAIRS, C), sb("BT", 2, PAIRS * P), sb("ArT", 2, PAIRS, C), sb("PC", PAIRS, 1)
        rmask = sb("masks", LEVELS + 4, S)
        ps = T.ps

        def pair(j):
            return slice(j * P, j * P + P)

        with nc.Block() as block:
            @block.sync
            def _(sync):
                clear(sync, rec["stale"])
                sync.dma_start(rmask[:, :, :], T.dram["rmask"]).then_inc(rec["masks_loaded"], 16)
                sync.wait_ge(rec["masks_loaded"], 16)

            @block.gpsimd
            def _(pool):
                for t in (aB, bB, kB, vB, M):
                    nc.gpsimd.memset(t[:, :, :], 0.0)

        with nc.Fori(0, NCH) as c:
            with nc.Block() as block:
                @block.sync
                def _(sync):
                    clear(sync, rec)

                @block.scalar
                def _(act):
                    now = ds(c * C, C)
                    for h in range(2):
                        q = slice(64 * h, 64 * h + 64)
                        nc.scalar.copy(aB[q, :, 64 * h:64 * h + 64], R.alpha[q, :, now]).then_inc(pre["blocks_act"], 1)
                        nc.scalar.copy(kB[q, :, 64 * h:64 * h + 64], R.kappa[q, :, now]).then_inc(pre["blocks_act"], 1)
                    nc.scalar.copy(PC[:, :, :], R.run[:, :, ds(c * C + C - 1, 1)])
                    for n, t in enumerate((bT, kT, vT)):
                        act.wait_ge(pre["turned"], n + 1)
                        nc.scalar.copy(flat(t[:, :, :]), ps[4 + n][:, :])
                    for lev in range(LEVELS):
                        act.wait_ge(pre["t1_done"], lev + 1)
                        nc.scalar.copy(flat(T1[:, :, :]), ps[0][:, :]).then_inc(pre["t1_taken"], 1)

                @block.gpsimd
                def _(pool):
                    pool.wait_ge(pre["lt_ready"], 1)
                    for lev in range(LEVELS):
                        if lev >= 2:
                            pool.wait_ge(pre["t1_done"], lev - 1)
                        nc.gpsimd.tensor_tensor(BT[:, lev % 2, :], flat(LT[:, :, :]), rmask[:, 3 + lev, :],
                                                ALU.mult).then_inc(pre["bt_ready"], 1)

                @block.vector
                def _(dve):
                    link = Chain(dve, pre["dve"])
                    now = ds(c * C, C)
                    for h in range(2):
                        q = slice(64 * h, 64 * h + 64)
                        nc.vector.tensor_copy(bB[q, :, 64 * h:64 * h + 64], R.beta[q, :, now]).then_inc(
                            pre["blocks_dve"], 1)
                        nc.vector.tensor_copy(vB[q, :, 64 * h:64 * h + 64], R.p[q, 8:12, now]).then_inc(
                            pre["blocks_dve"], 1)
                    nc.vector.tensor_copy(rho[:, :, :], R.rho[:, :, now]).then_inc(pre["blocks_dve"], 1)
                    dve.wait_ge(pre["products"], 1)
                    link(nc.vector.tensor_tensor(flat(LT[:, :, :]), ps[0][:, :], rmask[:, 0, :], ALU.mult))
                    dve.sem_inc(pre["lt_ready"], 1)
                    link(nc.vector.tensor_tensor(flat(XT[:, :, :]), flat(LT[:, :, :]), rmask[:, 2, :], ALU.mult))
                    link(nc.vector.tensor_tensor(flat(XT[:, :, :]), T.ident4[:, :], flat(XT[:, :, :]), ALU.subtract))
                    dve.wait_ge(pre["products"], 2)
                    link(nc.vector.tensor_tensor(flat(X[:, :, :]), ps[1][:, :], rmask[:, 8, :], ALU.mult))
                    nc.vector.tensor_tensor(flat(X[:, :, :]), T.ident4[:, :], flat(X[:, :, :]),
                                            ALU.subtract).then_inc(pre["x_ready"], 1)
                    dve.wait_ge(pre["products"], 3)
                    nc.vector.tensor_tensor(flat(AkT[:, :, :]), ps[2][:, :], rmask[:, 0, :], ALU.mult)
                    dve.wait_ge(pre["products"], 4)
                    nc.vector.tensor_tensor(ArT[:, :, :, :].rearrange("p a b c -> p (a b c)"), ps[3][:, :],
                                            rmask[:, 1, :], ALU.mult)
                    for lev in range(LEVELS):
                        dve.wait_ge(pre["xt_done"], lev + 1)
                        if lev < LEVELS - 1:
                            nc.vector.tensor_tensor(flat(X[:, :, :]), flat(X[:, :, :]), ps[1][:, :], ALU.subtract)
                        nc.vector.tensor_tensor(flat(XT[:, :, :]), flat(XT[:, :, :]), ps[7][:, :],
                                                ALU.subtract).then_inc(pre["x_ready"], 1)

                @block.tensor
                def _(pe):
                    pe.wait_ge(pre["blocks_act"], 4)
                    pe.wait_ge(pre["blocks_dve"], 5)
                    for bank, lhs, rhs in ((0, bB, aB), (1, aB, bB), (2, kB, aB)):
                        for j in range(PAIRS):
                            mm = nc.tensor.matmul(ps[bank][:, pair(j)], lhs[:, j, :], rhs[:, j, :], start=True,
                                                  stop=True)
                        mm.then_inc(pre["products"], 1)
                    for n, lhs in enumerate((bB, kB)):
                        for j in range(PAIRS):
                            mm = nc.tensor.matmul(ps[3][:, (4 * n + j) * C:(4 * n + j + 1) * C], lhs[:, j, :],
                                                  rho[:, j, :], start=True, stop=True)
                    mm.then_inc(pre["products"], 1)
                    for n, src in enumerate((bB, kB, vB)):
                        for j in range(PAIRS):
                            mm = nc.tensor.transpose(ps[4 + n][:, pair(j)], src[:, j, :], T.ident[:, :])
                        mm.then_inc(pre["turned"], 1)
                    for lev in range(LEVELS):
                        pe.wait_ge(pre["bt_ready"], lev + 1)
                        pe.wait_ge(pre["x_ready"], lev + 1)
                        for j in range(PAIRS):
                            mm = nc.tensor.matmul(ps[0][:, pair(j)], BT[:, lev % 2, pair(j)], X[:, j, :],
                                                  start=True, stop=True)
                        mm.then_inc(pre["t1_done"], 1)
                        pe.wait_ge(pre["t1_taken"], lev + 1)
                        for bank, lhs, rhs in ((1, XT, T1), (7, T1, XT)):
                            if bank == 1 and lev == LEVELS - 1:
                                continue
                            for j in range(PAIRS):
                                mm = nc.tensor.matmul(ps[bank][:, pair(j)], lhs[:, j, :], rhs[:, j, :],
                                                      start=True, stop=True)
                        mm.then_inc(pre["xt_done"], 1)

            with nc.Block() as block:
                @block.sync
                def _(sync):
                    clear(sync, pre)

                @block.tensor
                def _(pe):
                    for j in range(PAIRS):
                        nc.tensor.matmul(ps[0][:, pair(j)], aB[:, j, :], M[:, j, :], start=True, stop=False)
                        mm = nc.tensor.matmul(ps[0][:, pair(j)], AkT[:, j, :], vT[:, j, :], start=False, stop=True)
                    mm.then_inc(rec["right_done"], 1)
                    pe.wait_ge(rec["right_taken"], 1)
                    for j in range(PAIRS):
                        mm = nc.tensor.matmul(ps[1][:, pair(j)], XT[:, j, :], Rs[:, j, :], start=True, stop=True)
                    mm.then_inc(rec["u_done"], 1)
                    pe.wait_ge(rec["u_taken"], 1)
                    for j in range(PAIRS):
                        nc.tensor.matmul(ps[2][:, pair(j)], kT[:, j, :], vT[:, j, :], start=True, stop=False)
                        mm = nc.tensor.matmul(ps[2][:, pair(j)], bT[:, j, :], Un[:, j, :], start=False, stop=True)
                    mm.then_inc(rec["change_done"], 1)
                    for j in range(PAIRS):
                        o = slice(j * C, j * C + C)
                        nc.tensor.matmul(ps[3][:, o], M[:, j, :], rho[:, j, :], start=True, stop=False)
                        nc.tensor.matmul(ps[3][:, o], vT[:, j, :], ArT[:, 1, j, :], start=False, stop=False)
                        mm = nc.tensor.matmul(ps[3][:, o], Un[:, j, :], ArT[:, 0, j, :], start=False, stop=True)
                    mm.then_inc(rec["y_done"], 1)

                @block.scalar
                def _(act):
                    act.wait_ge(rec["right_done"], 1)
                    nc.scalar.copy(flat(Rs[:, :, :]), ps[0][:, :]).then_inc(rec["right_taken"], 1)
                    act.wait_ge(rec["u_done"], 1)
                    nc.scalar.mul(flat(Un[:, :, :]), ps[1][:, :], -1.0).then_inc(rec["u_taken"], 1)
                    act.wait_ge(rec["y_done"], 1)
                    nc.scalar.copy(R.y[:, :, ds(c * C, C)], ps[3][:, 0:PAIRS * C].rearrange(
                        "p (j t) -> p j t", j=PAIRS))

                @block.vector
                def _(dve):
                    dve.wait_ge(rec["y_done"], 1)
                    nc.vector.tensor_tensor(flat(M[:, :, :]), flat(M[:, :, :]), ps[2][:, :], ALU.add).then_inc(
                        rec["dve"], 1)
                    dve.wait_ge(rec["dve"], 1)
                    nc.vector.tensor_tensor(M[:, :, :], M[:, :, :], PC[:, :, :].to_broadcast([P, PAIRS, P]),
                                            ALU.mult)


RWKV_PRE_SEMS = ("blocks_act blocks_dve turned t1_done t1_taken lt_ready bt_ready dve products x_ready xt_done")
RWKV_REC_SEMS = "masks_loaded right_done right_taken u_done u_taken change_done y_done dve"


def rwkv_out_phase(nc, T, sems, stale, R, out):
    col = lambda name, j: T.lc[:, LCOLS[name][0] + j:LCOLS[name][0] + j + 1]
    with nc.sbuf_tensor([P, 2, S], F32) as sq, nc.sbuf_tensor([P, PAIRS, S], F32) as rstd, nc.Block() as block:
        @block.sync
        def _(sync):
            clear(sync, stale)

        @block.scalar
        def _(act):
            for j in range(PAIRS):
                act.wait_ge(sems["var_done"], j + 1)
                rsqrt(act, sems["rooted"], 2 * j, rstd[:, j, :], T.ps[4 + j][:, :], 1.0 / 64, T.eps(GN_EPS))

        @block.tensor
        def _(pe):
            for j in range(PAIRS):
                nc.tensor.matmul(T.ps[j][:, :], T.head_ones[:, :], R.y[:, j, :], start=True, stop=True).then_inc(
                    sems["mean_done"], 1)
            for j in range(PAIRS):
                pe.wait_ge(sems["squared"], j + 1)
                nc.tensor.matmul(T.ps[4 + j][:, :], T.head_ones[:, :], sq[:, j % 2, :], start=True,
                                 stop=True).then_inc(sems["var_done"], 1)

        @block.vector
        def _(dve):
            link = Chain(dve, sems["dve"])
            for j in range(PAIRS):
                y = R.y[:, j, :]
                dve.wait_ge(sems["mean_done"], j + 1)
                link(nc.vector.scalar_tensor_tensor(out=y, in0=T.ps[j][:, :], scalar=-1.0 / 64, in1=y,
                                                    op0=ALU.mult, op1=ALU.add))
                if j >= 2:
                    dve.wait_ge(sems["var_done"], j - 1)
                nc.vector.tensor_tensor(sq[:, j % 2, :], y, y, ALU.mult).then_inc(sems["squared"], 1)
            for j in range(PAIRS):
                y, rs = R.y[:, j, :], rstd[:, j, :]
                dve.wait_ge(sems["rooted"], 2 * j + 2)
                link(nc.vector.scalar_tensor_tensor(out=y, in0=y, scalar=col("lnx_g", j), in1=rs,
                                                    op0=ALU.mult, op1=ALU.mult))
                link(nc.vector.scalar_tensor_tensor(out=y, in0=y, scalar=col("lnx_b", j), in1=R.bonus[:, j, :],
                                                    op0=ALU.add, op1=ALU.add))
                nc.vector.tensor_tensor(out[:, j, :], y, R.gate[:, j, :], ALU.mult)


RWKV_OUT_SEMS = "mean_done squared var_done rooted dve"


RET_SEMS = ("loaded rotated rot_summed taken scored decayed summed squared sq_summed rooted done silu dve")


def retention_phase(nc, T, sems, stale, qk, vt, g, out):
    with nc.sbuf_tensor([P, RET_HEADS, S], F32) as decay, nc.sbuf_tensor([P, 2, S], F32) as cossin, \
            nc.sbuf_tensor([P, P], F32) as rot, nc.sbuf_tensor([P, 2, S], F32) as tmp, \
            nc.sbuf_tensor([P, 4, S], F32) as sc, nc.sbuf_tensor([P, S], F32) as rstd, nc.Block() as block:
        @block.sync
        def _(sync):
            clear(sync, stale)
            sync.dma_start(cossin[:, :, :], T.dram["ret_cossin"]).then_inc(sems["loaded"], 16)
            sync.dma_start(rot[:, :], T.dram["rot"]).then_inc(sems["loaded"], 16)
            sync.dma_start(decay[:, :, :], T.dram["ret_decay"]).then_inc(sems["loaded"], 16)

        @block.tensor
        def _(pe):
            pe.wait_ge(sems["loaded"], 48)
            for t in range(4):
                nc.tensor.matmul(T.ps[t][:, :], rot[:, :], qk[:, t, :], start=True, stop=True).then_inc(
                    sems["rot_summed"], 1)
            pe.wait_ge(sems["rotated"], 4)
            for h in range(RET_HEADS):
                q = slice(64 * (h % 2), 64 * (h % 2) + 64)
                for jc in range(4):
                    if h:
                        pe.wait_ge(sems["decayed"], 4 * (h - 1) + jc + 1)
                    nc.tensor.matmul(T.ps[jc][:, 0:S - jc * P], qk[q, 2 + h // 2, jc * P:jc * P + P],
                                     qk[q, h // 2, jc * P:S], start=True, stop=True).then_inc(sems["scored"], 1)
                for jc in range(4):
                    pe.wait_ge(sems["decayed"], 4 * h + jc + 1)
                    if h >= 2 and jc == 0:
                        pe.wait_ge(sems["done"], h - 1)
                    mm = nc.tensor.matmul(T.ps[4 + h % 2][:, jc * P:S], vt[:, jc, h * P:h * P + P],
                                          sc[:, jc, 0:S - jc * P], start=(jc == 0), stop=(jc == 3),
                                          skip_group_check=True)
                mm.then_inc(sems["summed"], 1)
                pe.wait_ge(sems["squared"], h + 1)
                nc.tensor.matmul(T.ps[6][:, :], T.ones[:, :], tmp[:, 1, :], start=True, stop=True).then_inc(
                    sems["sq_summed"], 1)

        @block.scalar
        def _(act):
            for h in range(RET_HEADS):
                nc.scalar.activation(g[:, h, :], g[:, h, :], ACT.Silu).then_inc(sems["silu"], 1)
            act.wait_ge(sems["rotated"], 4)
            for h in range(RET_HEADS):
                act.wait_ge(sems["summed"], h + 1)
                nc.scalar.activation(tmp[:, 1, :], T.ps[4 + h % 2][:, :], ACT.Square).then_inc(sems["squared"], 1)
                act.wait_ge(sems["sq_summed"], h + 1)
                if h:
                    act.wait_ge(sems["done"], h)
                rsqrt(act, sems["rooted"], 2 * h, rstd[:, :], T.ps[6][:, :], 1.0 / P, T.eps(EPS))

        @block.vector
        def _(dve):
            link = Chain(dve, sems["dve"])
            dve.wait_ge(sems["loaded"], 48)
            for t in range(4):
                dve.wait_ge(sems["rot_summed"], t + 1)
                if t:
                    dve.wait_ge(sems["rotated"], t)
                nc.vector.tensor_tensor(tmp[:, 0, :], T.ps[t][:, :], cossin[:, 1, :], ALU.mult)
                link(nc.vector.tensor_tensor(tmp[:, 1, :], qk[:, t, :], cossin[:, 0, :], ALU.mult))
                nc.vector.tensor_tensor(qk[:, t, :], tmp[:, 0, :], tmp[:, 1, :], ALU.add).then_inc(sems["rotated"], 1)
            dve.wait_ge(sems["silu"], 4)
            for h in range(RET_HEADS):
                if h:
                    dve.wait_ge(sems["summed"], h)
                for jc in range(4):
                    dve.wait_ge(sems["scored"], 4 * h + jc + 1)
                    n = S - jc * P
                    nc.vector.tensor_tensor(sc[:, jc, 0:n], T.ps[jc][:, 0:n], decay[:, h, 0:n], ALU.mult).then_inc(
                        sems["decayed"], 1)
                dve.wait_ge(sems["rooted"], 2 * h + 2)
                if h:
                    dve.wait_ge(sems["done"], h)
                link(nc.vector.tensor_tensor(tmp[:, 0, :], T.ps[4 + h % 2][:, :], rstd[:, :], ALU.mult))
                nc.vector.tensor_tensor(out[:, h, :], tmp[:, 0, :], g[:, h, :], ALU.mult).then_inc(sems["done"], 1)


SGU_SEMS = "loaded gelu_v gelu_u normed rooted stats mixed w_masked dve"


def sgu_phase(nc, T, sems, stale, u, vt, layer, out):
    with nc.sbuf_tensor([P, S], F32) as wsT, nc.sbuf_tensor([P, S], F32) as causal, nc.sbuf_tensor([P, 3, S], F32) as rows, \
            nc.sbuf_tensor([P, 4, 6], F32) as stats, nc.sbuf_tensor([P, 4, 2], F32) as mv, \
            nc.sbuf_tensor([P, 4], F32) as rstd, nc.sbuf_tensor([P, 2, S], F32) as tmp, nc.Block() as block:
        @block.sync
        def _(sync):
            clear(sync, stale)
            sync.dma_start(wsT[:, :], T.dram["sg_wT"][ds(layer, 1)].rearrange("l p c -> p (l c)")).then_inc(
                sems["loaded"], 16)
            sync.dma_start(causal[:, :], T.dram["causal"]).then_inc(sems["loaded"], 16)
            sync.dma_start(rows[:, :, :].rearrange("p a b -> p (a b)"),
                           T.dram["sg_rows"][ds(layer, 1), :].to_broadcast([P, 3 * S])).then_inc(sems["loaded"], 16)

        @block.scalar
        def _(act):
            for m in range(4):
                nc.scalar.activation(vt[:, m, :], vt[:, m, :], ACT.Gelu).then_inc(sems["gelu_v"], 1)
            for t in range(4):
                nc.scalar.activation(u[:, t, :], u[:, t, :], ACT.Gelu).then_inc(sems["gelu_u"], 1)
            act.wait_ge(sems["stats"], 4)
            rsqrt(act, sems["rooted"], 0, rstd[:, :], mv[:, :, 1:2].rearrange("p m a -> p (m a)"), 1.0, T.eps(EPS))

        @block.vector
        def _(dve):
            link = Chain(dve, sems["dve"])
            dve.wait_ge(sems["loaded"], 48)
            nc.vector.tensor_tensor(wsT[:, :], wsT[:, :], causal[:, :], ALU.mult).then_inc(sems["w_masked"], 1)
            for m in range(4):
                dve.wait_ge(sems["gelu_v"], m + 1)
                link(nc.vector.bn_stats(stats[:, m, :], vt[:, m, :]))
                nc.vector.bn_aggr(mv[:, m, :], stats[:, m, :]).then_inc(sems["stats"], 1)
            dve.wait_ge(sems["rooted"], 2)
            for m in range(4):
                v = vt[:, m, :]
                link(nc.vector.tensor_scalar(v, v, mv[:, m, 0:1], rstd[:, m:m + 1], ALU.subtract, ALU.mult))
                link(nc.vector.tensor_tensor(v, v, rows[:, 0, :], ALU.mult))
                nc.vector.tensor_tensor(v, v, rows[:, 1, :], ALU.add).then_inc(sems["normed"], 1)
            dve.wait_ge(sems["gelu_u"], 4)
            for g in range(SG_GROUPS):
                dve.wait_ge(sems["mixed"], g + 1)
                bias = rows[:, 2, g * P:g * P + P].unsqueeze(1).to_broadcast([P, 4, P])
                link(nc.vector.tensor_tensor(tmp[:, g % 2, :].rearrange("p (m i) -> p m i", m=4),
                                             T.ps[g][:, :].rearrange("p (m i) -> p m i", m=4), bias, ALU.add))
                link(nc.vector.tensor_tensor(out[:, g, :], tmp[:, g % 2, :], u[:, g, :], ALU.mult))

        @block.tensor
        def _(pe):
            pe.wait_ge(sems["w_masked"], 1)
            pe.wait_ge(sems["normed"], 4)
            for g in range(SG_GROUPS):
                for m in range(4):
                    mm = nc.tensor.matmul(T.ps[g][:, m * P:m * P + P], vt[:, m, g * P:g * P + P],
                                          wsT[:, g * P:g * P + P], start=True, stop=True)
                mm.then_inc(sems["mixed"], 1)


MERGE_SEMS = SPLIT_SEMS + " logits_done proj_done sig_done added zeroed dve"


def merge_phase(nc, T, sems, stale, weights, hT, branches, merged):
    with ExitStack() as ctx:
        sig = ctx.enter_context(nc.sbuf_tensor("merge_sig", [P, 4, S], F32))
        split = Split(nc, ctx, T, sems, KD)
        block = ctx.enter_context(nc.Block())

        @block.sync
        def _(sync):
            clear(sync, stale)
            with sync.Fori(0, 6) as i:
                for s in range(2):
                    sync.wait_ge(sems["added"], 4 * i + 2 * s + 2)
                    sync.dma_start(T.w[:, s, 0:12 * 256], weights(2 * i + s)).then_inc(sems["w_full"][s], 16)

        @block.gpsimd
        def _(pool):
            for i, s in two_slots(pool, 12):
                for t in range(2):
                    split.low(pool, 4 * i + 2 * s + t, split.raw(s, t * P, 256), t)

        @block.tensor
        def _(pe):
            pe.sem_inc(sems["logits_done"], 2)
            pe.wait_ge(sems["rhs_hi"], KD)
            for b in range(3):
                with pe.Fori(0, 2) as i:
                    for s in range(2):
                        for t in range(2):
                            n = 2 * s + t
                            tile = 4 * i + 8 * b + n
                            pe.wait_ge(sems["added"], tile + 1)
                            if t == 0:
                                pe.wait_ge(sems["w_full"][s], 16 * i + 32 * b + 16)
                            for k in range(4):
                                c = (KD + k) * 256 + t * P
                                mm = nc.tensor.matmul(T.ps[2 * n + 1][:, :], T.w[:, s, c:c + P],
                                                      branches[b][:, k, :], start=(k == 0), stop=(k == 3))
                            mm.then_inc(sems["proj_done"], 1)
                            split.products(pe, T.ps[2 * n][:, :], tile, tile + 1, t).then_inc(
                                sems["logits_done"], 1)

        @block.scalar
        def _(act):
            def high(i, s, t):
                act.wait_ge(sems["w_full"][s], 16 * i + 16)
                act.wait_ge(sems["logits_done"], 4 * i + 2 * s + t + 1)
                split.high(split.raw(s, t * P, 256), t)

            high(0, 0, 0)
            high(0, 0, 1)
            for (i, s), behind in with_next(act, 12):
                for t in range(2):
                    n = 2 * s + t
                    act.wait_ge(sems["logits_done"], 4 * i + n + 3)
                    act.wait_ge(sems["added"], 4 * i + n + 1)
                    nc.scalar.activation(sig[:, n, :], T.ps[2 * n][:, :], ACT.Sigmoid).then_inc(sems["sig_done"], 1)
                    if behind:
                        high(*behind, t)

        @block.vector
        def _(dve):
            link = Chain(dve, sems["dve"])
            split.rhs(dve, hT)
            for k in range(KD):
                ms = nc.vector.memset(merged[:, k, :], 0.0)
            ms.then_inc(sems["zeroed"], 1)
            dve.wait_ge(sems["zeroed"], 1)
            dve.sem_inc(sems["added"], 4)
            for b in range(3):
                with dve.Fori(0, 2) as i:
                    for n in range(4):
                        dve.wait_ge(sems["sig_done"], 4 * i + 8 * b + n + 1)
                        dve.wait_ge(sems["proj_done"], 4 * i + 8 * b + n + 1)
                        link(nc.vector.tensor_tensor(sig[:, n, :], sig[:, n, :], T.ps[2 * n + 1][:, :], ALU.mult))
                        m = merged[:, ds(4 * i + n, 1), :].rearrange("p a t -> p (a t)")
                        nc.vector.tensor_tensor(m, m, sig[:, n, :], ALU.add).then_inc(sems["added"], 1)
                    link.restart()


FFN_UP_SEMS = SPLIT_SEMS + " loaded gate_done val_done gate_taken val_taken conv_done silu_done made dve"


def ffn_up_phase(nc, T, sems, stale, weights, layer, hT, made_hi, made_lo):
    done = (sems["gate_done"], sems["val_done"])
    with ExitStack() as ctx:
        cw = ctx.enter_context(nc.sbuf_tensor("up_taps", [P, FT, 8], F32))
        conv = ctx.enter_context(nc.sbuf_tensor("up_conv", [P, 4, S], F32))
        split = Split(nc, ctx, T, sems, KD)
        block = ctx.enter_context(nc.Block())

        @block.sync
        def _(sync):
            clear(sync, stale)
            sync.dma_start(cw[:, :, :], T.dram["ffn_conv"][ds(layer, 1)].rearrange(
                "l p j c -> p (l j) c")).then_inc(sems["loaded"], 16)
            for i, s in two_slots(sync, FT):
                sync.wait_ge(sems["w_lo"], 4 * i + 2 * s + 2)
                sync.dma_start(T.w[:, s, 0:KD * 256], weights(2 * i + s)).then_inc(sems["w_full"][s], 16)

        @block.gpsimd
        def _(pool):
            pool.sem_inc(sems["w_lo"], 4)
            for i, s in two_slots(pool, FT):
                for t in range(2):
                    split.low(pool, 4 * i + 2 * s + t, split.raw(s, t * P, 256), t)

        @block.tensor
        def _(pe):
            pe.sem_inc(done[0], 1)
            pe.sem_inc(done[1], 1)
            pe.wait_ge(sems["rhs_hi"], KD)
            for i, s in two_slots(pe, FT):
                pe.wait_ge(sems["made"], 2 * i + s + 1)
                for t in range(2):
                    n = 4 * i + 2 * s + t
                    split.products(pe, T.ps[2 * s + t][:, :], n, n + 5, t).then_inc(done[t], 1)

        @block.scalar
        def _(act):
            def high(i, s, t):
                act.wait_ge(sems["w_full"][s], 16 * i + 16)
                act.wait_ge(done[t], 2 * i + s + 1)
                split.high(split.raw(s, t * P, 256), t)

            act.wait_ge(sems["loaded"], 16)
            high(0, 0, 0)
            high(0, 0, 1)
            for (i, s), behind in with_next(act, FT):
                j = 2 * i + s
                act.wait_ge(sems["made"], j + 1)
                for t in range(2):
                    if behind:
                        high(*behind, t)
                    act.wait_ge(done[t], j + 2)
                    w2 = cw[:, ds(j, 1), 4 * t + 2:4 * t + 3].rearrange("p a b -> p (a b)")
                    b = cw[:, ds(j, 1), 4 * t + 3:4 * t + 4].rearrange("p a b -> p (a b)")
                    nc.scalar.activation(conv[:, 2 * s + t, :], T.ps[2 * s + t][:, :], ACT.Identity, bias=b,
                                         scale=w2).then_inc((sems["gate_taken"], sems["val_taken"])[t], 1)
                act.wait_ge(sems["conv_done"], j + 1)
                nc.scalar.activation(conv[:, 2 * s, :], conv[:, 2 * s, :], ACT.Silu).then_inc(sems["silu_done"], 1)

        @block.vector
        def _(dve):
            link = Chain(dve, sems["dve"])
            dve.sem_inc(sems["made"], 2)
            split.rhs(dve, hT)
            dve.wait_ge(sems["loaded"], 16)
            for i, s in two_slots(dve, FT):
                j = 2 * i + s
                for t in range(2):
                    c, u = conv[:, 2 * s + t, :], T.ps[2 * s + t]
                    tap = lambda q: cw[:, ds(j, 1), 4 * t + q:4 * t + q + 1].rearrange("p a b -> p (a b)")
                    dve.wait_ge((sems["gate_taken"], sems["val_taken"])[t], j + 1)
                    link(nc.vector.scalar_tensor_tensor(out=c[:, 1:S], in0=u[:, 0:S - 1], scalar=tap(1),
                                                        in1=c[:, 1:S], op0=ALU.mult, op1=ALU.add))
                    st = nc.vector.scalar_tensor_tensor(out=c[:, 2:S], in0=u[:, 0:S - 2], scalar=tap(0),
                                                        in1=c[:, 2:S], op0=ALU.mult, op1=ALU.add)
                    if t == 0:
                        st.then_inc(sems["conv_done"], 1)
                    else:
                        link(st)
                dve.wait_ge(sems["silu_done"], j + 1)
                product = conv[:, 2 * s, :]
                hi, lo = (m[:, ds(j, 1), :].rearrange("p a t -> p (a t)") for m in (made_hi, made_lo))
                link(nc.vector.tensor_tensor(product, product, conv[:, 2 * s + 1, :], ALU.mult))
                link(nc.vector.tensor_copy(hi, product))
                nc.vector.tensor_tensor(lo, product, hi.bitcast(F32), ALU.subtract).then_inc(sems["made"], 1)
                if s == 1:
                    link.restart()


DOWN_SEMS = SPLIT_SEMS + " tile_done added"


def down_phase(nc, T, sems, stale, weights, kt, rhs, xT, parts=None):
    with ExitStack() as ctx:
        split = Split(nc, ctx, T, sems, kt, *(parts or ()))
        block = ctx.enter_context(nc.Block())

        @block.sync
        def _(sync):
            clear(sync, stale)
            for i, s in two_slots(sync, KD):
                sync.wait_ge(sems["w_lo"], 2 * i + s + 1)
                sync.dma_start(T.w[:, s, 0:kt * P], weights(2 * i + s)).then_inc(sems["w_full"][s], 16)

        @block.scalar
        def _(act):
            for i, s in two_slots(act, KD):
                act.wait_ge(sems["w_full"][s], 16 * i + 16)
                act.wait_ge(sems["tile_done"], 2 * i + s + 1)
                split.high(split.raw(s, 0, P), s)

        @block.gpsimd
        def _(pool):
            pool.sem_inc(sems["w_lo"], 2)
            for i, s in two_slots(pool, KD):
                split.low(pool, 2 * i + s, split.raw(s, 0, P), s)

        @block.tensor
        def _(pe):
            pe.sem_inc(sems["tile_done"], 2)
            if parts is None:
                pe.wait_ge(sems["rhs_hi"], kt)
            for i, s in two_slots(pe, KD):
                pe.wait_ge(sems["added"], 2 * i + s + 1)
                split.products(pe, T.ps[s][:, :], 2 * i + s, 2 * i + s + 3, s).then_inc(sems["tile_done"], 1)

        @block.vector
        def _(dve):
            dve.sem_inc(sems["added"], 2)
            if parts is None:
                split.rhs(dve, rhs)
            for i, s in two_slots(dve, KD):
                dve.wait_ge(sems["tile_done"], 2 * i + s + 3)
                x = xT[:, ds(2 * i + s, 1), :].rearrange("p a t -> p (a t)")
                nc.vector.tensor_tensor(x, x, T.ps[s][:, :], ALU.add).then_inc(sems["added"], 1)


def put(dst):
    def write(eng, c, t, psum):
        return copied(eng, dst[:, ds(2 * c + t, 1), :].rearrange("p a t -> p (a t)"), psum)
    return write


def put_tokens(dst):
    def write(eng, c, m, psum):
        return copied(eng, dst[:, m, ds(256 * c, 256)], psum)
    return write


def pick(dram, *index):
    ap = dram
    names = "abcdef"[:len(index)]
    ap = ap[tuple(ds(i, 1) for i in index)]
    return ap.rearrange(f"{' '.join(names)} p c -> p ({' '.join(names)} c)")


def shared(nc, ctx, dram):
    def sb(name, *shape):
        return ctx.enter_context(nc.sbuf_tensor(name, [P, *shape], F32))

    T = Named()
    T.dram = dram
    T.xT, T.hT = sb("xT", KD, S), sb("hT", KD, S)
    T.w = sb("w", 2, 12 * 256)
    T.ident4, T.head_ones, T.ones = sb("ident4", 4 * P), sb("head_ones", P), sb("ones", P)
    T.lc, T.scalars = sb("layer_cols", NLCOL), sb("scalars", 4)
    T.ident = T.ident4[:, 0:P]
    T.eps = lambda e: T.scalars[:, (EPS, GN_EPS, LN_EPS).index(e):][:, 0:1]
    T.half_17ln2 = T.scalars[:, 3:4]
    T.ps = [ctx.enter_context(nc.psum_tensor(f"bank{i}", [P, 512], F32)) for i in range(8)]
    return T


def pick4(dram, i):
    return dram[ds(i, 1)].rearrange("l p a c -> p (l a) c")


def shared_sems(nc, ctx):
    return {name: sem_set(nc, ctx, name, names) for name, names in (
        ("start", "loaded"), ("stored", "done"), ("head", "loaded"), ("norm", NORM_SEMS), ("norm2", NORM_SEMS), ("pa", PROJECT_SEMS),
        ("pb", PROJECT_SEMS), ("down", DOWN_SEMS))}


def block_one(nc, T):
    with ExitStack() as ctx:
        layers(nc, ctx, T)


def layers(nc, ctx, T):
    ss = lambda prefix, names: sem_set(nc, ctx, prefix, names)
    head, norm, pa, pb, down = (T.sems[n] for n in ("head", "norm", "pa", "pb", "down"))
    prep, pre, rec, rout = (ss("prep", RWKV_PREP_SEMS), ss("pre", RWKV_PRE_SEMS), ss("rec", RWKV_REC_SEMS),
                            ss("rout", RWKV_OUT_SEMS))
    ret, sgu, merge, up = (ss("ret", RET_SEMS), ss("sgu", SGU_SEMS), ss("merge", MERGE_SEMS),
                           ss("up", FFN_UP_SEMS))
    rec["stale"] = prep
    d = T.dram
    xT = T.xT

    with nc.Fori(0, DEPTH) as layer:
        with nc.Block() as block:
            @block.sync
            def _(sync):
                clear(sync, T.sems["start"])
                clear(sync, down)
                sync.dma_start(T.lc[:, :], pick(d["layer_cols"], layer)).then_inc(head["loaded"], 16)
                sync.wait_ge(head["loaded"], 16)
        hT = T.hT
        gain = lambda name: T.lc[:, LCOLS[name][0]:LCOLS[name][1]]
        w_in = lambda first: (lambda c: pick(d["w_in"], layer, c + first))
        norm_phase(nc, T, norm, head, xT, gain("norm1_g"), hT)
        with ExitStack() as branch:
            def keep_branch(name, *shape):
                return branch.enter_context(nc.sbuf_tensor(name, [P, *shape], F32))

            y_rw = keep_branch("y_rw", 4, S)
            with ExitStack() as rw:
                R = Named()
                R.up = lambda: pick4(d["rw_up"], layer)
                R.beta, R.kappa, R.alpha, R.rho, R.run, R.gate, R.bonus = (
                    rw.enter_context(nc.sbuf_tensor("rw_" + n, [P, PAIRS, S], F32))
                    for n in ("beta", "kappa", "alpha", "rho", "run", "gate", "bonus"))
                R.p = rw.enter_context(nc.sbuf_tensor("rw_p", [P, RW_T, S], F32))
                R.y = y_rw
                project_phase(nc, T, pa, norm, w_in(0), 7, hT, put(R.p))
                rwkv_prep_phase(nc, T, prep, pa, R)
                rwkv_chunk_phases(nc, T, pre, rec, R)
                rwkv_out_phase(nc, T, rout, rec, R, y_rw)
            y_ret, y_sg = keep_branch("y_ret", 4, S), keep_branch("y_sg", 4, S)
            with nc.sbuf_tensor([P, 4, S], F32) as qk, nc.sbuf_tensor([P, 4, S], F32) as vt, \
                    nc.sbuf_tensor([P, 4, S], F32) as g:
                project_phase(nc, T, pa, rout, w_in(7), 2, hT, put(qk))
                token_project_phase(nc, T, pb, pa, w_in(9), 2, hT, put_tokens(vt))
                project_phase(nc, T, pa, pb, w_in(11), 2, hT, put(g))
                retention_phase(nc, T, ret, pa, qk, vt, g, y_ret)
            with nc.sbuf_tensor([P, 4, S], F32) as u, nc.sbuf_tensor([P, 4, S], F32) as vt:
                project_phase(nc, T, pa, ret, w_in(13), 2, hT, put(u))
                token_project_phase(nc, T, pb, pa, w_in(15), 2, hT, put_tokens(vt))
                sgu_phase(nc, T, sgu, pb, u, vt, layer, y_sg)
            with nc.sbuf_tensor([P, KD, S], F32) as merged:
                merge_phase(nc, T, merge, sgu, lambda c: pick(d["w_merge"], layer, c), hT, (y_rw, y_ret, y_sg),
                            merged)
                down_phase(nc, T, down, merge, lambda c: pick(d["w_out"], layer, c), KD, merged, xT)
        norm_phase(nc, T, norm, down, xT, gain("norm2_g"), hT)
        with nc.sbuf_tensor([P, FT, S], F32R) as made_hi, nc.sbuf_tensor([P, FT, S], F32R) as made_lo:
            ffn_up_phase(nc, T, up, norm, lambda c: pick(d["ffn_up"], layer, c), layer, hT, made_hi, made_lo)
            down_phase(nc, T, down, up, lambda c: pick(d["ffn_down"], layer, c), FT, None, xT,
                       parts=(made_hi, made_lo))


CONV_SEMS = "loaded sig sums_done squared sq_done rooted half dve silu"


def conv_phase(nc, T, sems, stale, ag, out):
    half = CONV_KERNEL // 2
    with nc.sbuf_tensor([P, 2, S + 2 * half], F32) as padded, nc.sbuf_tensor([P, 2, S], F32) as acc, \
            nc.sbuf_tensor([P, 2, CONV_KERNEL + 3], F32) as par, nc.sbuf_tensor([P, 2, S], F32) as sq, \
            nc.sbuf_tensor([P, S], F32) as rstd, nc.Block() as block:
        @block.sync
        def _(sync):
            clear(sync, stale)
            sync.dma_start(par[:, :, :], T.dram["conv_par"]).then_inc(sems["loaded"], 16)

        @block.scalar
        def _(act):
            for t in range(2):
                nc.scalar.activation(ag[:, 2 + t, :], ag[:, 2 + t, :], ACT.Sigmoid).then_inc(sems["sig"], 1)
            act.wait_ge(sems["sq_done"], 1)
            rsqrt(act, sems["rooted"], 0, rstd[:, :], T.ps[1][:, :], 1.0 / CONV_CH, T.eps(LN_EPS))
            for t in range(2):
                act.wait_ge(sems["half"], 3 + t)
                nc.scalar.activation(out[:, t, :], acc[:, t, :], ACT.Silu)

        @block.vector
        def _(dve):
            link = Chain(dve, sems["dve"])
            link(nc.vector.memset(padded[:, :, :], 0.0))
            dve.wait_ge(sems["loaded"], 16)
            dve.wait_ge(sems["sig"], 2)
            for t in range(2):
                link(nc.vector.tensor_tensor(padded[:, t, half:half + S], ag[:, t, :], ag[:, 2 + t, :], ALU.mult))
            for t in range(2):
                nc.vector.tensor_scalar(acc[:, t, :], padded[:, t, 0:S], par[:, t, 0:1],
                                        par[:, t, CONV_KERNEL:CONV_KERNEL + 1], ALU.mult, ALU.add).then_inc(
                    sems["dve"], 1)
            for j in range(1, CONV_KERNEL):
                for t in range(2):
                    dve.wait_ge(sems["dve"], link.n + 1)
                    nc.vector.scalar_tensor_tensor(out=acc[:, t, :], in0=padded[:, t, j:j + S],
                                                   scalar=par[:, t, j:j + 1], in1=acc[:, t, :], op0=ALU.mult,
                                                   op1=ALU.add).then_inc(sems["dve"], 1)
                    link.n += 1
            dve.wait_ge(sems["dve"], link.n + 2)
            link.n += 2
            dve.sem_inc(sems["half"], 1)
            dve.wait_ge(sems["sums_done"], 1)
            for t in range(2):
                link(nc.vector.scalar_tensor_tensor(out=acc[:, t, :], in0=T.ps[0][:, :], scalar=-1.0 / CONV_CH,
                                                    in1=acc[:, t, :], op0=ALU.mult, op1=ALU.add))
                nc.vector.tensor_tensor(sq[:, t, :], acc[:, t, :], acc[:, t, :], ALU.mult).then_inc(sems["squared"], 1)
            dve.wait_ge(sems["rooted"], 2)
            dve.sem_inc(sems["half"], 1)
            for t in range(2):
                link(nc.vector.scalar_tensor_tensor(out=acc[:, t, :], in0=acc[:, t, :],
                                                    scalar=par[:, t, CONV_KERNEL + 1:CONV_KERNEL + 2],
                                                    in1=rstd[:, :], op0=ALU.mult, op1=ALU.mult))
                nc.vector.tensor_scalar(acc[:, t, :], acc[:, t, :], par[:, t, CONV_KERNEL + 2:CONV_KERNEL + 3],
                                        None, ALU.add).then_inc(sems["half"], 1)

        @block.tensor
        def _(pe):
            pe.wait_ge(sems["half"], 1)
            for t in range(2):
                mm = nc.tensor.matmul(T.ps[0][:, :], T.ones[:, :], acc[:, t, :], start=(t == 0), stop=(t == 1))
            mm.then_inc(sems["sums_done"], 1)
            for t in range(2):
                pe.wait_ge(sems["squared"], t + 1)
                mm = nc.tensor.matmul(T.ps[1][:, :], T.ones[:, :], sq[:, t, :], start=(t == 0), stop=(t == 1))
            mm.then_inc(sems["sq_done"], 1)


ROPE_SEMS = "loaded dve reduced tables turned half_done pool done"


def rope_phase(nc, T, sems, stale, qk, tiles):
    with nc.sbuf_tensor([P, S], mybir.dt.int32) as pos_i, nc.sbuf_tensor([P, 1], F32) as inv, \
            nc.sbuf_tensor([P, S], F32) as ang, nc.sbuf_tensor([P, S], F32) as turns, \
            nc.sbuf_tensor([P, 2, S], F32) as table, nc.sbuf_tensor([P, P], F32) as rot, \
            nc.sbuf_tensor([P, 4, S], F32) as tmp, nc.Block() as block:
        @block.sync
        def _(sync):
            clear(sync, stale)
            sync.dma_start(pos_i[:, :], T.dram["positions"].to_broadcast([P, S])).then_inc(sems["loaded"], 16)
            sync.dma_start(inv[:, :], T.dram["rope_inv"]).then_inc(sems["loaded"], 16)
            sync.dma_start(rot[:, :], T.dram["rot"]).then_inc(sems["loaded"], 16)

        @block.vector
        def _(dve):
            link = Chain(dve, sems["dve"])
            dve.wait_ge(sems["loaded"], 48)
            link(nc.vector.tensor_copy(ang[:, :], pos_i[:, :]))
            link(nc.vector.tensor_scalar(ang[:, :], ang[:, :], inv[:, 0:1], None, ALU.mult))
            for n, shift in enumerate((np.pi / 2, 0.0)):
                r = table[:, n, :]
                link(nc.vector.tensor_scalar(turns[:, :], ang[:, :], float(shift), float(1 / (2 * np.pi)), ALU.add,
                                             ALU.mult))
                link(nc.vector.tensor_scalar(turns[:, :], turns[:, :], 12582912.0, None, ALU.add))
                link(nc.vector.tensor_scalar(turns[:, :], turns[:, :], -12582912.0, None, ALU.add))
                link(nc.vector.scalar_tensor_tensor(out=r, in0=turns[:, :], scalar=-TWO_PI[0], in1=ang[:, :],
                                                    op0=ALU.mult, op1=ALU.add))
                for part in TWO_PI[1:]:
                    link(nc.vector.scalar_tensor_tensor(out=r, in0=turns[:, :], scalar=-part, in1=r,
                                                        op0=ALU.mult, op1=ALU.add))
                link(nc.vector.tensor_scalar(r, r, float(shift), None, ALU.add))
                link(nc.vector.tensor_scalar(r, r, 3.1415925, -3.1415925, ALU.min, ALU.max))
            dve.sem_inc(sems["reduced"], 1)
            dve.wait_ge(sems["tables"], 2)
            with dve.Fori(0, tiles // 4) as i:
                for b in range(4):
                    dve.wait_ge(sems["turned"], 4 * i + b + 1)
                    nc.vector.tensor_tensor(tmp[:, b, :], T.ps[b][:, :], table[:, 1, :], ALU.mult).then_inc(
                        sems["half_done"], 1)
                for b in range(4):
                    x = qk[:, ds(4 * i + b, 1), :].rearrange("p a t -> p (a t)")
                    dve.wait_ge(sems["half_done"], 4 * i + b + 1)
                    dve.wait_ge(sems["pool"], 4 * i + b + 1)
                    nc.vector.tensor_tensor(x, x, tmp[:, b, :], ALU.add).then_inc(sems["done"], 1)
                dve.wait_ge(sems["done"], 4 * i + 4)

        @block.gpsimd
        def _(pool):
            pool.wait_ge(sems["tables"], 2)
            with pool.Fori(0, tiles // 4) as i:
                for b in range(4):
                    x = qk[:, ds(4 * i + b, 1), :].rearrange("p a t -> p (a t)")
                    pool.wait_ge(sems["turned"], 4 * i + b + 1)
                    nc.gpsimd.tensor_tensor(x, x, table[:, 0, :], ALU.mult).then_inc(sems["pool"], 1)

        @block.scalar
        def _(act):
            act.wait_ge(sems["reduced"], 1)
            for n in range(2):
                nc.scalar.activation(table[:, n, :], table[:, n, :], ACT.Sin).then_inc(sems["tables"], 1)

        @block.tensor
        def _(pe):
            pe.wait_ge(sems["loaded"], 48)
            with pe.Fori(0, tiles // 4) as i:
                for b in range(4):
                    x = qk[:, ds(4 * i + b, 1), :].rearrange("p a t -> p (a t)")
                    nc.tensor.matmul(T.ps[b][:, :], rot[:, :], x, start=True, stop=True).then_inc(sems["turned"], 1)
                pe.wait_ge(sems["half_done"], 4 * i + 4)


ATT_SEMS = ("loaded staged scored scaled maxed exped normed dve turned act_took dve_took summed put")


def attention_phase(nc, T, sems, stale, q, k, k_first, v, out, groups, q_tiles, keys, scale, mask=None):
    kt = keys // P
    vc = q_tiles * P
    wide = q_tiles > 1
    with nc.sbuf_tensor([P, q_tiles, S], F32) as qs, nc.sbuf_tensor([P, kt, vc], F32) as vs, \
            nc.sbuf_tensor([P, q_tiles, keys], F32) as ks, \
            nc.sbuf_tensor([P, 2, 4, keys], F32) as sc, nc.sbuf_tensor([P, kt, S], F32) as pT, \
            nc.sbuf_tensor([P, 2, 3, 4], F32) as st, nc.Block() as block:
        @block.sync
        def _(sync):
            clear(sync, stale)

        @block.gpsimd
        def _(pool):
            with pool.Fori(0, groups) as g:
                pool.wait_ge(sems["put"], 2 * g + 1)
                nc.gpsimd.tensor_copy(qs[:, :, :], q[:, ds(q_tiles * g, q_tiles), :]).then_inc(sems["staged"], 1)
                nc.gpsimd.tensor_copy(ks[:, :, :], k[:, ds(q_tiles * g + k_first, q_tiles), :]).then_inc(
                    sems["staged"], 1)
                nc.gpsimd.tensor_copy(vs[:, :, :], v[:, :, ds(vc * g, vc)]).then_inc(sems["staged"], 1)

        def rows(u):
            return slice(0, P) if wide else slice(64 * u, 64 * u + 64)

        @block.tensor
        def _(pe):
            with pe.Fori(0, groups) as g:
                pe.wait_ge(sems["staged"], 3 * g + 3)
                for u in range(2):
                    for m in range(4):
                        pe.wait_ge(sems["scaled"], 8 * g + 4 * u + m + 1)
                        tiles = (2 * u, 2 * u + 1) if wide else (0,)
                        for n in tiles:
                            mm = nc.tensor.matmul(T.ps[m % 2][:, 0:keys], qs[rows(u), n, m * P:m * P + P],
                                                  ks[rows(u), n, :], start=(n == tiles[0]), stop=(n == tiles[-1]))
                        mm.then_inc(sems["scored"], 1)
                for u in range(2):
                    pe.wait_ge(sems["normed"], 2 * g + u + 1)
                    pe.wait_ge(sems["act_took"], 2 * g + u + 1)
                    pe.wait_ge(sems["dve_took"], 2 * g + u + 1)
                    for j in range(kt):
                        for m in range(4):
                            mm = nc.tensor.transpose(T.ps[2 + j][:, m * P:m * P + P], sc[:, u, m, j * P:j * P + P],
                                                     T.ident[:, :])
                    mm.then_inc(sems["turned"], 1)
                    pe.wait_ge(sems["act_took"], 2 * g + u + 2)
                    pe.wait_ge(sems["dve_took"], 2 * g + u + 2)
                    pe.wait_ge(sems["put"], 2 * g + u + 1)
                    for e in range(2 if wide else 1):
                        o = T.ps[6 + e][:, :] if wide else T.ps[6 + u][rows(u), :]
                        c = (2 * u + e) * P if wide else 64 * u
                        n = P if wide else 64
                        for j in range(kt):
                            mm = nc.tensor.matmul(o, vs[:, j, c:c + n], pT[:, j, :], start=(j == 0),
                                                  stop=(j == kt - 1))
                    mm.then_inc(sems["summed"], 1)

        @block.vector
        def _(dve):
            link = Chain(dve, sems["dve"])
            dve.sem_inc(sems["scaled"], 2)
            dve.sem_inc(sems["dve_took"], 1)
            with dve.Fori(0, groups) as g:
                for u in range(2):
                    for m in range(4):
                        dve.wait_ge(sems["scored"], 8 * g + 4 * u + m + 1)
                        s = sc[:, u, m, :]
                        if mask is None:
                            ins = nc.vector.tensor_scalar(s, T.ps[m % 2][:, 0:keys], scale, None, ALU.mult)
                        else:
                            ins = nc.vector.scalar_tensor_tensor(out=s, in0=T.ps[m % 2][:, 0:keys], scalar=scale,
                                                                 in1=mask[:, m, :], op0=ALU.mult, op1=ALU.add)
                        ins.then_inc(sems["scaled"], 1)
                        dve.wait_ge(sems["scaled"], 8 * g + 4 * u + m + 3)
                        link(nc.vector.reduce_max(st[:, u, 0, m:m + 1], s, AX.X))
                    nc.vector.tensor_scalar(st[:, u, 0, :], st[:, u, 0, :], -1.0, None, ALU.mult).then_inc(
                        sems["maxed"], 1)
                for u in range(2):
                    dve.wait_ge(sems["exped"], 8 * g + 4 * u + 4)
                    link(nc.vector.reciprocal(st[:, u, 2, :], st[:, u, 1, :]))
                    for m in range(4):
                        s = sc[:, u, m, :]
                        ins = nc.vector.tensor_scalar(s, s, st[:, u, 2, m:m + 1], None, ALU.mult)
                        if m < 3:
                            link(ins)
                    ins.then_inc(sems["normed"], 1)
                    dve.wait_ge(sems["turned"], 2 * g + u + 1)
                    for j in range(1, kt, 2):
                        ins = nc.vector.tensor_copy(pT[:, j, :], T.ps[2 + j][:, :])
                        if j < kt - 1:
                            link(ins)
                    ins.then_inc(sems["dve_took"], 1)
                link.restart()

        @block.scalar
        def _(act):
            act.sem_inc(sems["act_took"], 1)
            act.sem_inc(sems["put"], 1)
            with act.Fori(0, groups) as g:
                for u in range(2):
                    act.wait_ge(sems["maxed"], 2 * g + u + 1)
                    for m in range(4):
                        s = sc[:, u, m, :]
                        nc.scalar.activation(s, s, ACT.Exp, bias=st[:, u, 0, m:m + 1],
                                             accum_out=st[:, u, 1, m:m + 1]).then_inc(sems["exped"], 1)
                for u in range(2):
                    act.wait_ge(sems["turned"], 2 * g + u + 1)
                    act.wait_ge(sems["put"], 2 * g + u + 1)
                    for j in range(0, kt, 2):
                        ins = nc.scalar.copy(pT[:, j, :], T.ps[2 + j][:, :])
                        if j < kt - 2:
                            ins.then_inc(sems["loaded"], 1)
                    if kt > 2:
                        act.wait_ge(sems["loaded"], 2 * g + u + 1)
                    ins.then_inc(sems["act_took"], 1)
                    act.wait_ge(sems["summed"], 2 * g + u + 1)
                    if wide:
                        for e in range(2):
                            o = out[:, ds(4 * g + 2 * u + e, 1), :].rearrange("p a t -> p (a t)")
                            ins = nc.scalar.copy(o, T.ps[6 + e][:, :])
                            if e == 0:
                                ins.then_inc(sems["loaded"], 1)
                                act.wait_ge(sems["loaded"], 2 * g + u + 1)
                    else:
                        o = out[rows(u), ds(g, 1), :].rearrange("p a t -> p (a t)")
                        ins = nc.scalar.copy(o, T.ps[6 + u][rows(u), :])
                    ins.then_inc(sems["put"], 1)


ROUTE_SEMS = "loaded turned act_took dve_took logits dve exp_in exped ranks counted ready"


def route_phase(nc, T, sems, stale, hT, M):
    E, G = N_EXPERTS, N_GROUPS
    W = G + E
    with ExitStack() as ctx:
        def sb(name, *shape):
            return ctx.enter_context(nc.sbuf_tensor(f"route_{name}", [P, *shape], F32))

        wr, bias, lg, iota = sb("w", KD, W), sb("bias", W), sb("logits", 4, W), sb("iota", E)
        before = sb("before", P)
        ge, gt, goh, pg = sb("gexp", 4, G), sb("gtie", 4, G), sb("ghot", 4, G), sb("pg", 4, 1)
        em, tie, oh1, oh2 = sb("em", 4, E), sb("tie", 4, E), sb("hot1", 4, E), sb("hot2", 4, E)
        m0, m1, m2, t1, t2, g1, g2 = (sb(n, 4, 1) for n in "m0 m1 m2 t1 t2 g1 g2".split())
        chosen, pm, many = sb("chosen", 4, E), sb("pairmax", E // 2), sb("many", MOE_ROUNDS - 1, E // 2)
        block = ctx.enter_context(nc.Block())

        @block.sync
        def _(sync):
            clear(sync, stale)
            sync.dma_start(wr[:, :, :], T.dram["router_w"]).then_inc(sems["loaded"], 16)
            sync.dma_start(bias[:, :], T.dram["router_b"].to_broadcast([P, W])).then_inc(sems["loaded"], 16)
            sync.dma_start(iota[:, :], T.dram["iota"][:, 0:E]).then_inc(sems["loaded"], 16)
            sync.dma_start(before[:, :], T.dram["before"]).then_inc(sems["loaded"], 16)
            sync.dma_start(M.slots[:, :], T.dram["iota"]).then_inc(sems["loaded"], 16)

        @block.tensor
        def _(pe):
            pe.wait_ge(sems["loaded"], 80)
            for m in range(4):
                for k in range(KD):
                    mm = nc.tensor.matmul(T.ps[7][:, m * W:m * W + W], hT[:, k, m * P:m * P + P], wr[:, k, :],
                                          start=(k == 0), stop=(k == KD - 1))
            mm.then_inc(sems["logits"], 1)
            for m in range(4):
                for half in range(2):
                    if m >= 2:
                        pe.wait_ge((sems["act_took"], sems["dve_took"])[half], m - 1)
                    for k in range(4):
                        mm = nc.tensor.transpose(T.ps[2 * (m % 2) + half][:, k * P:k * P + P],
                                                 hT[:, 4 * half + k, m * P:m * P + P], T.ident[:, :])
                    mm.then_inc(sems["turned"], 1)
            pe.wait_ge(sems["ready"], 1)
            for m in range(4):
                for n in range(m + 1):
                    mm = nc.tensor.matmul(T.ps[5][:, m * E:m * E + E], (before if n == m else T.ones)[:, :],
                                          chosen[:, n, :], start=(n == 0), stop=(n == m))
            mm.then_inc(sems["ranks"], 1)
            for n in range(4):
                mm = nc.tensor.matmul(T.ps[6][:, 0:E], T.ones[:, :], chosen[:, n, :], start=(n == 0), stop=(n == 3))
            mm.then_inc(sems["counted"], 1)

        @block.scalar
        def _(act):
            act.wait_ge(sems["exp_in"], 1)
            nc.scalar.activation(ge[:, :, :], ge[:, :, :], ACT.Exp).then_inc(sems["exped"], 1)
            for m in range(4):
                act.wait_ge(sems["turned"], 2 * m + 1)
                nc.scalar.copy(M.h_tok[:, m, 0:512], T.ps[2 * (m % 2)][:, :]).then_inc(sems["act_took"], 1)
            act.wait_ge(sems["exp_in"], 2)
            nc.scalar.activation(t1[:, :, :], t1[:, :, :], ACT.Exp).then_inc(sems["exped"], 1)

        @block.vector
        def _(dve):
            link = Chain(dve, sems["dve"])
            v = nc.vector
            dve.wait_ge(sems["loaded"], 80)
            dve.wait_ge(sems["logits"], 1)
            link(v.tensor_tensor(lg[:, :, :], T.ps[7][:, 0:4 * W].rearrange("p (m w) -> p m w", m=4),
                                 bias[:, :].unsqueeze(1).to_broadcast([P, 4, W]), ALU.add))
            gl, el = lg[:, :, 0:G], lg[:, :, G:W]

            def first_max(x, width, best, tie_, hot):
                link(v.tensor_reduce(best[:, :, :], x, AX.X, ALU.max))
                link(v.tensor_tensor(tie_[:, :, :], x, best[:, :, :].to_broadcast([P, 4, width]), ALU.is_equal))
                link(v.tensor_scalar(tie_[:, :, :], tie_[:, :, :], -100.0, None, ALU.mult))
                link(v.tensor_tensor(tie_[:, :, :], tie_[:, :, :],
                                     iota[:, 0:width].unsqueeze(1).to_broadcast([P, 4, width]), ALU.add))
                link(v.tensor_reduce(t2[:, :, :], tie_[:, :, :], AX.X, ALU.min))
                link(v.tensor_tensor(hot[:, :, :], tie_[:, :, :], t2[:, :, :].to_broadcast([P, 4, width]),
                                     ALU.is_equal))

            first_max(gl, G, m0, gt, goh)
            v.tensor_tensor(ge[:, :, :], gl, m0[:, :, :].to_broadcast([P, 4, G]), ALU.subtract).then_inc(
                sems["exp_in"], 1)
            link(v.tensor_scalar(gt[:, :, :], goh[:, :, :], 1e30, -1e30, ALU.mult, ALU.add))
            for g in range(G):
                q = slice(8 * g, 8 * g + 8)
                link(v.tensor_tensor(em[:, :, q], el[:, :, q], gt[:, :, g:g + 1].to_broadcast([P, 4, 8]), ALU.add))
            first_max(em[:, :, :], E, m1, tie, oh1)
            link(v.tensor_scalar(tie[:, :, :], oh1[:, :, :], -2e30, None, ALU.mult))
            link(v.tensor_tensor(em[:, :, :], em[:, :, :], tie[:, :, :], ALU.add))
            first_max(em[:, :, :], E, m2, tie, oh2)
            v.tensor_tensor(t1[:, :, :], m2[:, :, :], m1[:, :, :], ALU.subtract).then_inc(sems["exp_in"], 1)
            v.tensor_tensor(chosen[:, :, :], oh1[:, :, :], oh2[:, :, :], ALU.add).then_inc(sems["ready"], 1)
            for m in range(4):
                dve.wait_ge(sems["turned"], 2 * m + 2)
                v.tensor_copy(M.h_tok[:, m, 512:1024], T.ps[2 * (m % 2) + 1][:, :]).then_inc(sems["dve_took"], 1)
            dve.wait_ge(sems["exped"], 2)
            link(v.tensor_reduce(pg[:, :, :], ge[:, :, :], AX.X, ALU.add))
            link(v.reciprocal(pg[:, :, :], pg[:, :, :]))
            link(v.tensor_scalar(g1[:, :, :], t1[:, :, :], 1.0, None, ALU.add))
            link(v.reciprocal(g1[:, :, :], g1[:, :, :]))
            link(v.tensor_tensor(g1[:, :, :], g1[:, :, :], pg[:, :, :], ALU.mult))
            link(v.tensor_tensor(g2[:, :, :], g1[:, :, :], t1[:, :, :], ALU.mult))
            link(v.tensor_tensor(oh1[:, :, :], oh1[:, :, :], g1[:, :, :].to_broadcast([P, 4, E]), ALU.mult))
            link(v.tensor_tensor(oh2[:, :, :], oh2[:, :, :], g2[:, :, :].to_broadcast([P, 4, E]), ALU.mult))
            link(v.memset(M.gates[:, :, E:], 0.0))
            link(v.memset(M.place[:, :, E:], BIG))
            link(v.tensor_tensor(M.gates[:, :, 0:E], oh1[:, :, :], oh2[:, :, :], ALU.add))
            link(v.tensor_scalar(tie[:, :, :], chosen[:, :, :], -BIG, BIG, ALU.mult, ALU.add))
            dve.wait_ge(sems["ranks"], 1)
            link(v.tensor_tensor(M.place[:, :, 0:E], T.ps[5][:, 0:4 * E].rearrange("p (m e) -> p m e", m=4),
                                 tie[:, :, :], ALU.add))
            dve.wait_ge(sems["counted"], 1)
            link(v.tensor_reduce(pm[:, :], T.ps[6][:, 0:E].rearrange("p (g u) -> p g u", u=2), AX.X, ALU.max))
            for r in range(1, MOE_ROUNDS):
                link(v.tensor_scalar(many[:, r - 1, :], pm[:, :], float(SLOTS * r), None, ALU.is_gt))
            link(v.tensor_copy(M.again[:, 1:], flat(many[:, :, :])))
            link(v.tensor_reduce(t2[:, 0, :], many[:, 0, :], AX.X, ALU.max))
            link(v.tensor_copy(M.again[:, 0:1], t2[:, 0, :]))


MOE_SEMS = ("w1_full*2 w3_full*2 w2_full*2 staged sel_ready selg_ready selT_done selT_taken gathered hg_act hg_dve "
            "up_done silu_done made half_down down_done yT_act yT_dve y_turned y_act y_dve scattered added")


def experts_phase(nc, T, sems, stale, M, pairs, first_pair):
    D1, F1 = 8 * 512, 4 * 1024
    with ExitStack() as ctx:
        def sb(name, *shape):
            return ctx.enter_context(nc.sbuf_tensor(f"moe_{name}_{nc.next_id()}", [P, *shape], F32))

        w1, w3, w2 = sb("w1", 2, D1), sb("w3", 2, D1), sb("w2", 2, F1)
        sel, selg, selT = sb("sel", 4, P), sb("selg", 4, P), sb("selT", S)
        hg, sil, mid, yT, y = sb("hg", KD, P), sb("silu", 2, 256), sb("mid", 2, 256), sb("yT", KD, P), sb("y", D)
        place, gate = sb("pair_place", 4, 2), sb("pair_gate", 4, 2)
        block = ctx.enter_context(nc.Block())
        ps = T.ps

        def turns(eng):
            if pairs == 1:
                yield 0
            else:
                with eng.Fori(0, pairs) as g:
                    yield g

        @block.sync
        def _(sync):
            clear(sync, stale)
            for g in turns(sync):
                for u in range(2):
                    e = 2 * g + u + 2 * first_pair
                    sync.wait_ge(sems["up_done"], 2 * g + u + 1)
                    sync.dma_start(w1[:, u, :], pick(T.dram["moe_w1"], e)).then_inc(sems["w1_full"][u], 16)
                    sync.dma_start(w3[:, u, :], pick(T.dram["moe_w3"], e)).then_inc(sems["w3_full"][u], 16)
                for u in range(2):
                    e = 2 * g + u + 2 * first_pair
                    sync.wait_ge(sems["down_done"], 2 * g + u + 1)
                    sync.dma_start(w2[:, u, :], pick(T.dram["moe_w2"], e)).then_inc(sems["w2_full"][u], 16)

        @block.gpsimd
        def _(pool):
            def select(n):
                two = ds(2 * n + 2 * first_pair, 2)
                nc.gpsimd.tensor_copy(place[:, :, :], M.place[:, :, two]).then_inc(sems["staged"], 1)
                nc.gpsimd.tensor_copy(gate[:, :, :], M.gates[:, :, two]).then_inc(sems["staged"], 1)
                pool.wait_ge(sems["staged"], 2)
                pool.sem_clear(sems["staged"])
                for m in range(4):
                    for u in range(2):
                        ins = nc.gpsimd.tensor_scalar(sel[:, m, SLOTS * u:SLOTS * u + SLOTS], M.slots[:, :],
                                                      place[:, m, u:u + 1], None, ALU.is_equal)
                ins.then_inc(sems["sel_ready"], 1)
                for m in range(4):
                    for u in range(2):
                        ins = nc.gpsimd.tensor_scalar(selg[:, m, SLOTS * u:SLOTS * u + SLOTS], M.slots[:, :],
                                                      place[:, m, u:u + 1], gate[:, m, u:u + 1], ALU.is_equal,
                                                      ALU.mult)
                ins.then_inc(sems["selg_ready"], 1)

            select(0)
            for g in turns(pool):
                pool.wait_ge(sems["gathered"], 2 * g + 2)
                pool.wait_ge(sems["selT_done"], g + 1)
                select(g + 1)

        @block.tensor
        def _(pe):
            def gather():
                for k in range(KD):
                    for m in range(4):
                        mm = nc.tensor.matmul(ps[k // 4][:, (k % 4) * P:(k % 4) * P + P],
                                              M.h_tok[:, m, k * P:k * P + P], sel[:, m, :], start=(m == 0),
                                              stop=(m == 3))
                    if k % 4 == 3:
                        mm.then_inc(sems["gathered"], 1)

            def turn_gates():
                for m in range(4):
                    mm = nc.tensor.transpose(ps[4][:, m * P:m * P + P], selg[:, m, :], T.ident[:, :])
                mm.then_inc(sems["selT_done"], 1)

            pe.sem_inc(sems["up_done"], 2)
            pe.sem_inc(sems["down_done"], 2)
            pe.wait_ge(sems["sel_ready"], 1)
            gather()
            pe.wait_ge(sems["selg_ready"], 1)
            turn_gates()
            for g in turns(pe):
                pe.wait_ge(sems["hg_act"], g + 1)
                pe.wait_ge(sems["hg_dve"], g + 1)
                for u in range(2):
                    c = slice(SLOTS * u, SLOTS * u + SLOTS)
                    pe.wait_ge(sems["w1_full"][u], 16 * g + 16)
                    pe.wait_ge(sems["w3_full"][u], 16 * g + 16)
                    pe.wait_ge(sems["added"], KD * g + 5 + u)
                    for half, w in ((0, w1), (1, w3)):
                        for f in range(4):
                            o = half * 256 + f * SLOTS
                            for k in range(KD):
                                mm = nc.tensor.matmul(ps[2 + u][:, o:o + SLOTS],
                                                      w[:, u, k * 512 + f * P:k * 512 + f * P + P], hg[:, k, c],
                                                      start=(k == 0), stop=(k == KD - 1))
                    mm.then_inc(sems["up_done"], 1)
                pe.wait_ge(sems["sel_ready"], g + 2)
                pe.wait_ge(sems["added"], KD * g + KD)
                gather()
                pe.wait_ge(sems["selT_taken"], g + 1)
                pe.wait_ge(sems["yT_dve"], g + 1)
                for half in range(2):
                    for u in range(2):
                        if half == 0:
                            pe.wait_ge(sems["w2_full"][u], 16 * g + 16)
                            pe.wait_ge(sems["made"], 2 * g + u + 1)
                        for k in range(4 * half, 4 * half + 4):
                            o = (k % 4) * P + SLOTS * u
                            for f in range(4):
                                mm = nc.tensor.matmul(ps[4 + half][:, o:o + SLOTS],
                                                      w2[:, u, f * D + k * P:f * D + k * P + P],
                                                      mid[:, u, f * SLOTS:f * SLOTS + SLOTS], start=(f == 0),
                                                      stop=(f == 3))
                        if half == 1:
                            mm.then_inc(sems["down_done"], 1)
                    if half == 0:
                        mm.then_inc(sems["half_down"], 1)
                for half, copied_, free in ((0, "yT_act", "y_act"), (1, "yT_dve", "y_dve")):
                    pe.wait_ge(sems[copied_], g + 2)
                    pe.wait_ge(sems[free], g + 1)
                    for k in range(4 * half, 4 * half + 4):
                        mm = nc.tensor.transpose(ps[6 + half][:, (k % 4) * P:(k % 4) * P + P], yT[:, k, :],
                                                 T.ident[:, :])
                    mm.then_inc(sems["y_turned"], 1)
                for k in range(KD):
                    if k == 0:
                        pe.wait_ge(sems["y_act"], g + 2)
                    if k == 2:
                        pe.wait_ge(sems["hg_act"], g + 2)
                        pe.wait_ge(sems["hg_dve"], g + 2)
                    if k >= 4:
                        pe.wait_ge(sems["added"], KD * g + KD + k - 3)
                        pe.wait_ge(sems["y_dve"], g + 2)
                    nc.tensor.matmul(ps[(2, 3, 0, 1)[k % 4]][:, :], y[:, k * P:k * P + P], selT[:, :], start=True,
                                     stop=True).then_inc(sems["scattered"], 1)
                pe.wait_ge(sems["selg_ready"], g + 2)
                turn_gates()

        @block.scalar
        def _(act):
            def rows(n):
                act.wait_ge(sems["gathered"], 2 * n + 1)
                nc.scalar.copy(flat(hg[:, 0:4, :]), ps[0][:, :]).then_inc(sems["hg_act"], 1)

            def gates(n):
                act.wait_ge(sems["selT_done"], n + 1)
                nc.scalar.copy(selT[:, :], ps[4][:, :]).then_inc(sems["selT_taken"], 1)

            act.sem_inc(sems["yT_act"], 1)
            act.sem_inc(sems["y_act"], 1)
            rows(0)
            gates(0)
            for g in turns(act):
                for u in range(2):
                    act.wait_ge(sems["up_done"], 2 * g + u + 3)
                    nc.scalar.activation(sil[:, u, :], ps[2 + u][:, 0:256], ACT.Silu).then_inc(
                        sems["silu_done"], 1)
                rows(g + 1)
                act.wait_ge(sems["half_down"], g + 1)
                nc.scalar.copy(flat(yT[:, 0:4, :]), ps[4][:, :]).then_inc(sems["yT_act"], 1)
                act.wait_ge(sems["y_turned"], 2 * g + 1)
                nc.scalar.copy(y[:, 0:512], ps[6][:, :]).then_inc(sems["y_act"], 1)
                gates(g + 1)

        @block.vector
        def _(dve):
            def rows(n):
                dve.wait_ge(sems["gathered"], 2 * n + 2)
                nc.vector.tensor_copy(flat(hg[:, 4:8, :]), ps[1][:, :]).then_inc(sems["hg_dve"], 1)

            dve.sem_inc(sems["yT_dve"], 1)
            dve.sem_inc(sems["y_dve"], 1)
            dve.sem_inc(sems["added"], KD)
            rows(0)
            for g in turns(dve):
                for u in range(2):
                    dve.wait_ge(sems["silu_done"], 2 * g + u + 1)
                    nc.vector.tensor_tensor(mid[:, u, :], sil[:, u, :], ps[2 + u][:, 256:512], ALU.mult).then_inc(
                        sems["made"], 1)
                rows(g + 1)
                dve.wait_ge(sems["down_done"], 2 * g + 4)
                nc.vector.tensor_copy(flat(yT[:, 4:8, :]), ps[5][:, :]).then_inc(sems["yT_dve"], 1)
                dve.wait_ge(sems["y_turned"], 2 * g + 2)
                nc.vector.tensor_copy(y[:, 512:1024], ps[7][:, :]).then_inc(sems["y_dve"], 1)
                for k in range(KD):
                    dve.wait_ge(sems["scattered"], KD * g + k + 1)
                    nc.vector.tensor_tensor(T.xT[:, k, :], T.xT[:, k, :], ps[(2, 3, 0, 1)[k % 4]][:, :],
                                            ALU.add).then_inc(sems["added"], 1)


def gains_phase(nc, sems, stale, dst, src):
    with nc.Block() as block:
        @block.sync
        def _(sync):
            clear(sync, stale)
            sync.dma_start(dst, src).then_inc(sems["loaded"], 16)
            sync.wait_ge(sems["loaded"], 16)


def next_places_phase(nc, stale, M):
    with nc.Block() as block:
        @block.sync
        def _(sync):
            clear(sync, stale)

        @block.vector
        def _(dve):
            nc.vector.tensor_scalar(M.place[:, :, :], M.place[:, :, :], float(-SLOTS), None, ALU.add)


def block_two(nc, T):
    sems, d, xT, hT = T.sems, T.dram, T.xT, T.hT
    norm, norm2, pa, pb, down, head = (sems[n] for n in ("norm", "norm2", "pa", "pb", "down", "head"))
    gain = lambda name: T.g2[:, GCOLS[name][0]:GCOLS[name][1]]
    with ExitStack() as ctx:
        conv, rope, att = (sem_set(nc, ctx, n, names) for n, names in (("conv", CONV_SEMS), ("rope", ROPE_SEMS),
                                                                      ("att", ATT_SEMS)))
        T.g2 = ctx.enter_context(nc.sbuf_tensor("gains2", [P, NGCOL], F32))
        gains_phase(nc, head, down, T.g2[:, :], d["gains2"])
        norm_phase(nc, T, norm, head, xT, gain("final_g"), xT)
        norm_phase(nc, T, norm2, norm, xT, gain("mix_norm_g_2"), hT)
        with nc.sbuf_tensor([P, KD, S], F32) as mixed:
            with nc.sbuf_tensor([P, 6, S], F32) as att_out, nc.sbuf_tensor([P, 2, S], F32) as conv_out:
                with nc.sbuf_tensor([P, 4, S], F32) as ag:
                    project_phase(nc, T, pa, norm2, lambda c: pick(d["w_in_2"], c), 2, hT, put(ag))
                    conv_phase(nc, T, conv, pa, ag, conv_out)
                with nc.sbuf_tensor([P, 12, S], F32) as qk, nc.sbuf_tensor([P, 4, 768], F32) as vt, \
                        nc.sbuf_tensor([P, 4, S], F32) as mask:
                    project_phase(nc, T, pa, conv, lambda c: pick(d["w_in_2"], c + 2), 6, hT, put(qk),
                                  load=lambda sync, sem: sync.dma_start(mask[:, :, :], d["att_mask"]).then_inc(
                                      sem, 16))
                    token_project_phase(nc, T, pb, pa, lambda c: pick(d["w_in_2"], c + 8), 3, hT, put_tokens(vt))
                    rope_phase(nc, T, rope, pb, qk, 12)
                    attention_phase(nc, T, att, rope, qk, qk, 6, vt, att_out, 6, 1, S, HEAD_DIM ** -0.5, mask)
                norm_phase(nc, T, norm, att, conv_out, gain("conv_out_g_2"), mixed[:, 0:2, :], tiles=2)
                norm_phase(nc, T, norm2, norm, att_out, gain("attn_out_g_2"), mixed[:, 2:8, :], tiles=6)
            down_phase(nc, T, down, norm2, lambda c: pick(d["w_out_2"], c), KD, mixed, xT)
        norm_phase(nc, T, norm, down, xT, gain("xattn_norm_g_2"), hT)
        with nc.sbuf_tensor([P, KD, MEM_LEN], F32) as mem, nc.sbuf_tensor([P, KD, MEM_LEN], F32) as mem_k, \
                nc.sbuf_tensor([P, 2, D], F32) as mem_v, nc.sbuf_tensor([P, KD, S], F32) as ox:
            norm_phase(nc, T, norm2, norm, mem, gain("mem_norm_g_2"), mem, width=MEM_LEN, eps=EPS,
                       load=lambda sync, sem: sync.dma_start(mem[:, :, :], d["memT"]).then_inc(sem, 16))
            project_phase(nc, T, pa, norm2, lambda c: pick(d["w_xk_2"], c), 4, mem, put(mem_k), width=MEM_LEN)
            token_project_phase(nc, T, pb, pa, lambda c: pick(d["w_xv_2"], c), 4, mem, put_tokens(mem_v), tiles=2)
            with nc.sbuf_tensor([P, KD, S], F32) as q:
                project_phase(nc, T, pa, pb, lambda c: pick(d["w_xq_2"], c), 4, hT, put(q))
                attention_phase(nc, T, att, pa, q, mem_k, 0, mem_v, ox, 2, 4, MEM_LEN, 256 ** -0.5)
            down_phase(nc, T, down, att, lambda c: pick(d["w_xo_2"], c), KD, ox, xT)
        norm_phase(nc, T, norm, down, xT, gain("moe_norm_g_2"), hT)
    with ExitStack() as ctx:
        route, moe = sem_set(nc, ctx, "route", ROUTE_SEMS), sem_set(nc, ctx, "moe", MOE_SEMS)
        T.g2 = ctx.enter_context(nc.sbuf_tensor("gains2b", [P, NGCOL], F32))

        def sb(name, *shape, dt=F32):
            return ctx.enter_context(nc.sbuf_tensor("moe_" + name, [P, *shape], dt))

        M = Named()
        M.h_tok = sb("h", 4, D)
        M.gates, M.place = sb("gates", 4, N_EXPERTS + 2), sb("place", 4, N_EXPERTS + 2)
        M.slots = sb("slots", SLOTS)
        M.again = sb("again", 1 + (MOE_ROUNDS - 1) * N_EXPERTS // 2, dt=mybir.dt.int32)
        route_phase(nc, T, route, norm, hT, M)
        experts_phase(nc, T, moe, route, M, N_EXPERTS // 2, 0)
        gains_phase(nc, head, moe, T.g2[:, :], d["gains2"])
        again = nc.values_load(M.again[0:1, 0:1], min_val=0, max_val=1)
        with nc.If(again > 0):
            with nc.Fori(0, MOE_ROUNDS - 1) as r:
                next_places_phase(nc, head, M)
                with nc.Fori(0, N_EXPERTS // 2) as pair:
                    needed = nc.values_load(M.again[0:1, ds(1 + N_EXPERTS // 2 * r + pair, 1)], min_val=0,
                                            max_val=1)
                    with nc.If(needed > 0):
                        experts_phase(nc, T, moe, head, M, 1, pair)
                        with nc.Block() as block:
                            @block.sync
                            def _(sync):
                                clear(sync, moe)
        norm_phase(nc, T, norm2, head, xT, gain("final_norm_g_2"), hT)


def two_blocks(nc, dram, out):
    with ExitStack() as ctx:
        T = shared(nc, ctx, dram)
        T.sems = shared_sems(nc, ctx)
        start = T.sems["start"]
        with nc.Block() as block:
            @block.sync
            def _(sync):
                loads = [(T.xT[:, :, :], dram["xT"]), (T.ident4[:, :], dram["ident4"]),
                         (T.head_ones[:, :], dram["head_ones"]), (T.scalars[:, :], dram["scalars"])]
                for dst, src in loads:
                    sync.dma_start(dst, src).then_inc(start["loaded"], 16)
                sync.wait_ge(start["loaded"], 16 * len(loads))

            @block.gpsimd
            def _(pool):
                nc.gpsimd.memset(T.ones[:, :], 1.0)

        block_one(nc, T)
        block_two(nc, T)
        with nc.Block() as block:
            @block.sync
            def _(sync):
                clear(sync, T.sems["norm2"])
                sync.dma_start(out, T.hT[:, :, :]).then_inc(T.sems["stored"]["done"], 16)
                sync.wait_ge(T.sems["stored"]["done"], 16)


def by_feature(v):
    v = np.asarray(v)
    return np.ascontiguousarray(np.swapaxes(v.reshape(v.shape[:-1] + (v.shape[-1] // P, P)), -1, -2))


def weight_chunks(w, cols):
    w = np.asarray(w)
    lead, (k, n) = w.shape[:-2], w.shape[-2:]
    w = w.reshape(lead + (k // P, P, n // cols, cols))
    m = len(lead)
    w = w.transpose(tuple(range(m)) + (m + 2, m + 1, m, m + 3))
    return np.ascontiguousarray(w).reshape(lead + (n // cols, P, k // P * cols))


def shape_constants():
    f4 = np.float32
    s = np.arange(P)
    head, tok = s // C, s % C
    same = head[:, None] == head[None, :]
    strict = (same & (tok[:, None] < tok[None, :])).astype(f4)
    upto = (tok[:, None] <= np.arange(C)[None, :]).astype(f4)
    masks = [np.tile(strict, (1, PAIRS)), np.tile(upto, (1, 2 * PAIRS))]
    for size in [1 << n for n in range(LEVELS + 1)]:
        m = same & (tok[:, None] // (2 * size) == tok[None, :] // (2 * size)) & \
            (tok[:, None] // size % 2 == 0) & (tok[None, :] // size % 2 == 1)
        masks.append(np.tile(m.astype(f4), (1, PAIRS)))
        if size == 1:
            first = m.astype(f4)
    masks.append(np.tile(first.T, (1, PAIRS)))
    return {
        "ident4": np.tile(np.eye(P, dtype=f4), (1, 4)),
        "head_ones": same.astype(f4),
        "chunk_start": np.tile((np.arange(S) % C != 0).astype(f4), (P, 1)),
        "scalars": np.tile(np.array([[EPS, GN_EPS, LN_EPS, 8.5 * np.log(2.0)]], f4), (P, 1)),
        "rmask": np.stack(masks, 1).astype(f4),
    }


def ret_tables():
    f4 = np.float32
    inv = 1.0 / (f4(10000.0) ** np.linspace(0.0, 1.0, 32, dtype=f4))
    ang = (np.arange(S, dtype=f4)[:, None] * inv[None, :]).astype(f4)
    rep = lambda t: np.tile(t.T, (4, 1))
    rot = np.zeros((P, P), f4)
    for q in range(P):
        if q % 64 < 32:
            rot[q + 32, q] = -1.0
        else:
            rot[q - 32, q] = 1.0
    gamma = np.log(f4(1.0) - f4(2.0) ** (f4(-5.0) - np.arange(RET_HEADS, dtype=f4))).astype(np.float64)
    diff = np.arange(S)[None, :] - np.arange(P)[:, None]
    decay = np.where(diff[:, None, :] >= 0, np.exp(np.maximum(diff, 0)[:, None, :] * gamma[None, :, None]), 0.0)
    return {"ret_cossin": np.stack([rep(np.cos(ang)), rep(np.sin(ang))], 1).astype(f4), "rot": rot,
            "ret_decay": (decay * 64 ** -0.5).astype(f4)}


def layout(a):
    a = {k: np.asarray(v) for k, v in a.items()}
    L = DEPTH
    flat2 = lambda n: a[n].reshape(L, -1)
    out = shape_constants()
    out["layer_cols"] = np.concatenate(
        [by_feature(flat2(n)) for n in ("norm1_g", "rw_mu", "rw_w0", "rw_a0", "rw_k_k", "rw_k_a", "rw_r_k",
                                        "rw_lnx_g", "rw_lnx_b", "norm2_g")], axis=-1)
    low = np.concatenate([a["rw_w_up"], a["rw_a_up"]], axis=1)
    out.update(ret_tables())
    x = a["x"][0]
    out["xT"] = np.ascontiguousarray(x.reshape(S, KD, P).transpose(2, 1, 0))
    w_in = weight_chunks(a["w_in"], 256)
    first_gate = (RW_T * P + 1536 + 1024) // 256
    gates = w_in[:, first_gate:]
    out["w_in"] = w_in[:, :first_gate]
    out["w_merge"] = np.concatenate([gates, weight_chunks(a["w_branch"], 256).reshape(L, 12, P, -1)], axis=-1)
    out["w_out"] = weight_chunks(a["w_out"], P)
    up = a["ffn_w_up"]
    gate, val = (weight_chunks(up[:, :, o:o + D_FF], P).reshape(L, FT, P, KD, P) for o in (0, D_FF))
    out["ffn_up"] = np.concatenate([gate, val], axis=-1).reshape(L, FT, P, KD * 256)
    out["ffn_down"] = weight_chunks(a["ffn_w_down"], P)
    taps = np.concatenate([a["ffn_conv_w"], a["ffn_conv_b"][:, None]], axis=1)
    taps = taps.reshape(L, 4, 2, FT, P).transpose(0, 4, 3, 2, 1)
    out["ffn_conv"] = np.ascontiguousarray(taps).reshape(L, P, FT, 8)
    out["sg_wT"] = np.ascontiguousarray(a["sg_w_s"].transpose(0, 3, 1, 2)).reshape(L, P, S)
    out["sg_rows"] = np.concatenate([a["sg_ln_g"], a["sg_ln_b"], a["sg_b"].reshape(L, -1)], axis=-1)
    out["causal"] = np.tile((np.arange(P)[:, None] <= np.arange(P)[None, :]).astype(np.float32), (1, 4))
    out["gains2"] = np.concatenate([by_feature(a[n].reshape(-1)) for n in GCOLS], axis=-1)
    out["w_in_2"] = weight_chunks(a["w_in_2"][0], 256)
    for n in ("w_xq_2", "w_xk_2", "w_xv_2"):
        out[n] = weight_chunks(a[n][0], 256)
    for n in ("w_out_2", "w_xo_2"):
        out[n] = weight_chunks(a[n][0], P)
    par = np.concatenate([a["conv_dw_w_2"][0], a["conv_dw_b_2"], a["conv_ln_g_2"], a["conv_ln_b_2"]], axis=0)
    out["conv_par"] = np.ascontiguousarray(par.reshape(CONV_KERNEL + 3, 2, P).transpose(2, 1, 0))
    out["positions"] = a["positions_2"].reshape(1, S)
    out["memT"] = np.ascontiguousarray(a["mem_2"][0].reshape(MEM_LEN, KD, P).transpose(2, 1, 0))
    inv = 1.0 / (np.float32(10000.0) ** (np.arange(32, dtype=np.float32) * np.float32(2.0 / 64)))
    out["rope_inv"] = np.tile(inv.astype(np.float32), 4)[:, None]
    off = np.abs(np.arange(S)[:, None] - np.arange(S)[None, :])
    seen = (off <= 64).astype(int) + ((off <= 256) & (off % 4 == 0)) + (off % 16 == 0)
    mask = np.where(seen > 0, np.log(np.maximum(seen, 1)), -1e30).astype(np.float32)
    out["att_mask"] = np.ascontiguousarray(mask.reshape(4, P, S).transpose(1, 0, 2))
    out["router_w"] = np.ascontiguousarray(np.concatenate([a["w_group_2"][0], a["w_router_2"][0]], axis=-1).reshape(
        KD, P, -1).transpose(1, 0, 2))
    out["router_b"] = np.concatenate([a["b_group_2"], a["b_router_2"]], axis=-1)
    out["iota"] = np.tile(np.arange(SLOTS, dtype=np.float32), (P, 1))
    out["before"] = (np.arange(P)[:, None] < np.arange(P)[None, :]).astype(np.float32)
    for n in ("w1_2", "w3_2", "w2_2"):
        w = a[n][0]
        out["moe_" + n[:2]] = np.ascontiguousarray(w.reshape(N_EXPERTS, -1, P, w.shape[-1]).transpose(
            0, 2, 1, 3)).reshape(N_EXPERTS, P, -1)
    out["rw_up"] = np.stack([low, a["rw_g_up"]], axis=2)
    return out


def kernel(**inputs):
    import concourse.bacc as bacc
    from concourse.bass_utils import run_bass_kernel_spmd

    nc = bacc.Bacc("TRN2", target_bir_lowering=False, num_devices=1)
    arrays = {f"in_{name}": a for name, a in layout(inputs).items()}
    dram = {name[3:]: nc.dram_tensor(name, a.shape, mybir.dt.from_np(a.dtype), kind="ExternalInput").ap()
            for name, a in arrays.items()}
    out = nc.dram_tensor("out", (P, KD, S), F32, kind="ExternalOutput").ap()
    two_blocks(nc, dram, out)
    got = run_bass_kernel_spmd(nc, [arrays], core_ids=[0]).results[0]["out"]
    return np.ascontiguousarray(got.transpose(2, 1, 0)).reshape(1, S, D)
```

```python
from contextlib import ExitStack

import numpy as np

import concourse.bass as bass
from concourse import mybir

F32 = mybir.dt.float32
F32R = mybir.dt.float32r
ALU = mybir.AluOpType
ACT = mybir.ActivationFunctionType
AX = mybir.AxisListType

P = 128
D = 1024
S = 512
KD = D // P
DEPTH = 2
RW_W = 512
RW_T = 14
PAIRS = RW_W // P
C = 64
NCH = S // C
LEVELS = 5
GN_EPS = 64e-5
LN_EPS = 1e-5
EPS = 1e-6
DECAY = float(np.exp(-0.5))
RET_HEADS = 4
SG_GROUPS = 4
D_FF = 2816
FT = D_FF // P
CONV_CH = 256
CONV_KERNEL = 31
HEAD_DIM = 64
ATT_W = 768
MEM_LEN = 256
N_GROUPS = 4
N_EXPERTS = 32
SLOTS = 64
MOE_ROUNDS = S // SLOTS
BIG = 16384.0
TWO_PI = (6.28125, 0.0019353032, 2 * np.pi - 6.28125 - 0.0019353032)
ds = bass.ds

LCOLS = {}
_n = 0
for _name, _k in (("norm1_g", 8), ("mu", 14), ("w0", 4), ("a0", 4), ("k_k", 4), ("k_a", 4), ("r_k", 4),
                  ("lnx_g", 4), ("lnx_b", 4), ("norm2_g", 8)):
    LCOLS[_name] = (_n, _n + _k)
    _n += _k
NLCOL = _n

GCOLS = {}
_n = 0
for _name, _k in (("final_g", 8), ("mix_norm_g_2", 8), ("conv_out_g_2", 2), ("attn_out_g_2", 6),
                  ("xattn_norm_g_2", 8), ("mem_norm_g_2", 8), ("moe_norm_g_2", 8), ("final_norm_g_2", 8)):
    GCOLS[_name] = (_n, _n + _k)
    _n += _k
NGCOL = _n


class Chain:

    def __init__(self, eng, sem):
        self.eng, self.sem, self.n = eng, sem, 0

    def __call__(self, ins):
        self.n += 1
        ins.then_inc(self.sem, 1)
        self.eng.wait_ge(self.sem, self.n)

    def restart(self):
        self.eng.sem_clear(self.sem)
        self.n = 0


def two_slots(eng, n, first=0):
    if n // 2 > first:
        with eng.Fori(first, n // 2) as i:
            for s in (0, 1):
                yield i, s
    if n % 2:
        yield n // 2, 0


def fetch_first(T, sems, cols, weights):
    def fetch(sync, s):
        sync.dma_start(T.w[:, s, 0:cols], weights(s)).then_inc(sems["w_full"][s], 16)
    return fetch


def fetch_both(sync, ahead):
    if ahead is not None:
        ahead(sync, 0)
        ahead(sync, 1)


def last_chunk(n, s):
    return n - 1 - (n - 1 - s) % 2


def flat(ap):
    return ap.rearrange("p a b -> p (a b)")


class Named:
    pass


def clear(sync, sems):
    for s in sems["all"]:
        sync.sem_clear(s)


def sem_set(nc, ctx, prefix, names):
    named, every = {}, []
    for n in names.split():
        n, _, k = n.partition("*")
        made = [ctx.enter_context(nc.semaphore(f"{prefix}_{n}{i if k else ''}")) for i in range(int(k or 1))]
        named[n] = made if k else made[0]
        every += made
    return {"all": every, **named}


def rsqrt(act, sem, before, out, sums, scale, eps):
    act.activation(out, sums, ACT.Ln, bias=eps, scale=scale).then_inc(sem, 1)
    act.wait_ge(sem, before + 1)
    act.activation(out, out, ACT.Exp, scale=-0.5).then_inc(sem, 1)


NORM_SEMS = "loaded squared summed rooted"


def norm_phase(nc, T, sems, stale, src, gain, dst, tiles=KD, width=S, eps=EPS, load=None, ahead=None):
    with nc.sbuf_tensor([P, tiles, width], F32) as sq, nc.sbuf_tensor([P, width], F32) as rstd, \
            nc.Block() as block:
        @block.sync
        def _(sync):
            clear(sync, stale)
            if load is not None:
                load(sync, sems["loaded"])
            fetch_both(sync, ahead)

        @block.scalar
        def _(act):
            if load is not None:
                act.wait_ge(sems["loaded"], 16)
            for k in range(tiles):
                nc.scalar.activation(sq[:, k, :], src[:, k, :], ACT.Square).then_inc(sems["squared"], 1)
            act.wait_ge(sems["summed"], 1)
            rsqrt(act, sems["rooted"], 0, rstd[:, :], T.ps[0][:, 0:width], 1.0 / (tiles * P), T.eps(eps))

        @block.tensor
        def _(pe):
            for k in range(tiles):
                pe.wait_ge(sems["squared"], k + 1)
                mm = nc.tensor.matmul(T.ps[0][:, 0:width], T.ones[:, :], sq[:, k, :], start=(k == 0),
                                      stop=(k == tiles - 1))
            mm.then_inc(sems["summed"], 1)

        @block.vector
        def _(dve):
            if load is not None:
                dve.wait_ge(sems["loaded"], 16)
            dve.wait_ge(sems["rooted"], 2)
            for k in range(tiles):
                nc.vector.scalar_tensor_tensor(out=dst[:, k, :], in0=src[:, k, :], scalar=gain[:, k:k + 1],
                                               in1=rstd[:, :], op0=ALU.mult, op1=ALU.mult)


SPLIT_SEMS = "w_full*2 w_hi w_lo rhs_hi rhs_lo"


class Split:

    def __init__(self, nc, ctx, T, sems, kt, rhs_hi=None, rhs_lo=None, width=S):
        self.nc, self.T, self.sems, self.kt, self.rhs_tiles = nc, T, sems, kt, 0
        n = nc.next_id()

        def part(name, *shape):
            return ctx.enter_context(nc.sbuf_tensor(f"{name}_{n}", [P, *shape], F32R))

        self.w_hi, self.w_lo = part("w_hi", 2, kt, P), part("w_lo", 2, kt, P)
        self.rhs_hi, self.rhs_lo = rhs_hi, rhs_lo
        if rhs_hi is None:
            self.rhs_hi, self.rhs_lo = part("rhs_hi", kt, width), part("rhs_lo", kt, width)
            self.rhs_tiles = kt

    def raw(self, s, c, cols):
        return self.T.w[:, s, 0:self.kt * cols].rearrange("p (k c) -> p k c", k=self.kt)[:, :, c:c + P]

    def high(self, raw, t):
        self.nc.scalar.copy(self.w_hi[:, t, :, :], raw).then_inc(self.sems["w_hi"], 1)

    def low(self, pool, n, raw, t):
        pool.wait_ge(self.sems["w_hi"], n + 1)
        self.nc.gpsimd.tensor_tensor(self.w_lo[:, t, :, :], raw, self.w_hi[:, t, :, :].bitcast(F32),
                                     ALU.subtract).then_inc(self.sems["w_lo"], 1)

    def rhs(self, dve, rhs):
        for k in range(self.kt):
            self.nc.vector.tensor_copy(self.rhs_hi[:, k, :], rhs[:, k, :]).then_inc(self.sems["rhs_hi"], 1)
        dve.wait_ge(self.sems["rhs_hi"], self.kt)
        for k in range(self.kt):
            self.nc.vector.tensor_tensor(self.rhs_lo[:, k, :], rhs[:, k, :], self.rhs_hi[:, k, :].bitcast(F32),
                                         ALU.subtract).then_inc(self.sems["rhs_lo"], 1)

    def products(self, pe, bank, n, lows, t):
        hi, lo, kt = self.w_hi, self.w_lo, self.kt
        pe.wait_ge(self.sems["w_hi"], n + 1)
        for k in range(kt):
            self.nc.tensor.matmul(bank, hi[:, t, k, :], self.rhs_hi[:, k, :], start=(k == 0), stop=False)
        if self.rhs_tiles:
            pe.wait_ge(self.sems["rhs_lo"], self.rhs_tiles)
        for k in range(kt):
            self.nc.tensor.matmul(bank, hi[:, t, k, :], self.rhs_lo[:, k, :], start=False, stop=False)
        pe.wait_ge(self.sems["w_lo"], lows)
        for k in range(kt):
            mm = self.nc.tensor.matmul(bank, lo[:, t, k, :], self.rhs_hi[:, k, :], start=False, stop=(k == kt - 1))
        return mm


def with_next(eng, n):
    last = (n - 1) // 2
    if last:
        with eng.Fori(0, last) as i:
            yield (i, 0), (i, 1)
            yield (i, 1), (i + 1, 0)
    if n % 2 == 0:
        yield (last, 0), (last, 1)
    yield (last, (n - 1) % 2), None


PROJECT_SEMS = SPLIT_SEMS + " loaded act_took dve_took even_done odd_done"


def project_phase(nc, T, sems, stale, weights, chunks, rhs, write, kt=KD, width=S, load=None, ahead=None):
    done = (sems["even_done"], sems["odd_done"])
    with ExitStack() as ctx:
        split = Split(nc, ctx, T, sems, kt, width=width)
        block = ctx.enter_context(nc.Block())

        @block.sync
        def _(sync):
            clear(sync, stale)
            if load is not None:
                load(sync, sems["loaded"])
            for i, s in two_slots(sync, chunks, first=1):
                sync.wait_ge(sems["w_lo"], 4 * i + 2 * s + 2)
                sync.dma_start(T.w[:, s, 0:kt * 256], weights(2 * i + s)).then_inc(sems["w_full"][s], 16)
            if ahead is not None:
                for s in range(2):
                    sync.wait_ge(sems["w_lo"], 4 + 2 * last_chunk(chunks, s) + 2)
                    ahead(sync, s)

        @block.gpsimd
        def _(pool):
            pool.sem_inc(sems["w_lo"], 4)
            for i, s in two_slots(pool, chunks):
                for t in range(2):
                    split.low(pool, 4 * i + 2 * s + t, split.raw(s, t * P, 256), t)

        @block.tensor
        def _(pe):
            pe.sem_inc(done[0], 1)
            pe.sem_inc(done[1], 1)
            pe.wait_ge(sems["rhs_hi"], kt)
            for i, s in two_slots(pe, chunks):
                for t in range(2):
                    pe.wait_ge((sems["act_took"], sems["dve_took"])[t], 2 * i + s + 1)
                    n = 4 * i + 2 * s + t
                    split.products(pe, T.ps[2 * s + t][:, 0:width], n, n + 5, t).then_inc(done[t], 1)

        @block.scalar
        def _(act):
            act.sem_inc(sems["act_took"], 2)
            if load is not None:
                act.wait_ge(sems["loaded"], 16)

            def high(i, s, t):
                act.wait_ge(sems["w_full"][s], 16 * i + 16)
                act.wait_ge(done[t], 2 * i + s + 1)
                split.high(split.raw(s, t * P, 256), t)

            high(0, 0, 0)
            high(0, 0, 1)
            for (i, s), behind in with_next(act, chunks):
                if behind:
                    high(*behind, 0)
                act.wait_ge(done[0], 2 * i + s + 2)
                write(nc.scalar, 2 * i + s, 0, T.ps[2 * s][:, 0:width]).then_inc(sems["act_took"], 1)
                if behind:
                    high(*behind, 1)

        @block.vector
        def _(dve):
            dve.sem_inc(sems["dve_took"], 2)
            split.rhs(dve, rhs)
            if load is not None:
                dve.wait_ge(sems["loaded"], 16)
            for i, s in two_slots(dve, chunks):
                dve.wait_ge(done[1], 2 * i + s + 2)
                write(nc.vector, 2 * i + s, 1, T.ps[2 * s + 1][:, 0:width]).then_inc(sems["dve_took"], 1)


def token_project_phase(nc, T, sems, stale, weights, chunks, lhs, write, tiles=4, ahead=None):
    with nc.Block() as block:
        @block.sync
        def _(sync):
            clear(sync, stale)
            for i, s in two_slots(sync, chunks, first=1):
                sync.wait_ge(sems["dve_took"], 2 * i + s + 1)
                sync.dma_start(T.w[:, s, 0:KD * 256], weights(2 * i + s)).then_inc(sems["w_full"][s], 16)
            if ahead is not None:
                for s in range(2):
                    sync.wait_ge(sems["odd_done"], (last_chunk(chunks, s) + 1) * (tiles // 2))
                    ahead(sync, s)

        @block.tensor
        def _(pe):
            for i, s in two_slots(pe, chunks):
                pe.wait_ge(sems["w_full"][s], 16 * i + 16)
                pe.wait_ge(sems["act_took"], 2 * i + s + 1)
                pe.wait_ge(sems["dve_took"], 2 * i + s + 1)
                for m in range(tiles):
                    for k in range(KD):
                        mm = nc.tensor.matmul(T.ps[4 * s + m][:, 0:256], lhs[:, k, m * P:m * P + P],
                                              T.w[:, s, k * 256:k * 256 + 256], start=(k == 0), stop=(k == KD - 1))
                    mm.then_inc((sems["even_done"], sems["odd_done"])[m % 2], 1)

        @block.scalar
        def _(act):
            act.sem_inc(sems["act_took"], 2)
            for i, s in two_slots(act, chunks):
                for m in range(0, tiles, 2):
                    act.wait_ge(sems["even_done"], (2 * i + s) * (tiles // 2) + m // 2 + 1)
                    w = write(nc.scalar, 2 * i + s, m, T.ps[4 * s + m][:, 0:256])
                w.then_inc(sems["act_took"], 1)

        @block.vector
        def _(dve):
            dve.sem_inc(sems["dve_took"], 2)
            for i, s in two_slots(dve, chunks):
                for m in range(1, tiles, 2):
                    dve.wait_ge(sems["odd_done"], (2 * i + s) * (tiles // 2) + m // 2 + 1)
                    w = write(nc.vector, 2 * i + s, m, T.ps[4 * s + m][:, 0:256])
                w.then_inc(sems["dve_took"], 1)


def copied(eng, dst, src):
    return eng.copy(dst, src) if eng.engine == mybir.EngineType.Activation else eng.tensor_copy(dst, src)


def rwkv_prep_phase(nc, T, sems, stale, R):
    p = R.p
    col = lambda name, j: T.lc[:, LCOLS[name][0] + j:LCOLS[name][0] + j + 1]
    with nc.sbuf_tensor([P, 2, RW_W], F32) as up, nc.sbuf_tensor([P, 2, S], F32) as tmp, \
            nc.sbuf_tensor([P, PAIRS, S], F32) as w, nc.sbuf_tensor([P, PAIRS, S], F32) as a, \
            nc.sbuf_tensor([P, PAIRS, S], F32) as norm, \
            nc.sbuf_tensor([P, 2, S], F32) as sq, nc.sbuf_tensor([P, 2, S], F32) as rk, \
            nc.sbuf_tensor([P, 4], F32) as one_less_ka, nc.sbuf_tensor([P, S], F32) as chunk_start, \
            nc.Block() as block:
        @block.sync
        def _(sync):
            clear(sync, stale)
            sync.dma_start(up[:, :, :], R.up()).then_inc(sems["loaded"], 16)
            sync.dma_start(chunk_start[:, :], T.dram["chunk_start"]).then_inc(sems["loaded"], 16)

        @block.vector
        def _(dve):
            link = Chain(dve, sems["dve"])
            dve.wait_ge(sems["loaded"], 32)
            for n, t in enumerate((12, 13) + tuple(range(12))):
                d = tmp[:, n % 2, :]
                nc.vector.tensor_tensor(d[:, 1:S], p[:, t, 0:S - 1], p[:, t, 1:S], ALU.subtract)
                link(nc.vector.tensor_scalar(d[:, 0:1], p[:, t, 0:1], -1.0, None, ALU.mult))
                nc.vector.scalar_tensor_tensor(out=p[:, t, :], in0=d, scalar=col("mu", t), in1=p[:, t, :],
                                               op0=ALU.mult, op1=ALU.add).then_inc(sems["shifted"], 1)
            dve.wait_ge(sems["shifted"], 14)
            link(nc.vector.tensor_scalar(one_less_ka[:, :], T.lc[:, LCOLS["k_a"][0]:LCOLS["k_a"][1]], -1.0, 1.0,
                                         ALU.mult, ALU.add))
            for j in range(PAIRS):
                r, k, v = p[:, j, :], p[:, 4 + j, :], p[:, 8 + j, :]
                kk = R.alpha[:, j, :]
                link(nc.vector.tensor_scalar(kk, k, col("k_k", j), None, ALU.mult))
                if j >= 2:
                    dve.wait_ge(sems["kk_summed"], j - 1)
                nc.vector.tensor_tensor(sq[:, j % 2, :], kk, kk, ALU.mult).then_inc(sems["kk_squared"], 1)
                dve.wait_ge(sems["rate_ready"], j + 1)
                d = tmp[:, 0, :]
                link(nc.vector.tensor_scalar(d, a[:, j, :], col("k_a", j), one_less_ka[:, j:j + 1], ALU.mult,
                                             ALU.add))
                link(nc.vector.tensor_tensor(k, k, d, ALU.mult))
                if j >= 2:
                    dve.wait_ge(sems["rk_summed"], j - 1)
                nc.vector.scalar_tensor_tensor(out=rk[:, j % 2, :], in0=r, scalar=col("r_k", j), in1=k,
                                               op0=ALU.mult, op1=ALU.mult).then_inc(sems["rk_ready"], 1)
                dve.wait_ge(sems["kk_summed"], j + 1)
                nc.vector.tensor_scalar(norm[:, j, :], T.ps[4 + j % 2][:, :], 1e-24, None, ALU.max).then_inc(
                    sems["norm_guarded"], 1)
                dve.wait_ge(sems["decay_ready"], j + 1)
                nc.vector.tensor_tensor_scan(w[:, j, :], chunk_start[:, :], w[:, j, :], 0.0, ALU.mult,
                                             ALU.add).then_inc(sems["decay_scanned"], 1)
                dve.wait_ge(sems["norm_rooted"], 2 * j + 2)
                link(nc.vector.tensor_tensor(kk, kk, norm[:, j, :], ALU.mult))
                link(nc.vector.tensor_tensor(d, kk, a[:, j, :], ALU.mult))
                run = R.run[:, j, :]
                dve.wait_ge(sems["run_ready"], 2 * j + 2)
                nc.vector.tensor_tensor(R.beta[:, j, :], d, w[:, j, :], ALU.mult)
                nc.vector.tensor_tensor(R.kappa[:, j, :], k, w[:, j, :], ALU.mult)
                nc.vector.tensor_tensor(R.rho[:, j, :], r, run, ALU.mult)
                link(nc.vector.tensor_copy(tmp[:, 1, 0:S:C], kk[:, 0:S:C]))
                nc.vector.tensor_tensor(tmp[:, 0, 1:S], kk[:, 1:S], run[:, 0:S - 1], ALU.mult)
                link(nc.vector.tensor_copy(tmp[:, 0, 0:1], kk[:, 0:1]))
                link(nc.vector.tensor_copy(R.alpha[:, j, :], tmp[:, 0, :]))
                link(nc.vector.tensor_copy(R.alpha[:, j, 0:S:C], tmp[:, 1, 0:S:C]))
                dve.wait_ge(sems["rk_summed"], j + 1)
                nc.vector.tensor_tensor(R.bonus[:, j, :], T.ps[6 + j % 2][:, :], v, ALU.mult).then_inc(
                    sems["bonus_done"], 1)

        @block.scalar
        def _(act):
            act.wait_ge(sems["shifted"], 2)
            nc.scalar.activation(p[0:64, 12, :], p[0:64, 12, :], ACT.Tanh).then_inc(sems["low_ready"], 1)
            nc.scalar.activation(p[:, 13, :], p[:, 13, :], ACT.Sigmoid).then_inc(sems["low_ready"], 1)
            for j in range(PAIRS):
                act.wait_ge(sems["decay_summed"], j + 1)
                nc.scalar.activation(w[:, j, :], T.ps[0][:, :], ACT.Sigmoid, bias=col("w0", j)).then_inc(
                    sems["decay_ready"], 1)
                act.wait_ge(sems["rate_summed"], j + 1)
                nc.scalar.activation(a[:, j, :], T.ps[1][:, :], ACT.Sigmoid, bias=col("a0", j)).then_inc(
                    sems["rate_ready"], 1)
                act.wait_ge(sems["gate_summed"], j + 1)
                nc.scalar.copy(R.gate[:, j, :], T.ps[2][:, :]).then_inc(sems["gate_taken"], 1)
            for j in range(PAIRS):
                act.wait_ge(sems["norm_guarded"], j + 1)
                nc.scalar.activation(norm[:, j, :], norm[:, j, :], ACT.Ln, scale=2.0 ** 17).then_inc(
                    sems["norm_rooted"], 1)
                act.wait_ge(sems["norm_rooted"], 2 * j + 1)
                nc.scalar.activation(norm[:, j, :], norm[:, j, :], ACT.Exp, scale=-0.5,
                                     bias=T.half_17ln2[:, :]).then_inc(sems["norm_rooted"], 1)
                act.wait_ge(sems["decay_scanned"], j + 1)
                nc.scalar.activation(R.run[:, j, :], w[:, j, :], ACT.Exp, scale=-DECAY).then_inc(sems["run_ready"], 1)
                nc.scalar.activation(w[:, j, :], w[:, j, :], ACT.Exp, scale=DECAY).then_inc(sems["run_ready"], 1)

        @block.tensor
        def _(pe):
            pe.wait_ge(sems["loaded"], 32)
            pe.wait_ge(sems["low_ready"], 2)
            for j in range(PAIRS):
                if j:
                    pe.wait_ge(sems["decay_ready"], j)
                    pe.wait_ge(sems["rate_ready"], j)
                    pe.wait_ge(sems["gate_taken"], j)
                o = slice(j * P, j * P + P)
                nc.tensor.matmul(T.ps[0][:, :], up[0:64, 0, o], p[0:64, 12, :], start=True, stop=True).then_inc(
                    sems["decay_summed"], 1)
                nc.tensor.matmul(T.ps[1][:, :], up[64:128, 0, o], p[64:128, 12, :], start=True,
                                 stop=True).then_inc(sems["rate_summed"], 1)
                nc.tensor.matmul(T.ps[2][:, :], up[:, 1, o], p[:, 13, :], start=True, stop=True).then_inc(
                    sems["gate_summed"], 1)
            for j in range(PAIRS):
                if j >= 2:
                    pe.wait_ge(sems["bonus_done"], j - 1)
                pe.wait_ge(sems["kk_squared"], j + 1)
                nc.tensor.matmul(T.ps[4 + j % 2][:, :], T.head_ones[:, :], sq[:, j % 2, :], start=True,
                                 stop=True).then_inc(sems["kk_summed"], 1)
                pe.wait_ge(sems["rk_ready"], j + 1)
                nc.tensor.matmul(T.ps[6 + j % 2][:, :], T.head_ones[:, :], rk[:, j % 2, :], start=True,
                                 stop=True).then_inc(sems["rk_summed"], 1)


RWKV_PREP_SEMS = ("loaded shifted dve low_ready norm_guarded norm_rooted decay_scanned run_ready decay_summed rate_summed gate_summed rate_ready gate_taken "
                  "decay_ready kk_squared kk_summed rk_ready rk_summed bonus_done")


def rwkv_chunk_phases(nc, T, pre, rec, R):
    with ExitStack() as ctx:
        def sb(name, *shape):
            return ctx.enter_context(nc.sbuf_tensor(f"rec_{name}", [P, *shape], F32))

        def own_buffers(X, square):
            X.aB, X.bB, X.kB, X.vB, X.LT, X.AkT = (square(n) for n in "aB bB kB vB LT AkT".split())
            X.X, X.XT, X.T1, X.bT, X.kT, X.vT = (square(n) for n in "X XT T1 bT kT vT".split())
            X.PC = sb("PC" + X.name, PAIRS, 1)
            return X

        even, odd = Named(), Named()
        even.name, odd.name = "0", "1"
        own_buffers(even, lambda n: sb(n, PAIRS, P))
        even.BT, even.ArT, even.rho = sb("BT", 2, PAIRS * P), sb("ArT", 2, PAIRS, C), sb("rho", PAIRS, C)
        spare = iter(range(12))
        weights = T.w.rearrange("p s c -> p (s c)")

        def in_weights(_):
            i = next(spare)
            return weights[:, i * S:i * S + S].rearrange("p (j c) -> p j c", j=PAIRS)

        own_buffers(odd, in_weights)
        odd.BT = R.p[:, 0:2, :]
        odd.ArT = R.p[:, 2, :].rearrange("p (a b c) -> p a b c", a=2, b=PAIRS)
        odd.rho = R.p[:, 3, 0:PAIRS * C].rearrange("p (j c) -> p j c", j=PAIRS)
        sets = (even, odd)
        M, Rs, Un = sb("M", PAIRS, P), sb("Rs", PAIRS, P), sb("Un", PAIRS, P)
        rmask = sb("masks", LEVELS + 4, S)

        def pair(j):
            return slice(j * P, j * P + P)

        with nc.Block() as block:
            @block.sync
            def _(sync):
                clear(sync, rec["stale"])
                sync.dma_start(rmask[:, :, :], T.dram["rmask"]).then_inc(rec["masks_loaded"], 16)
                sync.wait_ge(rec["masks_loaded"], 16)

            @block.gpsimd
            def _(pool):
                for B in sets:
                    for t in (B.aB, B.bB, B.kB, B.vB):
                        nc.gpsimd.memset(t[:, :, :], 0.0)
                nc.gpsimd.memset(M[:, :, :], 0.0)

        with nc.Fori(0, NCH // 2) as c:
            with nc.Block() as block:
                @block.sync
                def _(sync):
                    clear(sync, rec)

                @block.scalar
                def _(act):
                    for s, B in enumerate(sets):
                        now = ds(2 * c * C + s * C, C)
                        for h in range(2):
                            q = slice(64 * h, 64 * h + 64)
                            nc.scalar.copy(B.aB[q, :, 64 * h:64 * h + 64], R.alpha[q, :, now]).then_inc(
                                pre[s]["blocks_act"], 1)
                            nc.scalar.copy(B.kB[q, :, 64 * h:64 * h + 64], R.kappa[q, :, now]).then_inc(
                                pre[s]["blocks_act"], 1)
                        nc.scalar.copy(B.PC[:, :, :], R.run[:, :, ds(2 * c * C + s * C + C - 1, 1)])
                    for s, B in enumerate(sets):
                        for n, t in enumerate((B.bT, B.kT, B.vT)):
                            act.wait_ge(pre[s]["turned"], n + 1)
                            nc.scalar.copy(flat(t[:, :, :]), T.ps[4 * s + n][:, :]).then_inc(
                                pre[s]["turned_taken"], 1)
                    for lev in range(LEVELS):
                        for s, B in enumerate(sets):
                            act.wait_ge(pre[s]["t1_done"], lev + 1)
                            nc.scalar.copy(flat(B.T1[:, :, :]), T.ps[4 * s + 3][:, :]).then_inc(
                                pre[s]["t1_taken"], 1)

                @block.gpsimd
                def _(pool):
                    for lev in range(LEVELS):
                        for s, B in enumerate(sets):
                            if lev == 0:
                                pool.wait_ge(pre[s]["lt_ready"], 1)
                            if lev >= 2:
                                pool.wait_ge(pre[s]["t1_done"], lev - 1)
                            nc.gpsimd.tensor_tensor(B.BT[:, lev % 2, :], flat(B.LT[:, :, :]),
                                                    rmask[:, 3 + lev, :], ALU.mult).then_inc(pre[s]["bt_ready"], 1)

                @block.vector
                def _(dve):
                    for s, B in enumerate(sets):
                        now = ds(2 * c * C + s * C, C)
                        for h in range(2):
                            q = slice(64 * h, 64 * h + 64)
                            nc.vector.tensor_copy(B.bB[q, :, 64 * h:64 * h + 64], R.beta[q, :, now]).then_inc(
                                pre[s]["blocks_dve"], 1)
                        for h in range(2):
                            q = slice(64 * h, 64 * h + 64)
                            nc.vector.tensor_copy(B.vB[q, :, 64 * h:64 * h + 64], R.p[q, 8:12, now]).then_inc(
                                pre[s]["blocks_dve"], 1)
                        nc.vector.tensor_copy(B.rho[:, :, :], R.rho[:, :, now]).then_inc(pre[s]["blocks_dve"], 1)
                    for s, B in enumerate(sets):
                        link = Chain(dve, pre[s]["dve"])
                        X, XT, LT = flat(B.X[:, :, :]), flat(B.XT[:, :, :]), flat(B.LT[:, :, :])
                        dve.wait_ge(pre[s]["products"], 1)
                        nc.vector.tensor_tensor(LT, T.ps[4 * s + 3][:, :], rmask[:, 0, :], ALU.mult).then_inc(
                            pre[s]["lt_ready"], 1)
                        dve.wait_ge(pre[s]["lt_ready"], 1)
                        link(nc.vector.tensor_tensor(XT, LT, rmask[:, 2, :], ALU.mult))
                        nc.vector.tensor_tensor(XT, T.ident4[:, :], XT, ALU.subtract)
                        dve.wait_ge(pre[s]["products"], 2)
                        link(nc.vector.tensor_tensor(X, T.ps[4 * s][:, :], rmask[:, 8, :], ALU.mult))
                        nc.vector.tensor_tensor(X, T.ident4[:, :], X, ALU.subtract).then_inc(pre[s]["x_ready"], 1)
                        dve.wait_ge(pre[s]["products"], 3)
                        nc.vector.tensor_tensor(flat(B.AkT[:, :, :]), T.ps[4 * s + 1][:, :], rmask[:, 0, :],
                                                ALU.mult)
                        dve.wait_ge(pre[s]["products"], 4)
                        nc.vector.tensor_tensor(B.ArT[:, :, :, :].rearrange("p a b c -> p (a b c)"),
                                                T.ps[4 * s + 2][:, :], rmask[:, 1, :], ALU.mult).then_inc(
                                                    pre[s]["masked"], 1)
                    for lev in range(LEVELS):
                        for s, B in enumerate(sets):
                            X, XT = flat(B.X[:, :, :]), flat(B.XT[:, :, :])
                            dve.wait_ge(pre[s]["xt_done"], lev + 1)
                            dve.wait_ge(pre[s]["x_ready"], lev + 1)
                            if lev < LEVELS - 1:
                                nc.vector.tensor_tensor(X, X, T.ps[4 * s][:, :], ALU.subtract)
                            nc.vector.tensor_tensor(XT, XT, T.ps[4 * s + 1][:, :], ALU.subtract).then_inc(
                                pre[s]["x_ready"], 1)

                @block.tensor
                def _(pe):
                    for s, B in enumerate(sets):
                        pe.wait_ge(pre[s]["blocks_act"], 4)
                        pe.wait_ge(pre[s]["blocks_dve"], 2)

                        def product(bank, lhs, rhs):
                            for j in range(PAIRS):
                                mm = nc.tensor.matmul(T.ps[4 * s + bank][:, pair(j)], lhs[:, j, :], rhs[:, j, :],
                                                      start=True, stop=True)
                            mm.then_inc(pre[s]["products"], 1)

                        product(3, B.bB, B.aB)
                        pe.wait_ge(pre[s]["blocks_dve"], 5)
                        for n, src in enumerate((B.bB, B.kB, B.vB)):
                            for j in range(PAIRS):
                                mm = nc.tensor.transpose(T.ps[4 * s + n][:, pair(j)], src[:, j, :], T.ident[:, :])
                            mm.then_inc(pre[s]["turned"], 1)
                        pe.wait_ge(pre[s]["turned_taken"], 1)
                        product(0, B.aB, B.bB)
                        pe.wait_ge(pre[s]["turned_taken"], 2)
                        product(1, B.kB, B.aB)
                        pe.wait_ge(pre[s]["turned_taken"], 3)
                        for n, lhs in enumerate((B.bB, B.kB)):
                            for j in range(PAIRS):
                                o = (4 * n + j) * C
                                mm = nc.tensor.matmul(T.ps[4 * s + 2][:, o:o + C], lhs[:, j, :], B.rho[:, j, :],
                                                      start=True, stop=True)
                        mm.then_inc(pre[s]["products"], 1)
                    for lev in range(LEVELS):
                        for s, B in enumerate(sets):
                            pe.wait_ge(pre[s]["bt_ready"], lev + 1)
                            pe.wait_ge(pre[s]["x_ready"], lev + 1)
                            for j in range(PAIRS):
                                mm = nc.tensor.matmul(T.ps[4 * s + 3][:, pair(j)], B.BT[:, lev % 2, pair(j)],
                                                      B.X[:, j, :], start=True, stop=True)
                            mm.then_inc(pre[s]["t1_done"], 1)
                        for s, B in enumerate(sets):
                            pe.wait_ge(pre[s]["t1_taken"], lev + 1)
                            if lev == 0:
                                pe.wait_ge(pre[s]["masked"], 1)
                            for bank, lhs, rhs in ((0, B.XT, B.T1), (1, B.T1, B.XT)):
                                if bank == 0 and lev == LEVELS - 1:
                                    continue
                                for j in range(PAIRS):
                                    mm = nc.tensor.matmul(T.ps[4 * s + bank][:, pair(j)], lhs[:, j, :],
                                                          rhs[:, j, :], start=True, stop=True)
                            mm.then_inc(pre[s]["xt_done"], 1)

            with nc.Block() as block:
                @block.sync
                def _(sync):
                    for s in range(2):
                        clear(sync, pre[s])

                @block.tensor
                def _(pe):
                    for s, B in enumerate(sets):
                        right, u, change, y = T.ps[4 * s:4 * s + 4]
                        for j in range(PAIRS):
                            nc.tensor.matmul(right[:, pair(j)], B.AkT[:, j, :], B.vT[:, j, :], start=(j == 0),
                                             stop=False)
                        if s:
                            pe.wait_ge(rec["state_ready"], s)
                        for j in range(PAIRS):
                            mm = nc.tensor.matmul(right[:, pair(j)], B.aB[:, j, :], M[:, j, :], start=False,
                                                  stop=(j == PAIRS - 1))
                        mm.then_inc(rec["right_done"], 1)
                        for j in range(PAIRS):
                            nc.tensor.matmul(change[:, pair(j)], B.kT[:, j, :], B.vT[:, j, :], start=(j == 0),
                                             stop=False)
                        pe.wait_ge(rec["right_taken"], s + 1)
                        for j in range(PAIRS):
                            mm = nc.tensor.matmul(u[:, pair(j)], B.XT[:, j, :], Rs[:, j, :], start=True, stop=True)
                        mm.then_inc(rec["u_done"], 1)
                        for j in range(PAIRS):
                            o = slice(j * C, j * C + C)
                            nc.tensor.matmul(y[:, o], M[:, j, :], B.rho[:, j, :], start=(j == 0), stop=False)
                            nc.tensor.matmul(y[:, o], B.vT[:, j, :], B.ArT[:, 1, j, :], start=False, stop=False)
                        pe.wait_ge(rec["u_taken"], s + 1)
                        for j in range(PAIRS):
                            mm = nc.tensor.matmul(change[:, pair(j)], B.bT[:, j, :], Un[:, j, :], start=False,
                                                  stop=(j == PAIRS - 1))
                        mm.then_inc(rec["change_done"], 1)
                        for j in range(PAIRS):
                            mm = nc.tensor.matmul(y[:, j * C:j * C + C], Un[:, j, :], B.ArT[:, 0, j, :],
                                                  start=False, stop=(j == PAIRS - 1))
                        mm.then_inc(rec["y_done"], 1)

                @block.scalar
                def _(act):
                    for s in range(2):
                        right, u, change, y = T.ps[4 * s:4 * s + 4]
                        act.wait_ge(rec["right_done"], s + 1)
                        nc.scalar.copy(flat(Rs[:, :, :]), right[:, :]).then_inc(rec["right_taken"], 1)
                        act.wait_ge(rec["u_done"], s + 1)
                        nc.scalar.mul(flat(Un[:, :, :]), u[:, :], -1.0).then_inc(rec["u_taken"], 1)
                        act.wait_ge(rec["y_done"], s + 1)
                        nc.scalar.copy(R.y[:, :, ds(2 * c * C + s * C, C)], y[:, 0:PAIRS * C].rearrange(
                            "p (j t) -> p j t", j=PAIRS))

                @block.vector
                def _(dve):
                    for s, B in enumerate(sets):
                        dve.wait_ge(rec["change_done"], s + 1)
                        if s:
                            dve.wait_ge(rec["state_ready"], s)
                        nc.vector.tensor_tensor(flat(M[:, :, :]), flat(M[:, :, :]), T.ps[4 * s + 2][:, :],
                                                ALU.add).then_inc(rec["dve"], 1)
                        dve.wait_ge(rec["dve"], s + 1)
                        nc.vector.tensor_tensor(M[:, :, :], M[:, :, :], B.PC[:, :, :].to_broadcast([P, PAIRS, P]),
                                                ALU.mult).then_inc(rec["state_ready"], 1)


RWKV_PRE_SEMS = ("blocks_act blocks_dve turned turned_taken t1_done t1_taken lt_ready bt_ready dve products masked x_ready "
                 "xt_done")
RWKV_REC_SEMS = "masks_loaded right_done right_taken u_done u_taken change_done y_done state_ready dve"


def rwkv_out_phase(nc, T, sems, stale, R, out, ahead):
    col = lambda name, j: T.lc[:, LCOLS[name][0] + j:LCOLS[name][0] + j + 1]
    with nc.sbuf_tensor([P, 2, S], F32) as sq, nc.sbuf_tensor([P, PAIRS, S], F32) as rstd, nc.Block() as block:
        @block.sync
        def _(sync):
            clear(sync, stale)
            fetch_both(sync, ahead)

        @block.scalar
        def _(act):
            for j in range(PAIRS):
                act.wait_ge(sems["var_done"], j + 1)
                rsqrt(act, sems["rooted"], 2 * j, rstd[:, j, :], T.ps[4 + j][:, :], 1.0 / 64, T.eps(GN_EPS))

        @block.tensor
        def _(pe):
            for j in range(PAIRS):
                nc.tensor.matmul(T.ps[j][:, :], T.head_ones[:, :], R.y[:, j, :], start=True, stop=True).then_inc(
                    sems["mean_done"], 1)
            for j in range(PAIRS):
                pe.wait_ge(sems["squared"], j + 1)
                nc.tensor.matmul(T.ps[4 + j][:, :], T.head_ones[:, :], sq[:, j % 2, :], start=True,
                                 stop=True).then_inc(sems["var_done"], 1)

        @block.vector
        def _(dve):
            link = Chain(dve, sems["dve"])
            for j in range(PAIRS):
                y = R.y[:, j, :]
                dve.wait_ge(sems["mean_done"], j + 1)
                link(nc.vector.scalar_tensor_tensor(out=y, in0=T.ps[j][:, :], scalar=-1.0 / 64, in1=y,
                                                    op0=ALU.mult, op1=ALU.add))
                if j >= 2:
                    dve.wait_ge(sems["var_done"], j - 1)
                nc.vector.tensor_tensor(sq[:, j % 2, :], y, y, ALU.mult).then_inc(sems["squared"], 1)
            for j in range(PAIRS):
                y, rs = R.y[:, j, :], rstd[:, j, :]
                dve.wait_ge(sems["rooted"], 2 * j + 2)
                link(nc.vector.scalar_tensor_tensor(out=y, in0=y, scalar=col("lnx_g", j), in1=rs,
                                                    op0=ALU.mult, op1=ALU.mult))
                link(nc.vector.scalar_tensor_tensor(out=y, in0=y, scalar=col("lnx_b", j), in1=R.bonus[:, j, :],
                                                    op0=ALU.add, op1=ALU.add))
                nc.vector.tensor_tensor(out[:, j, :], y, R.gate[:, j, :], ALU.mult)


RWKV_OUT_SEMS = "mean_done squared var_done rooted dve"


RET_SEMS = ("loaded rotated rot_summed taken scored decayed summed squared sq_summed rooted done silu dve")


def retention_phase(nc, T, sems, stale, qk, vt, g, out, ahead):
    with nc.sbuf_tensor([P, RET_HEADS, S], F32) as decay, nc.sbuf_tensor([P, 2, S], F32) as cossin, \
            nc.sbuf_tensor([P, P], F32) as rot, nc.sbuf_tensor([P, 2, S], F32) as tmp, \
            nc.sbuf_tensor([P, 4, S], F32) as sc, nc.sbuf_tensor([P, S], F32) as rstd, nc.Block() as block:
        @block.sync
        def _(sync):
            clear(sync, stale)
            sync.dma_start(cossin[:, :, :], T.dram["ret_cossin"]).then_inc(sems["loaded"], 16)
            sync.dma_start(rot[:, :], T.dram["rot"]).then_inc(sems["loaded"], 16)
            sync.dma_start(decay[:, :, :], T.dram["ret_decay"]).then_inc(sems["loaded"], 16)
            fetch_both(sync, ahead)

        @block.tensor
        def _(pe):
            pe.wait_ge(sems["loaded"], 48)
            for t in range(4):
                nc.tensor.matmul(T.ps[t][:, :], rot[:, :], qk[:, t, :], start=True, stop=True).then_inc(
                    sems["rot_summed"], 1)
            pe.wait_ge(sems["rotated"], 4)
            for h in range(RET_HEADS):
                q = slice(64 * (h % 2), 64 * (h % 2) + 64)
                for jc in range(4):
                    if h:
                        pe.wait_ge(sems["decayed"], 4 * (h - 1) + jc + 1)
                    nc.tensor.matmul(T.ps[jc][:, 0:S - jc * P], qk[q, 2 + h // 2, jc * P:jc * P + P],
                                     qk[q, h // 2, jc * P:S], start=True, stop=True).then_inc(sems["scored"], 1)
                for jc in range(4):
                    pe.wait_ge(sems["decayed"], 4 * h + jc + 1)
                    if h >= 2 and jc == 0:
                        pe.wait_ge(sems["done"], h - 1)
                    mm = nc.tensor.matmul(T.ps[4 + h % 2][:, jc * P:S], vt[:, jc, h * P:h * P + P],
                                          sc[:, jc, 0:S - jc * P], start=(jc == 0), stop=(jc == 3),
                                          skip_group_check=True)
                mm.then_inc(sems["summed"], 1)
                pe.wait_ge(sems["squared"], h + 1)
                nc.tensor.matmul(T.ps[6][:, :], T.ones[:, :], tmp[:, 1, :], start=True, stop=True).then_inc(
                    sems["sq_summed"], 1)

        @block.scalar
        def _(act):
            for h in range(RET_HEADS):
                nc.scalar.activation(g[:, h, :], g[:, h, :], ACT.Silu).then_inc(sems["silu"], 1)
            act.wait_ge(sems["rotated"], 4)
            for h in range(RET_HEADS):
                act.wait_ge(sems["summed"], h + 1)
                nc.scalar.activation(tmp[:, 1, :], T.ps[4 + h % 2][:, :], ACT.Square).then_inc(sems["squared"], 1)
                act.wait_ge(sems["sq_summed"], h + 1)
                if h:
                    act.wait_ge(sems["done"], h)
                rsqrt(act, sems["rooted"], 2 * h, rstd[:, :], T.ps[6][:, :], 1.0 / P, T.eps(EPS))

        @block.vector
        def _(dve):
            link = Chain(dve, sems["dve"])
            dve.wait_ge(sems["loaded"], 48)
            for t in range(4):
                dve.wait_ge(sems["rot_summed"], t + 1)
                if t:
                    dve.wait_ge(sems["rotated"], t)
                nc.vector.tensor_tensor(tmp[:, 0, :], T.ps[t][:, :], cossin[:, 1, :], ALU.mult)
                link(nc.vector.tensor_tensor(tmp[:, 1, :], qk[:, t, :], cossin[:, 0, :], ALU.mult))
                nc.vector.tensor_tensor(qk[:, t, :], tmp[:, 0, :], tmp[:, 1, :], ALU.add).then_inc(sems["rotated"], 1)
            dve.wait_ge(sems["silu"], 4)
            for h in range(RET_HEADS):
                if h:
                    dve.wait_ge(sems["summed"], h)
                for jc in range(4):
                    dve.wait_ge(sems["scored"], 4 * h + jc + 1)
                    n = S - jc * P
                    nc.vector.tensor_tensor(sc[:, jc, 0:n], T.ps[jc][:, 0:n], decay[:, h, 0:n], ALU.mult).then_inc(
                        sems["decayed"], 1)
                dve.wait_ge(sems["rooted"], 2 * h + 2)
                if h:
                    dve.wait_ge(sems["done"], h)
                link(nc.vector.tensor_tensor(tmp[:, 0, :], T.ps[4 + h % 2][:, :], rstd[:, :], ALU.mult))
                nc.vector.tensor_tensor(out[:, h, :], tmp[:, 0, :], g[:, h, :], ALU.mult).then_inc(sems["done"], 1)


SGU_SEMS = "loaded gelu_v gelu_u normed rooted stats mixed w_masked dve"


def sgu_phase(nc, T, sems, stale, u, vt, layer, out, ahead):
    with nc.sbuf_tensor([P, S], F32) as wsT, nc.sbuf_tensor([P, S], F32) as causal, nc.sbuf_tensor([P, 3, S], F32) as rows, \
            nc.sbuf_tensor([P, 4, 6], F32) as stats, nc.sbuf_tensor([P, 4, 2], F32) as mv, \
            nc.sbuf_tensor([P, 4], F32) as rstd, nc.sbuf_tensor([P, 2, S], F32) as tmp, nc.Block() as block:
        @block.sync
        def _(sync):
            clear(sync, stale)
            sync.dma_start(wsT[:, :], T.dram["sg_wT"][ds(layer, 1)].rearrange("l p c -> p (l c)")).then_inc(
                sems["loaded"], 16)
            sync.dma_start(causal[:, :], T.dram["causal"]).then_inc(sems["loaded"], 16)
            sync.dma_start(rows[:, :, :].rearrange("p a b -> p (a b)"),
                           T.dram["sg_rows"][ds(layer, 1), :].to_broadcast([P, 3 * S])).then_inc(sems["loaded"], 16)
            fetch_both(sync, ahead)

        @block.scalar
        def _(act):
            for m in range(4):
                nc.scalar.activation(vt[:, m, :], vt[:, m, :], ACT.Gelu).then_inc(sems["gelu_v"], 1)
            for t in range(4):
                nc.scalar.activation(u[:, t, :], u[:, t, :], ACT.Gelu).then_inc(sems["gelu_u"], 1)
            act.wait_ge(sems["stats"], 4)
            rsqrt(act, sems["rooted"], 0, rstd[:, :], mv[:, :, 1:2].rearrange("p m a -> p (m a)"), 1.0, T.eps(EPS))

        @block.vector
        def _(dve):
            link = Chain(dve, sems["dve"])
            dve.wait_ge(sems["loaded"], 48)
            nc.vector.tensor_tensor(wsT[:, :], wsT[:, :], causal[:, :], ALU.mult).then_inc(sems["w_masked"], 1)
            for m in range(4):
                dve.wait_ge(sems["gelu_v"], m + 1)
                link(nc.vector.bn_stats(stats[:, m, :], vt[:, m, :]))
                nc.vector.bn_aggr(mv[:, m, :], stats[:, m, :]).then_inc(sems["stats"], 1)
            dve.wait_ge(sems["rooted"], 2)
            for m in range(4):
                v = vt[:, m, :]
                link(nc.vector.tensor_scalar(v, v, mv[:, m, 0:1], rstd[:, m:m + 1], ALU.subtract, ALU.mult))
                link(nc.vector.tensor_tensor(v, v, rows[:, 0, :], ALU.mult))
                nc.vector.tensor_tensor(v, v, rows[:, 1, :], ALU.add).then_inc(sems["normed"], 1)
            dve.wait_ge(sems["gelu_u"], 4)
            for g in range(SG_GROUPS):
                dve.wait_ge(sems["mixed"], g + 1)
                bias = rows[:, 2, g * P:g * P + P].unsqueeze(1).to_broadcast([P, 4, P])
                link(nc.vector.tensor_tensor(tmp[:, g % 2, :].rearrange("p (m i) -> p m i", m=4),
                                             T.ps[g][:, :].rearrange("p (m i) -> p m i", m=4), bias, ALU.add))
                link(nc.vector.tensor_tensor(out[:, g, :], tmp[:, g % 2, :], u[:, g, :], ALU.mult))

        @block.tensor
        def _(pe):
            pe.wait_ge(sems["w_masked"], 1)
            pe.wait_ge(sems["normed"], 4)
            for g in range(SG_GROUPS):
                for m in range(4):
                    mm = nc.tensor.matmul(T.ps[g][:, m * P:m * P + P], vt[:, m, g * P:g * P + P],
                                          wsT[:, g * P:g * P + P], start=True, stop=True)
                mm.then_inc(sems["mixed"], 1)


MERGE_SEMS = SPLIT_SEMS + " logits_done proj_done sig_done added zeroed dve"


def merge_phase(nc, T, sems, stale, weights, hT, branches, merged, ahead):
    with ExitStack() as ctx:
        sig = ctx.enter_context(nc.sbuf_tensor("merge_sig", [P, 4, S], F32))
        split = Split(nc, ctx, T, sems, KD)
        block = ctx.enter_context(nc.Block())

        @block.sync
        def _(sync):
            clear(sync, stale)
            with sync.Fori(1, 6) as i:
                for s in range(2):
                    sync.wait_ge(sems["added"], 4 * i + 2 * s + 2)
                    sync.dma_start(T.w[:, s, 0:12 * 256], weights(2 * i + s)).then_inc(sems["w_full"][s], 16)
            for s in range(2):
                sync.wait_ge(sems["logits_done"], 2 + 22 + 2 * s)
                ahead(sync, s)

        @block.gpsimd
        def _(pool):
            for i, s in two_slots(pool, 12):
                for t in range(2):
                    split.low(pool, 4 * i + 2 * s + t, split.raw(s, t * P, 256), t)

        @block.tensor
        def _(pe):
            pe.sem_inc(sems["logits_done"], 2)
            pe.wait_ge(sems["rhs_hi"], KD)
            for b in range(3):
                with pe.Fori(0, 2) as i:
                    for s in range(2):
                        for t in range(2):
                            n = 2 * s + t
                            tile = 4 * i + 8 * b + n
                            pe.wait_ge(sems["added"], tile + 1)
                            if t == 0:
                                pe.wait_ge(sems["w_full"][s], 16 * i + 32 * b + 16)
                            for k in range(4):
                                c = (KD + k) * 256 + t * P
                                mm = nc.tensor.matmul(T.ps[2 * n + 1][:, :], T.w[:, s, c:c + P],
                                                      branches[b][:, k, :], start=(k == 0), stop=(k == 3))
                            mm.then_inc(sems["proj_done"], 1)
                            split.products(pe, T.ps[2 * n][:, :], tile, tile + 1, t).then_inc(
                                sems["logits_done"], 1)

        @block.scalar
        def _(act):
            def high(i, s, t):
                act.wait_ge(sems["w_full"][s], 16 * i + 16)
                act.wait_ge(sems["logits_done"], 4 * i + 2 * s + t + 1)
                split.high(split.raw(s, t * P, 256), t)

            high(0, 0, 0)
            high(0, 0, 1)
            for (i, s), behind in with_next(act, 12):
                for t in range(2):
                    n = 2 * s + t
                    act.wait_ge(sems["logits_done"], 4 * i + n + 3)
                    act.wait_ge(sems["added"], 4 * i + n + 1)
                    nc.scalar.activation(sig[:, n, :], T.ps[2 * n][:, :], ACT.Sigmoid).then_inc(sems["sig_done"], 1)
                    if behind:
                        high(*behind, t)

        @block.vector
        def _(dve):
            link = Chain(dve, sems["dve"])
            split.rhs(dve, hT)
            for k in range(KD):
                ms = nc.vector.memset(merged[:, k, :], 0.0)
            ms.then_inc(sems["zeroed"], 1)
            dve.wait_ge(sems["zeroed"], 1)
            dve.sem_inc(sems["added"], 4)
            for b in range(3):
                with dve.Fori(0, 2) as i:
                    for n in range(4):
                        dve.wait_ge(sems["sig_done"], 4 * i + 8 * b + n + 1)
                        dve.wait_ge(sems["proj_done"], 4 * i + 8 * b + n + 1)
                        link(nc.vector.tensor_tensor(sig[:, n, :], sig[:, n, :], T.ps[2 * n + 1][:, :], ALU.mult))
                        m = merged[:, ds(4 * i + n, 1), :].rearrange("p a t -> p (a t)")
                        nc.vector.tensor_tensor(m, m, sig[:, n, :], ALU.add).then_inc(sems["added"], 1)
                    link.restart()


FFN_UP_SEMS = SPLIT_SEMS + " loaded gate_done val_done gate_taken val_taken conv_done silu_done made dve"


def ffn_up_phase(nc, T, sems, stale, weights, layer, hT, made_hi, made_lo, ahead):
    done = (sems["gate_done"], sems["val_done"])
    with ExitStack() as ctx:
        cw = ctx.enter_context(nc.sbuf_tensor("up_taps", [P, FT, 8], F32))
        conv = ctx.enter_context(nc.sbuf_tensor("up_conv", [P, 4, S], F32))
        split = Split(nc, ctx, T, sems, KD)
        block = ctx.enter_context(nc.Block())

        @block.sync
        def _(sync):
            clear(sync, stale)
            sync.dma_start(cw[:, :, :], T.dram["ffn_conv"][ds(layer, 1)].rearrange(
                "l p j c -> p (l j) c")).then_inc(sems["loaded"], 16)
            for i, s in two_slots(sync, FT, first=1):
                sync.wait_ge(sems["w_lo"], 4 * i + 2 * s + 2)
                sync.dma_start(T.w[:, s, 0:KD * 256], weights(2 * i + s)).then_inc(sems["w_full"][s], 16)
            for s in range(2):
                sync.wait_ge(sems["w_lo"], 4 + 2 * last_chunk(FT, s) + 2)
                ahead(sync, s)

        @block.gpsimd
        def _(pool):
            pool.sem_inc(sems["w_lo"], 4)
            for i, s in two_slots(pool, FT):
                for t in range(2):
                    split.low(pool, 4 * i + 2 * s + t, split.raw(s, t * P, 256), t)

        @block.tensor
        def _(pe):
            pe.sem_inc(done[0], 1)
            pe.sem_inc(done[1], 1)
            pe.wait_ge(sems["rhs_hi"], KD)
            for i, s in two_slots(pe, FT):
                pe.wait_ge(sems["made"], 2 * i + s + 1)
                for t in range(2):
                    n = 4 * i + 2 * s + t
                    split.products(pe, T.ps[2 * s + t][:, :], n, n + 5, t).then_inc(done[t], 1)

        @block.scalar
        def _(act):
            def high(i, s, t):
                act.wait_ge(sems["w_full"][s], 16 * i + 16)
                act.wait_ge(done[t], 2 * i + s + 1)
                split.high(split.raw(s, t * P, 256), t)

            act.wait_ge(sems["loaded"], 16)
            high(0, 0, 0)
            high(0, 0, 1)
            for (i, s), behind in with_next(act, FT):
                j = 2 * i + s
                act.wait_ge(sems["made"], j + 1)
                for t in range(2):
                    if behind:
                        high(*behind, t)
                    act.wait_ge(done[t], j + 2)
                    w2 = cw[:, ds(j, 1), 4 * t + 2:4 * t + 3].rearrange("p a b -> p (a b)")
                    b = cw[:, ds(j, 1), 4 * t + 3:4 * t + 4].rearrange("p a b -> p (a b)")
                    nc.scalar.activation(conv[:, 2 * s + t, :], T.ps[2 * s + t][:, :], ACT.Identity, bias=b,
                                         scale=w2).then_inc((sems["gate_taken"], sems["val_taken"])[t], 1)
                act.wait_ge(sems["conv_done"], j + 1)
                nc.scalar.activation(conv[:, 2 * s, :], conv[:, 2 * s, :], ACT.Silu).then_inc(sems["silu_done"], 1)

        @block.vector
        def _(dve):
            link = Chain(dve, sems["dve"])
            dve.sem_inc(sems["made"], 2)
            split.rhs(dve, hT)
            dve.wait_ge(sems["loaded"], 16)
            for i, s in two_slots(dve, FT):
                j = 2 * i + s
                for t in range(2):
                    c, u = conv[:, 2 * s + t, :], T.ps[2 * s + t]
                    tap = lambda q: cw[:, ds(j, 1), 4 * t + q:4 * t + q + 1].rearrange("p a b -> p (a b)")
                    dve.wait_ge((sems["gate_taken"], sems["val_taken"])[t], j + 1)
                    link(nc.vector.scalar_tensor_tensor(out=c[:, 1:S], in0=u[:, 0:S - 1], scalar=tap(1),
                                                        in1=c[:, 1:S], op0=ALU.mult, op1=ALU.add))
                    st = nc.vector.scalar_tensor_tensor(out=c[:, 2:S], in0=u[:, 0:S - 2], scalar=tap(0),
                                                        in1=c[:, 2:S], op0=ALU.mult, op1=ALU.add)
                    if t == 0:
                        st.then_inc(sems["conv_done"], 1)
                    else:
                        link(st)
                dve.wait_ge(sems["silu_done"], j + 1)
                product = conv[:, 2 * s, :]
                hi, lo = (m[:, ds(j, 1), :].rearrange("p a t -> p (a t)") for m in (made_hi, made_lo))
                link(nc.vector.tensor_tensor(product, product, conv[:, 2 * s + 1, :], ALU.mult))
                link(nc.vector.tensor_copy(hi, product))
                nc.vector.tensor_tensor(lo, product, hi.bitcast(F32), ALU.subtract).then_inc(sems["made"], 1)
                if s == 1:
                    link.restart()


DOWN_SEMS = SPLIT_SEMS + " tile_done added"


def down_phase(nc, T, sems, stale, weights, kt, rhs, xT, parts=None):
    with ExitStack() as ctx:
        split = Split(nc, ctx, T, sems, kt, *(parts or ()))
        block = ctx.enter_context(nc.Block())

        @block.sync
        def _(sync):
            clear(sync, stale)
            for i, s in two_slots(sync, KD, first=1):
                sync.wait_ge(sems["w_lo"], 2 * i + s + 1)
                sync.dma_start(T.w[:, s, 0:kt * P], weights(2 * i + s)).then_inc(sems["w_full"][s], 16)

        @block.scalar
        def _(act):
            for i, s in two_slots(act, KD):
                act.wait_ge(sems["w_full"][s], 16 * i + 16)
                act.wait_ge(sems["tile_done"], 2 * i + s + 1)
                split.high(split.raw(s, 0, P), s)

        @block.gpsimd
        def _(pool):
            pool.sem_inc(sems["w_lo"], 2)
            for i, s in two_slots(pool, KD):
                split.low(pool, 2 * i + s, split.raw(s, 0, P), s)

        @block.tensor
        def _(pe):
            pe.sem_inc(sems["tile_done"], 2)
            if parts is None:
                pe.wait_ge(sems["rhs_hi"], kt)
            for i, s in two_slots(pe, KD):
                pe.wait_ge(sems["added"], 2 * i + s + 1)
                split.products(pe, T.ps[s][:, :], 2 * i + s, 2 * i + s + 3, s).then_inc(sems["tile_done"], 1)

        @block.vector
        def _(dve):
            dve.sem_inc(sems["added"], 2)
            if parts is None:
                split.rhs(dve, rhs)
            for i, s in two_slots(dve, KD):
                dve.wait_ge(sems["tile_done"], 2 * i + s + 3)
                x = xT[:, ds(2 * i + s, 1), :].rearrange("p a t -> p (a t)")
                nc.vector.tensor_tensor(x, x, T.ps[s][:, :], ALU.add).then_inc(sems["added"], 1)


def put(dst):
    def write(eng, c, t, psum):
        return copied(eng, dst[:, ds(2 * c + t, 1), :].rearrange("p a t -> p (a t)"), psum)
    return write


def put_tokens(dst):
    def write(eng, c, m, psum):
        return copied(eng, dst[:, m, ds(256 * c, 256)], psum)
    return write


def pick(dram, *index):
    ap = dram
    names = "abcdef"[:len(index)]
    ap = ap[tuple(ds(i, 1) for i in index)]
    return ap.rearrange(f"{' '.join(names)} p c -> p ({' '.join(names)} c)")


def shared(nc, ctx, dram):
    def sb(name, *shape):
        return ctx.enter_context(nc.sbuf_tensor(name, [P, *shape], F32))

    T = Named()
    T.dram = dram
    T.xT, T.hT = sb("xT", KD, S), sb("hT", KD, S)
    T.w = sb("w", 2, 12 * 256)
    T.ident4, T.head_ones, T.ones = sb("ident4", 4 * P), sb("head_ones", P), sb("ones", P)
    T.lc, T.scalars = sb("layer_cols", NLCOL), sb("scalars", 4)
    T.ident = T.ident4[:, 0:P]
    T.eps = lambda e: T.scalars[:, (EPS, GN_EPS, LN_EPS).index(e):][:, 0:1]
    T.half_17ln2 = T.scalars[:, 3:4]
    T.ps = [ctx.enter_context(nc.psum_tensor(f"bank{i}", [P, 512], F32)) for i in range(8)]
    return T


def pick4(dram, i):
    return dram[ds(i, 1)].rearrange("l p a c -> p (l a) c")


def shared_sems(nc, ctx):
    return {name: sem_set(nc, ctx, name, names) for name, names in (
        ("start", "loaded"), ("stored", "done"), ("head", "loaded"), ("norm", NORM_SEMS),
        ("norm2", NORM_SEMS), ("pa", PROJECT_SEMS), ("pb", PROJECT_SEMS), ("down", DOWN_SEMS))}


def block_one(nc, T):
    with ExitStack() as ctx:
        layers(nc, ctx, T)


def layers(nc, ctx, T):
    ss = lambda prefix, names: sem_set(nc, ctx, prefix, names)
    head, norm, pa, pb, down = (T.sems[n] for n in ("head", "norm", "pa", "pb", "down"))
    prep, pre, rec, rout = (ss("prep", RWKV_PREP_SEMS), (ss("pre0", RWKV_PRE_SEMS), ss("pre1", RWKV_PRE_SEMS)), ss("rec", RWKV_REC_SEMS),
                            ss("rout", RWKV_OUT_SEMS))
    ret, sgu, merge, up = (ss("ret", RET_SEMS), ss("sgu", SGU_SEMS), ss("merge", MERGE_SEMS),
                           ss("up", FFN_UP_SEMS))
    rec["stale"] = prep
    d = T.dram
    xT = T.xT

    with nc.Fori(0, DEPTH) as layer:
        with nc.Block() as block:
            @block.sync
            def _(sync):
                clear(sync, T.sems["start"])
                clear(sync, down)
                sync.dma_start(T.lc[:, :], pick(d["layer_cols"], layer)).then_inc(head["loaded"], 16)
                sync.wait_ge(head["loaded"], 16)
        hT = T.hT
        gain = lambda name: T.lc[:, LCOLS[name][0]:LCOLS[name][1]]
        w_in = lambda first: (lambda c: pick(d["w_in"], layer, c + first))
        chunk = KD * 256
        project_first = lambda first: fetch_first(T, pa, chunk, w_in(first))
        token_first = lambda first: fetch_first(T, pb, chunk, w_in(first))
        w_merge, w_out, ffn_up, ffn_down = ((lambda c, w=d[n]: pick(w, layer, c))
                                            for n in ("w_merge", "w_out", "ffn_up", "ffn_down"))
        norm_phase(nc, T, norm, head, xT, gain("norm1_g"), hT, ahead=project_first(0))
        with ExitStack() as branch:
            def keep_branch(name, *shape):
                return branch.enter_context(nc.sbuf_tensor(name, [P, *shape], F32))

            y_rw = keep_branch("y_rw", 4, S)
            with ExitStack() as rw:
                R = Named()
                R.up = lambda: pick4(d["rw_up"], layer)
                R.beta, R.kappa, R.alpha, R.rho, R.run, R.gate, R.bonus = (
                    rw.enter_context(nc.sbuf_tensor("rw_" + n, [P, PAIRS, S], F32))
                    for n in ("beta", "kappa", "alpha", "rho", "run", "gate", "bonus"))
                R.p = rw.enter_context(nc.sbuf_tensor("rw_p", [P, RW_T, S], F32))
                R.y = y_rw
                project_phase(nc, T, pa, norm, w_in(0), 7, hT, put(R.p))
                rwkv_prep_phase(nc, T, prep, pa, R)
                rwkv_chunk_phases(nc, T, pre, rec, R)
                rwkv_out_phase(nc, T, rout, rec, R, y_rw, project_first(7))
            y_ret, y_sg = keep_branch("y_ret", 4, S), keep_branch("y_sg", 4, S)
            with nc.sbuf_tensor([P, 4, S], F32) as qk, nc.sbuf_tensor([P, 4, S], F32) as vt, \
                    nc.sbuf_tensor([P, 4, S], F32) as g:
                project_phase(nc, T, pa, rout, w_in(7), 2, hT, put(qk), ahead=token_first(9))
                token_project_phase(nc, T, pb, pa, w_in(9), 2, hT, put_tokens(vt), ahead=project_first(11))
                project_phase(nc, T, pa, pb, w_in(11), 2, hT, put(g))
                retention_phase(nc, T, ret, pa, qk, vt, g, y_ret, project_first(13))
            with nc.sbuf_tensor([P, 4, S], F32) as u, nc.sbuf_tensor([P, 4, S], F32) as vt:
                project_phase(nc, T, pa, ret, w_in(13), 2, hT, put(u), ahead=token_first(15))
                token_project_phase(nc, T, pb, pa, w_in(15), 2, hT, put_tokens(vt))
                sgu_phase(nc, T, sgu, pb, u, vt, layer, y_sg,
                          fetch_first(T, merge, 12 * 256, w_merge))
            with nc.sbuf_tensor([P, KD, S], F32) as merged:
                merge_phase(nc, T, merge, sgu, w_merge, hT, (y_rw, y_ret, y_sg), merged,
                            fetch_first(T, down, KD * P, w_out))
                down_phase(nc, T, down, merge, w_out, KD, merged, xT)
        norm_phase(nc, T, norm, down, xT, gain("norm2_g"), hT, ahead=fetch_first(T, up, chunk, ffn_up))
        with nc.sbuf_tensor([P, FT, S], F32R) as made_hi, nc.sbuf_tensor([P, FT, S], F32R) as made_lo:
            ffn_up_phase(nc, T, up, norm, ffn_up, layer, hT, made_hi, made_lo,
                         fetch_first(T, down, FT * P, ffn_down))
            down_phase(nc, T, down, up, ffn_down, FT, None, xT,
                       parts=(made_hi, made_lo))


CONV_SEMS = "loaded sig sums_done squared sq_done rooted half dve silu"


def conv_phase(nc, T, sems, stale, ag, out, ahead):
    half = CONV_KERNEL // 2
    with nc.sbuf_tensor([P, 2, S + 2 * half], F32) as padded, nc.sbuf_tensor([P, 2, S], F32) as acc, \
            nc.sbuf_tensor([P, 2, CONV_KERNEL + 3], F32) as par, nc.sbuf_tensor([P, 2, S], F32) as sq, \
            nc.sbuf_tensor([P, S], F32) as rstd, nc.Block() as block:
        @block.sync
        def _(sync):
            clear(sync, stale)
            sync.dma_start(par[:, :, :], T.dram["conv_par"]).then_inc(sems["loaded"], 16)
            fetch_both(sync, ahead)

        @block.scalar
        def _(act):
            for t in range(2):
                nc.scalar.activation(ag[:, 2 + t, :], ag[:, 2 + t, :], ACT.Sigmoid).then_inc(sems["sig"], 1)
            act.wait_ge(sems["sq_done"], 1)
            rsqrt(act, sems["rooted"], 0, rstd[:, :], T.ps[1][:, :], 1.0 / CONV_CH, T.eps(LN_EPS))
            for t in range(2):
                act.wait_ge(sems["half"], 3 + t)
                nc.scalar.activation(out[:, t, :], acc[:, t, :], ACT.Silu)

        @block.vector
        def _(dve):
            link = Chain(dve, sems["dve"])
            link(nc.vector.memset(padded[:, :, :], 0.0))
            dve.wait_ge(sems["loaded"], 16)
            dve.wait_ge(sems["sig"], 2)
            for t in range(2):
                link(nc.vector.tensor_tensor(padded[:, t, half:half + S], ag[:, t, :], ag[:, 2 + t, :], ALU.mult))
            for t in range(2):
                nc.vector.tensor_scalar(acc[:, t, :], padded[:, t, 0:S], par[:, t, 0:1],
                                        par[:, t, CONV_KERNEL:CONV_KERNEL + 1], ALU.mult, ALU.add).then_inc(
                    sems["dve"], 1)
            for j in range(1, CONV_KERNEL):
                for t in range(2):
                    dve.wait_ge(sems["dve"], link.n + 1)
                    nc.vector.scalar_tensor_tensor(out=acc[:, t, :], in0=padded[:, t, j:j + S],
                                                   scalar=par[:, t, j:j + 1], in1=acc[:, t, :], op0=ALU.mult,
                                                   op1=ALU.add).then_inc(sems["dve"], 1)
                    link.n += 1
            dve.wait_ge(sems["dve"], link.n + 2)
            link.n += 2
            dve.sem_inc(sems["half"], 1)
            dve.wait_ge(sems["sums_done"], 1)
            for t in range(2):
                link(nc.vector.scalar_tensor_tensor(out=acc[:, t, :], in0=T.ps[0][:, :], scalar=-1.0 / CONV_CH,
                                                    in1=acc[:, t, :], op0=ALU.mult, op1=ALU.add))
                nc.vector.tensor_tensor(sq[:, t, :], acc[:, t, :], acc[:, t, :], ALU.mult).then_inc(sems["squared"], 1)
            dve.wait_ge(sems["rooted"], 2)
            dve.sem_inc(sems["half"], 1)
            for t in range(2):
                link(nc.vector.scalar_tensor_tensor(out=acc[:, t, :], in0=acc[:, t, :],
                                                    scalar=par[:, t, CONV_KERNEL + 1:CONV_KERNEL + 2],
                                                    in1=rstd[:, :], op0=ALU.mult, op1=ALU.mult))
                nc.vector.tensor_scalar(acc[:, t, :], acc[:, t, :], par[:, t, CONV_KERNEL + 2:CONV_KERNEL + 3],
                                        None, ALU.add).then_inc(sems["half"], 1)

        @block.tensor
        def _(pe):
            pe.wait_ge(sems["half"], 1)
            for t in range(2):
                mm = nc.tensor.matmul(T.ps[0][:, :], T.ones[:, :], acc[:, t, :], start=(t == 0), stop=(t == 1))
            mm.then_inc(sems["sums_done"], 1)
            for t in range(2):
                pe.wait_ge(sems["squared"], t + 1)
                mm = nc.tensor.matmul(T.ps[1][:, :], T.ones[:, :], sq[:, t, :], start=(t == 0), stop=(t == 1))
            mm.then_inc(sems["sq_done"], 1)


ROPE_SEMS = "loaded dve reduced tables turned half_done pool done"


def rope_phase(nc, T, sems, stale, qk, tiles):
    with nc.sbuf_tensor([P, S], mybir.dt.int32) as pos_i, nc.sbuf_tensor([P, 1], F32) as inv, \
            nc.sbuf_tensor([P, S], F32) as ang, nc.sbuf_tensor([P, S], F32) as turns, \
            nc.sbuf_tensor([P, 2, S], F32) as table, nc.sbuf_tensor([P, P], F32) as rot, \
            nc.sbuf_tensor([P, 4, S], F32) as tmp, nc.Block() as block:
        @block.sync
        def _(sync):
            clear(sync, stale)
            sync.dma_start(pos_i[:, :], T.dram["positions"].to_broadcast([P, S])).then_inc(sems["loaded"], 16)
            sync.dma_start(inv[:, :], T.dram["rope_inv"]).then_inc(sems["loaded"], 16)
            sync.dma_start(rot[:, :], T.dram["rot"]).then_inc(sems["loaded"], 16)

        @block.vector
        def _(dve):
            link = Chain(dve, sems["dve"])
            dve.wait_ge(sems["loaded"], 48)
            link(nc.vector.tensor_copy(ang[:, :], pos_i[:, :]))
            link(nc.vector.tensor_scalar(ang[:, :], ang[:, :], inv[:, 0:1], None, ALU.mult))
            for n, shift in enumerate((np.pi / 2, 0.0)):
                r = table[:, n, :]
                link(nc.vector.tensor_scalar(turns[:, :], ang[:, :], float(shift), float(1 / (2 * np.pi)), ALU.add,
                                             ALU.mult))
                link(nc.vector.tensor_scalar(turns[:, :], turns[:, :], 12582912.0, None, ALU.add))
                link(nc.vector.tensor_scalar(turns[:, :], turns[:, :], -12582912.0, None, ALU.add))
                link(nc.vector.scalar_tensor_tensor(out=r, in0=turns[:, :], scalar=-TWO_PI[0], in1=ang[:, :],
                                                    op0=ALU.mult, op1=ALU.add))
                for part in TWO_PI[1:]:
                    link(nc.vector.scalar_tensor_tensor(out=r, in0=turns[:, :], scalar=-part, in1=r,
                                                        op0=ALU.mult, op1=ALU.add))
                link(nc.vector.tensor_scalar(r, r, float(shift), None, ALU.add))
                link(nc.vector.tensor_scalar(r, r, 3.1415925, -3.1415925, ALU.min, ALU.max))
            dve.sem_inc(sems["reduced"], 1)
            dve.wait_ge(sems["tables"], 2)
            with dve.Fori(0, tiles // 4) as i:
                for b in range(4):
                    dve.wait_ge(sems["turned"], 4 * i + b + 1)
                    nc.vector.tensor_tensor(tmp[:, b, :], T.ps[b][:, :], table[:, 1, :], ALU.mult).then_inc(
                        sems["half_done"], 1)
                for b in range(4):
                    x = qk[:, ds(4 * i + b, 1), :].rearrange("p a t -> p (a t)")
                    dve.wait_ge(sems["half_done"], 4 * i + b + 1)
                    dve.wait_ge(sems["pool"], 4 * i + b + 1)
                    nc.vector.tensor_tensor(x, x, tmp[:, b, :], ALU.add).then_inc(sems["done"], 1)
                dve.wait_ge(sems["done"], 4 * i + 4)

        @block.gpsimd
        def _(pool):
            pool.wait_ge(sems["tables"], 2)
            with pool.Fori(0, tiles // 4) as i:
                for b in range(4):
                    x = qk[:, ds(4 * i + b, 1), :].rearrange("p a t -> p (a t)")
                    pool.wait_ge(sems["turned"], 4 * i + b + 1)
                    nc.gpsimd.tensor_tensor(x, x, table[:, 0, :], ALU.mult).then_inc(sems["pool"], 1)

        @block.scalar
        def _(act):
            act.wait_ge(sems["reduced"], 1)
            for n in range(2):
                nc.scalar.activation(table[:, n, :], table[:, n, :], ACT.Sin).then_inc(sems["tables"], 1)

        @block.tensor
        def _(pe):
            pe.wait_ge(sems["loaded"], 48)
            with pe.Fori(0, tiles // 4) as i:
                for b in range(4):
                    x = qk[:, ds(4 * i + b, 1), :].rearrange("p a t -> p (a t)")
                    nc.tensor.matmul(T.ps[b][:, :], rot[:, :], x, start=True, stop=True).then_inc(sems["turned"], 1)
                pe.wait_ge(sems["half_done"], 4 * i + 4)


ATT_SEMS = ("loaded qk_staged v_staged scored scaled maxed exped normed dve turned act_took dve_took summed put")


def attention_phase(nc, T, sems, stale, q, k, k_first, v, out, groups, q_tiles, keys, scale, mask=None, ahead=None):
    kt = keys // P
    vc = q_tiles * P
    wide = q_tiles > 1
    with nc.sbuf_tensor([P, q_tiles, S], F32) as qs, nc.sbuf_tensor([P, kt, vc], F32) as vs, \
            nc.sbuf_tensor([P, q_tiles, keys], F32) as ks, \
            nc.sbuf_tensor([P, 2, 4, keys], F32) as sc, nc.sbuf_tensor([P, kt, S], F32) as pT, \
            nc.sbuf_tensor([P, 2, 3, 4], F32) as st, nc.Block() as block:
        @block.sync
        def _(sync):
            clear(sync, stale)
            fetch_both(sync, ahead)

        @block.gpsimd
        def _(pool):
            def stage_qk(g):
                nc.gpsimd.tensor_copy(qs[:, :, :], q[:, ds(q_tiles * g, q_tiles), :]).then_inc(
                    sems["qk_staged"], 1)
                nc.gpsimd.tensor_copy(ks[:, :, :], k[:, ds(q_tiles * g + k_first, q_tiles), :]).then_inc(
                    sems["qk_staged"], 1)

            def stage_v(g):
                nc.gpsimd.tensor_copy(vs[:, :, :], v[:, :, ds(vc * g, vc)]).then_inc(sems["v_staged"], 1)

            stage_qk(0)
            stage_v(0)
            with pool.Fori(0, groups - 1) as g:
                pool.wait_ge(sems["scored"], 8 * g + 8)
                stage_qk(g + 1)
                pool.wait_ge(sems["summed"], 2 * g + 2)
                stage_v(g + 1)

        def rows(u):
            return slice(0, P) if wide else slice(64 * u, 64 * u + 64)

        @block.tensor
        def _(pe):
            def scores(g, u, tiles_m):
                pe.wait_ge(sems["qk_staged"], 2 * g + 2)
                for m in tiles_m:
                    pe.wait_ge(sems["scaled"], 8 * g + 4 * u + m + 1)
                    tiles = (2 * u, 2 * u + 1) if wide else (0,)
                    for n in tiles:
                        mm = nc.tensor.matmul(T.ps[m % 2][:, 0:keys], qs[rows(u), n, m * P:m * P + P],
                                              ks[rows(u), n, :], start=(n == tiles[0]), stop=(n == tiles[-1]))
                    mm.then_inc(sems["scored"], 1)

            scores(0, 0, range(4))
            for (g, u), behind in with_next(pe, 2 * groups):
                if behind:
                    scores(*behind, (0, 1))
                pe.wait_ge(sems["normed"], 2 * g + u + 1)
                pe.wait_ge(sems["act_took"], 2 * g + u + 1)
                pe.wait_ge(sems["dve_took"], 2 * g + u + 1)
                for j in range(kt):
                    for m in range(4):
                        mm = nc.tensor.transpose(T.ps[2 + j][:, m * P:m * P + P], sc[:, u, m, j * P:j * P + P],
                                                 T.ident[:, :])
                mm.then_inc(sems["turned"], 1)
                if behind:
                    scores(*behind, (2, 3))
                pe.wait_ge(sems["act_took"], 2 * g + u + 2)
                pe.wait_ge(sems["dve_took"], 2 * g + u + 2)
                pe.wait_ge(sems["v_staged"], g + 1)
                pe.wait_ge(sems["put"], 2 * g + u + 1)
                for e in range(2 if wide else 1):
                    o = T.ps[6 + e][:, :] if wide else T.ps[6 + u][rows(u), :]
                    c = (2 * u + e) * P if wide else 64 * u
                    n = P if wide else 64
                    for j in range(kt):
                        mm = nc.tensor.matmul(o, vs[:, j, c:c + n], pT[:, j, :], start=(j == 0),
                                              stop=(j == kt - 1))
                mm.then_inc(sems["summed"], 1)

        @block.vector
        def _(dve):
            link = Chain(dve, sems["dve"])

            def scaled(g, u, tiles_m):
                for m in tiles_m:
                    dve.wait_ge(sems["scored"], 8 * g + 4 * u + m + 1)
                    s = sc[:, u, m, :]
                    if mask is None:
                        ins = nc.vector.tensor_scalar(s, T.ps[m % 2][:, 0:keys], scale, None, ALU.mult)
                    else:
                        ins = nc.vector.scalar_tensor_tensor(out=s, in0=T.ps[m % 2][:, 0:keys], scalar=scale,
                                                             in1=mask[:, m, :], op0=ALU.mult, op1=ALU.add)
                    ins.then_inc(sems["scaled"], 1)
                    dve.wait_ge(sems["scaled"], 8 * g + 4 * u + m + 3)
                    link(nc.vector.reduce_max(st[:, u, 0, m:m + 1], s, AX.X))

            def negated(g, u):
                nc.vector.tensor_scalar(st[:, u, 0, :], st[:, u, 0, :], -1.0, None, ALU.mult).then_inc(
                    sems["maxed"], 1)

            dve.sem_inc(sems["scaled"], 2)
            dve.sem_inc(sems["dve_took"], 1)
            scaled(0, 0, range(4))
            negated(0, 0)
            link.restart()
            for (g, u), behind in with_next(dve, 2 * groups):
                dve.wait_ge(sems["exped"], 8 * g + 4 * u + 4)
                link(nc.vector.reciprocal(st[:, u, 2, :], st[:, u, 1, :]))
                for m in range(4):
                    s = sc[:, u, m, :]
                    ins = nc.vector.tensor_scalar(s, s, st[:, u, 2, m:m + 1], None, ALU.mult)
                    if m < 3:
                        link(ins)
                ins.then_inc(sems["normed"], 1)
                if behind:
                    scaled(*behind, (0, 1))
                dve.wait_ge(sems["turned"], 2 * g + u + 1)
                for j in range(1, kt, 2):
                    ins = nc.vector.tensor_copy(pT[:, j, :], T.ps[2 + j][:, :])
                    if j < kt - 1:
                        link(ins)
                ins.then_inc(sems["dve_took"], 1)
                if behind:
                    scaled(*behind, (2, 3))
                    negated(*behind)
                if u == 1:
                    link.restart()

        @block.scalar
        def _(act):
            def exps(g, u):
                act.wait_ge(sems["maxed"], 2 * g + u + 1)
                for m in range(4):
                    s = sc[:, u, m, :]
                    nc.scalar.activation(s, s, ACT.Exp, bias=st[:, u, 0, m:m + 1],
                                         accum_out=st[:, u, 1, m:m + 1]).then_inc(sems["exped"], 1)

            act.sem_inc(sems["act_took"], 1)
            act.sem_inc(sems["put"], 1)
            exps(0, 0)
            for (g, u), behind in with_next(act, 2 * groups):
                act.wait_ge(sems["turned"], 2 * g + u + 1)
                for j in range(0, kt, 2):
                    ins = nc.scalar.copy(pT[:, j, :], T.ps[2 + j][:, :])
                    if j < kt - 2:
                        ins.then_inc(sems["loaded"], 1)
                if kt > 2:
                    act.wait_ge(sems["loaded"], 2 * g + u + 1)
                ins.then_inc(sems["act_took"], 1)
                if behind:
                    exps(*behind)
                act.wait_ge(sems["summed"], 2 * g + u + 1)
                if wide:
                    for e in range(2):
                        o = out[:, ds(4 * g + 2 * u + e, 1), :].rearrange("p a t -> p (a t)")
                        ins = nc.scalar.copy(o, T.ps[6 + e][:, :])
                        if e == 0:
                            ins.then_inc(sems["loaded"], 1)
                            act.wait_ge(sems["loaded"], 2 * g + u + 1)
                else:
                    o = out[rows(u), ds(g, 1), :].rearrange("p a t -> p (a t)")
                    ins = nc.scalar.copy(o, T.ps[6 + u][rows(u), :])
                ins.then_inc(sems["put"], 1)


ROUTE_SEMS = "loaded turned act_took dve_took logits dve exp_in exped ranks counted ready"


def route_phase(nc, T, sems, stale, hT, M, moe):
    E, G = N_EXPERTS, N_GROUPS
    W = G + E
    with ExitStack() as ctx:
        def sb(name, *shape):
            return ctx.enter_context(nc.sbuf_tensor(f"route_{name}", [P, *shape], F32))

        wr, bias, lg, iota = sb("w", KD, W), sb("bias", W), sb("logits", 4, W), sb("iota", E)
        before = sb("before", P)
        ge, gt, goh, pg = sb("gexp", 4, G), sb("gtie", 4, G), sb("ghot", 4, G), sb("pg", 4, 1)
        em, tie, oh1, oh2 = sb("em", 4, E), sb("tie", 4, E), sb("hot1", 4, E), sb("hot2", 4, E)
        m0, m1, m2, t1, t2, g1, g2 = (sb(n, 4, 1) for n in "m0 m1 m2 t1 t2 g1 g2".split())
        chosen, pm, many = sb("chosen", 4, E), sb("pairmax", E // 2), sb("many", MOE_ROUNDS - 1, E // 2)
        block = ctx.enter_context(nc.Block())

        @block.sync
        def _(sync):
            clear(sync, stale)
            sync.dma_start(wr[:, :, :], T.dram["router_w"]).then_inc(sems["loaded"], 16)
            sync.dma_start(bias[:, :], T.dram["router_b"].to_broadcast([P, W])).then_inc(sems["loaded"], 16)
            sync.dma_start(iota[:, :], T.dram["iota"][:, 0:E]).then_inc(sems["loaded"], 16)
            sync.dma_start(before[:, :], T.dram["before"]).then_inc(sems["loaded"], 16)
            sync.dma_start(M.slots[:, :], T.dram["iota"]).then_inc(sems["loaded"], 16)
            for _ in fetch_up(sync, T, moe, M, 0):
                pass
            fetch_down(sync, T, moe, M, 0)

        @block.tensor
        def _(pe):
            pe.wait_ge(sems["loaded"], 80)
            for m in range(4):
                for k in range(KD):
                    mm = nc.tensor.matmul(T.ps[7][:, m * W:m * W + W], hT[:, k, m * P:m * P + P], wr[:, k, :],
                                          start=(k == 0), stop=(k == KD - 1))
            mm.then_inc(sems["logits"], 1)
            for m in range(4):
                for half in range(2):
                    if m >= 2:
                        pe.wait_ge((sems["act_took"], sems["dve_took"])[half], m - 1)
                    for k in range(4):
                        mm = nc.tensor.transpose(T.ps[2 * (m % 2) + half][:, k * P:k * P + P],
                                                 hT[:, 4 * half + k, m * P:m * P + P], T.ident[:, :])
                    mm.then_inc(sems["turned"], 1)
            pe.wait_ge(sems["ready"], 1)
            for m in range(4):
                for n in range(m + 1):
                    mm = nc.tensor.matmul(T.ps[5][:, m * E:m * E + E], (before if n == m else T.ones)[:, :],
                                          chosen[:, n, :], start=(n == 0), stop=(n == m))
            mm.then_inc(sems["ranks"], 1)
            for n in range(4):
                mm = nc.tensor.matmul(T.ps[6][:, 0:E], T.ones[:, :], chosen[:, n, :], start=(n == 0), stop=(n == 3))
            mm.then_inc(sems["counted"], 1)

        @block.scalar
        def _(act):
            act.wait_ge(sems["exp_in"], 1)
            nc.scalar.activation(ge[:, :, :], ge[:, :, :], ACT.Exp).then_inc(sems["exped"], 1)
            for m in range(4):
                act.wait_ge(sems["turned"], 2 * m + 1)
                nc.scalar.copy(M.h_tok[:, m, 0:512], T.ps[2 * (m % 2)][:, :]).then_inc(sems["act_took"], 1)
            act.wait_ge(sems["exp_in"], 2)
            nc.scalar.activation(t1[:, :, :], t1[:, :, :], ACT.Exp).then_inc(sems["exped"], 1)

        @block.vector
        def _(dve):
            link = Chain(dve, sems["dve"])
            v = nc.vector
            dve.wait_ge(sems["loaded"], 80)
            dve.wait_ge(sems["logits"], 1)
            link(v.tensor_tensor(lg[:, :, :], T.ps[7][:, 0:4 * W].rearrange("p (m w) -> p m w", m=4),
                                 bias[:, :].unsqueeze(1).to_broadcast([P, 4, W]), ALU.add))
            gl, el = lg[:, :, 0:G], lg[:, :, G:W]

            def first_max(x, width, best, tie_, hot):
                link(v.tensor_reduce(best[:, :, :], x, AX.X, ALU.max))
                link(v.tensor_tensor(tie_[:, :, :], x, best[:, :, :].to_broadcast([P, 4, width]), ALU.is_equal))
                link(v.tensor_scalar(tie_[:, :, :], tie_[:, :, :], -100.0, None, ALU.mult))
                link(v.tensor_tensor(tie_[:, :, :], tie_[:, :, :],
                                     iota[:, 0:width].unsqueeze(1).to_broadcast([P, 4, width]), ALU.add))
                link(v.tensor_reduce(t2[:, :, :], tie_[:, :, :], AX.X, ALU.min))
                link(v.tensor_tensor(hot[:, :, :], tie_[:, :, :], t2[:, :, :].to_broadcast([P, 4, width]),
                                     ALU.is_equal))

            first_max(gl, G, m0, gt, goh)
            v.tensor_tensor(ge[:, :, :], gl, m0[:, :, :].to_broadcast([P, 4, G]), ALU.subtract).then_inc(
                sems["exp_in"], 1)
            link(v.tensor_scalar(gt[:, :, :], goh[:, :, :], 1e30, -1e30, ALU.mult, ALU.add))
            for g in range(G):
                q = slice(8 * g, 8 * g + 8)
                link(v.tensor_tensor(em[:, :, q], el[:, :, q], gt[:, :, g:g + 1].to_broadcast([P, 4, 8]), ALU.add))
            first_max(em[:, :, :], E, m1, tie, oh1)
            link(v.tensor_scalar(tie[:, :, :], oh1[:, :, :], -2e30, None, ALU.mult))
            link(v.tensor_tensor(em[:, :, :], em[:, :, :], tie[:, :, :], ALU.add))
            first_max(em[:, :, :], E, m2, tie, oh2)
            v.tensor_tensor(t1[:, :, :], m2[:, :, :], m1[:, :, :], ALU.subtract).then_inc(sems["exp_in"], 1)
            v.tensor_tensor(chosen[:, :, :], oh1[:, :, :], oh2[:, :, :], ALU.add).then_inc(sems["ready"], 1)
            for m in range(4):
                dve.wait_ge(sems["turned"], 2 * m + 2)
                v.tensor_copy(M.h_tok[:, m, 512:1024], T.ps[2 * (m % 2) + 1][:, :]).then_inc(sems["dve_took"], 1)
            dve.wait_ge(sems["exped"], 2)
            link(v.tensor_reduce(pg[:, :, :], ge[:, :, :], AX.X, ALU.add))
            link(v.reciprocal(pg[:, :, :], pg[:, :, :]))
            link(v.tensor_scalar(g1[:, :, :], t1[:, :, :], 1.0, None, ALU.add))
            link(v.reciprocal(g1[:, :, :], g1[:, :, :]))
            link(v.tensor_tensor(g1[:, :, :], g1[:, :, :], pg[:, :, :], ALU.mult))
            link(v.tensor_tensor(g2[:, :, :], g1[:, :, :], t1[:, :, :], ALU.mult))
            link(v.tensor_tensor(oh1[:, :, :], oh1[:, :, :], g1[:, :, :].to_broadcast([P, 4, E]), ALU.mult))
            link(v.tensor_tensor(oh2[:, :, :], oh2[:, :, :], g2[:, :, :].to_broadcast([P, 4, E]), ALU.mult))
            link(v.tensor_tensor(M.gates[:, :, :], oh1[:, :, :], oh2[:, :, :], ALU.add))
            link(v.tensor_scalar(tie[:, :, :], chosen[:, :, :], -BIG, BIG, ALU.mult, ALU.add))
            dve.wait_ge(sems["ranks"], 1)
            link(v.tensor_tensor(M.place[:, :, :], T.ps[5][:, 0:4 * E].rearrange("p (m e) -> p m e", m=4),
                                 tie[:, :, :], ALU.add))
            dve.wait_ge(sems["counted"], 1)
            link(v.tensor_reduce(pm[:, :], T.ps[6][:, 0:E].rearrange("p (g u) -> p g u", u=2), AX.X, ALU.max))
            for r in range(1, MOE_ROUNDS):
                link(v.tensor_scalar(many[:, r - 1, :], pm[:, :], float(SLOTS * r), None, ALU.is_gt))
            link(v.tensor_copy(M.again[:, 1:], flat(many[:, :, :])))
            link(v.tensor_reduce(t2[:, 0, :], many[:, 0, :], AX.X, ALU.max))
            link(v.tensor_copy(M.again[:, 0:1], t2[:, 0, :]))


MOE_SEMS = ("up_full*2 w2_full staged sel_ready selg_ready selT_done selT_taken gathered hg_act hg_dve up_half up_done "
            "silu_done made mid_turned midT_taken down_done y_act y_dve scattered added")


def fetch_up(sync, T, sems, M, n):
    D1 = M.w1.shape[2]
    for h in range(2):
        for u in range(2):
            e, c = 2 * n + u, slice(h * D1 // 2, (h + 1) * D1 // 2)
            for w, name in ((M.w1, "moe_w1"), (M.w3, "moe_w3")):
                sync.dma_start(w[:, u, c], pick(T.dram[name], e)[:, c]).then_inc(sems["up_full"][h], 16)
        yield h


def fetch_down(sync, T, sems, M, n):
    for u in range(2):
        sync.dma_start(M.w2[:, u, :], pick(T.dram["moe_w2"], 2 * n + u)).then_inc(sems["w2_full"], 16)


def experts_phase(nc, T, sems, stale, M, pairs, first_pair, fetched=0):
    W2 = 2 * SLOTS
    w1, w3, w2 = M.w1, M.w3, M.w2
    with ExitStack() as ctx:
        def sb(name, *shape):
            return ctx.enter_context(nc.sbuf_tensor(f"moe_{name}_{nc.next_id()}", [P, *shape], F32))

        sel, selg, selT = sb("sel", 4, W2), sb("selg", 4, W2), sb("selT", S)
        hg, sil, mid, midT, y = sb("hg", KD, W2), sb("silu", 512), sb("mid", 512), sb("midT", 4, W2), sb("y", D)
        place, gate = sb("pair_place", 4, 2), sb("pair_gate", 4, 2)
        block = ctx.enter_context(nc.Block())
        up_banks, y_banks, hg_banks, add_banks = T.ps[0:2], T.ps[2:4], T.ps[4:6], T.ps[6:8]

        def half_of(u):
            return slice(SLOTS * u, SLOTS * u + SLOTS)

        def in_loop(eng, n, first=0):
            if n - first == 1:
                yield first
            elif n - first > 1:
                with eng.Fori(first, n) as g:
                    yield g

        def pairs_and_more(eng):
            for g in in_loop(eng, pairs - 1):
                yield g, True
            yield pairs - 1, False

        @block.sync
        def _(sync):
            clear(sync, stale)
            for g in in_loop(sync, pairs, fetched):
                sync.wait_ge(sems["up_half"], g + 1)
                for h in fetch_up(sync, T, sems, M, g + first_pair):
                    if h == 0:
                        sync.wait_ge(sems["up_done"], g + 1)
                sync.wait_ge(sems["down_done"], 2 * g + 2)
                fetch_down(sync, T, sems, M, g + first_pair)

        @block.gpsimd
        def _(pool):
            def select(n):
                nc.gpsimd.tensor_copy(place[:, :, :], M.place[:, :, ds(2 * n + 2 * first_pair, 2)]).then_inc(
                    sems["staged"], 1)
                pool.wait_ge(sems["staged"], 1)
                pool.sem_clear(sems["staged"])
                for m in range(4):
                    for u in range(2):
                        ins = nc.gpsimd.tensor_scalar(sel[:, m, half_of(u)], M.slots[:, :], place[:, m, u:u + 1],
                                                      None, ALU.is_equal)
                ins.then_inc(sems["sel_ready"], 1)

            def select_gates(n):
                nc.gpsimd.tensor_copy(gate[:, :, :], M.gates[:, :, ds(2 * n + 2 * first_pair, 2)]).then_inc(
                    sems["staged"], 1)
                pool.wait_ge(sems["staged"], 1)
                pool.sem_clear(sems["staged"])
                for m in range(4):
                    for u in range(2):
                        ins = nc.gpsimd.tensor_scalar(selg[:, m, half_of(u)], M.slots[:, :], place[:, m, u:u + 1],
                                                      gate[:, m, u:u + 1], ALU.is_equal, ALU.mult)
                ins.then_inc(sems["selg_ready"], 1)

            select(0)
            select_gates(0)
            for g in in_loop(pool, pairs - 1):
                pool.wait_ge(sems["gathered"], 2 * g + 2)
                pool.wait_ge(sems["selg_ready"], g + 1)
                select(g + 1)
                pool.wait_ge(sems["selT_done"], g + 1)
                select_gates(g + 1)

        @block.tensor
        def _(pe):
            def gather(n):
                pe.wait_ge(sems["sel_ready"], n + 1)
                pe.wait_ge(sems["hg_act"], n + 1)
                pe.wait_ge(sems["hg_dve"], n + 1)
                for k in range(KD):
                    for m in range(4):
                        mm = nc.tensor.matmul(hg_banks[k // 4][:, (k % 4) * P:(k % 4) * P + P],
                                              M.h_tok[:, m, k * P:k * P + P], sel[:, m, :], start=(m == 0),
                                              stop=(m == 3))
                    if k % 4 == 3:
                        mm.then_inc(sems["gathered"], 1)

            def up(n):
                pe.wait_ge(sems["hg_act"], n + 2)
                pe.wait_ge(sems["hg_dve"], n + 2)
                pe.wait_ge(sems["selT_taken"], n + 1)
                for k in range(KD):
                    if k % 4 == 0:
                        pe.wait_ge(sems["up_full"][k // 4], 64 * n + 64)
                    for w, bank in ((w1, up_banks[0]), (w3, up_banks[1])):
                        for u in range(2):
                            mm = nc.tensor.matmul(bank[half_of(u), :], hg[:, k, half_of(u)],
                                                  w[:, u, k * 512:k * 512 + 512], start=(k == 0),
                                                  stop=(k == KD - 1))
                    if k == 3:
                        mm.then_inc(sems["up_half"], 1)
                mm.then_inc(sems["up_done"], 1)

            for name, credit in (("hg_act", 1), ("hg_dve", 1), ("selT_taken", 1), ("up_half", 1), ("up_done", 1),
                                 ("down_done", 2), ("y_act", 1), ("y_dve", 1), ("added", 2)):
                pe.sem_inc(sems[name], credit)
            gather(0)
            up(0)
            for g, more in pairs_and_more(pe):
                if more:
                    gather(g + 1)
                pe.wait_ge(sems["made"], g + 1)
                for f in range(4):
                    mm = nc.tensor.transpose(up_banks[0][:, f * P:f * P + P], mid[:, f * P:f * P + P],
                                             T.ident[:, :])
                mm.then_inc(sems["mid_turned"], 1)
                pe.wait_ge(sems["selg_ready"], g + 1)
                for m in range(4):
                    mm = nc.tensor.transpose(up_banks[1][:, m * P:m * P + P], selg[:, m, :], T.ident[:, :])
                mm.then_inc(sems["selT_done"], 1)
                pe.wait_ge(sems["midT_taken"], g + 1)
                pe.wait_ge(sems["w2_full"], 32 * g + 32)
                for half, free in ((0, "y_act"), (1, "y_dve")):
                    pe.wait_ge(sems[free], g + 1)
                    for f in range(4):
                        for u in range(2):
                            c = f * D + half * 512
                            mm = nc.tensor.matmul(y_banks[half][half_of(u), :], midT[:, f, half_of(u)],
                                                  w2[:, u, c:c + 512], start=(f == 0), stop=(f == 3))
                    mm.then_inc(sems["down_done"], 1)
                if more:
                    up(g + 1)
                else:
                    pe.wait_ge(sems["selT_taken"], g + 2)
                pe.wait_ge(sems["y_act"], g + 2)
                pe.wait_ge(sems["y_dve"], g + 2)
                for k in range(KD):
                    pe.wait_ge(sems["added"], KD * g + k + 1)
                    nc.tensor.matmul(add_banks[k % 2][:, :], y[:, k * P:k * P + P], selT[:, :], start=True,
                                     stop=True).then_inc(sems["scattered"], 1)

        @block.scalar
        def _(act):
            def rows(n):
                act.wait_ge(sems["gathered"], 2 * n + 1)
                nc.scalar.copy(flat(hg[:, 0:4, :]), hg_banks[0][:, :]).then_inc(sems["hg_act"], 1)

            def silu(n):
                act.wait_ge(sems["up_done"], n + 2)
                nc.scalar.activation(sil[:, :], up_banks[0][:, :], ACT.Silu).then_inc(sems["silu_done"], 1)

            rows(0)
            silu(0)
            for g, more in pairs_and_more(act):
                if more:
                    rows(g + 1)
                act.wait_ge(sems["mid_turned"], g + 1)
                nc.scalar.copy(flat(midT[:, :, :]), up_banks[0][:, :]).then_inc(sems["midT_taken"], 1)
                act.wait_ge(sems["selT_done"], g + 1)
                nc.scalar.copy(selT[:, :], up_banks[1][:, :]).then_inc(sems["selT_taken"], 1)
                act.wait_ge(sems["down_done"], 2 * g + 3)
                nc.scalar.copy(y[:, 0:512], y_banks[0][:, :]).then_inc(sems["y_act"], 1)
                if more:
                    silu(g + 1)

        @block.vector
        def _(dve):
            def rows(n):
                dve.wait_ge(sems["gathered"], 2 * n + 2)
                nc.vector.tensor_copy(flat(hg[:, 4:8, :]), hg_banks[1][:, :]).then_inc(sems["hg_dve"], 1)

            def gated(n):
                dve.wait_ge(sems["silu_done"], n + 1)
                nc.vector.tensor_tensor(mid[:, :], sil[:, :], up_banks[1][:, :], ALU.mult).then_inc(sems["made"], 1)

            rows(0)
            gated(0)
            for g, more in pairs_and_more(dve):
                if more:
                    rows(g + 1)
                dve.wait_ge(sems["down_done"], 2 * g + 4)
                nc.vector.tensor_copy(y[:, 512:1024], y_banks[1][:, :]).then_inc(sems["y_dve"], 1)
                for k in range(KD):
                    if k == 1 and more:
                        gated(g + 1)
                    dve.wait_ge(sems["scattered"], KD * g + k + 1)
                    nc.vector.tensor_tensor(T.xT[:, k, :], T.xT[:, k, :], add_banks[k % 2][:, :],
                                            ALU.add).then_inc(sems["added"], 1)


def gains_phase(nc, sems, stale, dst, src):
    with nc.Block() as block:
        @block.sync
        def _(sync):
            clear(sync, stale)
            sync.dma_start(dst, src).then_inc(sems["loaded"], 16)
            sync.wait_ge(sems["loaded"], 16)


def next_places_phase(nc, stale, M):
    with nc.Block() as block:
        @block.sync
        def _(sync):
            clear(sync, stale)

        @block.vector
        def _(dve):
            nc.vector.tensor_scalar(M.place[:, :, :], M.place[:, :, :], float(-SLOTS), None, ALU.add)


def block_two(nc, T):
    sems, d, xT, hT = T.sems, T.dram, T.xT, T.hT
    norm, norm2, pa, pb, down, head = (sems[n] for n in ("norm", "norm2", "pa", "pb", "down", "head"))
    gain = lambda name: T.g2[:, GCOLS[name][0]:GCOLS[name][1]]
    with ExitStack() as ctx:
        conv, rope, att = (sem_set(nc, ctx, n, names) for n, names in (("conv", CONV_SEMS), ("rope", ROPE_SEMS),
                                                                      ("att", ATT_SEMS)))
        T.g2 = ctx.enter_context(nc.sbuf_tensor("gains2", [P, NGCOL], F32))
        gains_phase(nc, head, down, T.g2[:, :], d["gains2"])
        norm_phase(nc, T, norm, head, xT, gain("final_g"), xT)
        chunk = KD * 256
        part = lambda name, first=0: (lambda c: pick(d[name], c + first))
        norm_phase(nc, T, norm2, norm, xT, gain("mix_norm_g_2"), hT, ahead=fetch_first(T, pa, chunk, part("w_in_2")))
        with nc.sbuf_tensor([P, KD, S], F32) as mixed:
            with nc.sbuf_tensor([P, 6, S], F32) as att_out, nc.sbuf_tensor([P, 2, S], F32) as conv_out:
                with nc.sbuf_tensor([P, 4, S], F32) as ag:
                    project_phase(nc, T, pa, norm2, part("w_in_2"), 2, hT, put(ag))
                    conv_phase(nc, T, conv, pa, ag, conv_out, fetch_first(T, pa, chunk, part("w_in_2", 2)))
                with nc.sbuf_tensor([P, 12, S], F32) as qk, nc.sbuf_tensor([P, 4, 768], F32) as vt, \
                        nc.sbuf_tensor([P, 4, S], F32) as mask:
                    project_phase(nc, T, pa, conv, part("w_in_2", 2), 6, hT, put(qk),
                                  load=lambda sync, sem: sync.dma_start(mask[:, :, :], d["att_mask"]).then_inc(
                                      sem, 16), ahead=fetch_first(T, pb, chunk, part("w_in_2", 8)))
                    token_project_phase(nc, T, pb, pa, part("w_in_2", 8), 3, hT, put_tokens(vt))
                    rope_phase(nc, T, rope, pb, qk, 12)
                    attention_phase(nc, T, att, rope, qk, qk, 6, vt, att_out, 6, 1, S, HEAD_DIM ** -0.5, mask)
                norm_phase(nc, T, norm, att, conv_out, gain("conv_out_g_2"), mixed[:, 0:2, :], tiles=2)
                norm_phase(nc, T, norm2, norm, att_out, gain("attn_out_g_2"), mixed[:, 2:8, :], tiles=6,
                           ahead=fetch_first(T, down, KD * P, part("w_out_2")))
            down_phase(nc, T, down, norm2, part("w_out_2"), KD, mixed, xT)
        norm_phase(nc, T, norm, down, xT, gain("xattn_norm_g_2"), hT)
        with nc.sbuf_tensor([P, KD, MEM_LEN], F32) as mem, nc.sbuf_tensor([P, KD, MEM_LEN], F32) as mem_k, \
                nc.sbuf_tensor([P, 2, D], F32) as mem_v, nc.sbuf_tensor([P, KD, S], F32) as ox:
            norm_phase(nc, T, norm2, norm, mem, gain("mem_norm_g_2"), mem, width=MEM_LEN, eps=EPS,
                       load=lambda sync, sem: sync.dma_start(mem[:, :, :], d["memT"]).then_inc(sem, 16),
                       ahead=fetch_first(T, pa, chunk, part("w_xk_2")))
            project_phase(nc, T, pa, norm2, part("w_xk_2"), 4, mem, put(mem_k), width=MEM_LEN,
                          ahead=fetch_first(T, pb, chunk, part("w_xv_2")))
            token_project_phase(nc, T, pb, pa, part("w_xv_2"), 4, mem, put_tokens(mem_v), tiles=2,
                                ahead=fetch_first(T, pa, chunk, part("w_xq_2")))
            with nc.sbuf_tensor([P, KD, S], F32) as q:
                project_phase(nc, T, pa, pb, part("w_xq_2"), 4, hT, put(q))
                attention_phase(nc, T, att, pa, q, mem_k, 0, mem_v, ox, 2, 4, MEM_LEN, 256 ** -0.5,
                                ahead=fetch_first(T, down, KD * P, part("w_xo_2")))
            down_phase(nc, T, down, att, part("w_xo_2"), KD, ox, xT)
        norm_phase(nc, T, norm, down, xT, gain("moe_norm_g_2"), hT)
    with ExitStack() as ctx:
        route, moe = sem_set(nc, ctx, "route", ROUTE_SEMS), sem_set(nc, ctx, "moe", MOE_SEMS)
        T.g2 = ctx.enter_context(nc.sbuf_tensor("gains2b", [P, NGCOL], F32))

        def sb(name, *shape, dt=F32):
            return ctx.enter_context(nc.sbuf_tensor("moe_" + name, [P, *shape], dt))

        M = Named()
        M.h_tok = sb("h", 4, D)
        M.gates, M.place = sb("gates", 4, N_EXPERTS), sb("place", 4, N_EXPERTS)
        M.slots = sb("slots", SLOTS)
        M.again = sb("again", 1 + (MOE_ROUNDS - 1) * N_EXPERTS // 2, dt=mybir.dt.int32)
        M.w1, M.w3, M.w2 = sb("w1", 2, 8 * 512), sb("w3", 2, 8 * 512), sb("w2", 2, 4 * D)
        route_phase(nc, T, route, norm, hT, M, moe)
        experts_phase(nc, T, moe, route, M, N_EXPERTS // 2, 0, fetched=1)
        gains_phase(nc, head, moe, T.g2[:, :], d["gains2"])
        again = nc.values_load(M.again[0:1, 0:1], min_val=0, max_val=1)
        with nc.If(again > 0):
            with nc.Fori(0, MOE_ROUNDS - 1) as r:
                next_places_phase(nc, head, M)
                with nc.Fori(0, N_EXPERTS // 2) as pair:
                    needed = nc.values_load(M.again[0:1, ds(1 + N_EXPERTS // 2 * r + pair, 1)], min_val=0,
                                            max_val=1)
                    with nc.If(needed > 0):
                        experts_phase(nc, T, moe, head, M, 1, pair)
                        with nc.Block() as block:
                            @block.sync
                            def _(sync):
                                clear(sync, moe)
        norm_phase(nc, T, norm2, head, xT, gain("final_norm_g_2"), hT)


def two_blocks(nc, dram, out):
    with ExitStack() as ctx:
        T = shared(nc, ctx, dram)
        T.sems = shared_sems(nc, ctx)
        start = T.sems["start"]
        with nc.Block() as block:
            @block.sync
            def _(sync):
                loads = [(T.xT[:, :, :], dram["xT"]), (T.ident4[:, :], dram["ident4"]),
                         (T.head_ones[:, :], dram["head_ones"]), (T.scalars[:, :], dram["scalars"])]
                for dst, src in loads:
                    sync.dma_start(dst, src).then_inc(start["loaded"], 16)
                sync.wait_ge(start["loaded"], 16 * len(loads))

            @block.gpsimd
            def _(pool):
                nc.gpsimd.memset(T.ones[:, :], 1.0)

        block_one(nc, T)
        block_two(nc, T)
        with nc.Block() as block:
            @block.sync
            def _(sync):
                clear(sync, T.sems["norm2"])
                sync.dma_start(out, T.hT[:, :, :]).then_inc(T.sems["stored"]["done"], 16)
                sync.wait_ge(T.sems["stored"]["done"], 16)


def by_feature(v):
    v = np.asarray(v)
    return np.ascontiguousarray(np.swapaxes(v.reshape(v.shape[:-1] + (v.shape[-1] // P, P)), -1, -2))


def weight_chunks(w, cols):
    w = np.asarray(w)
    lead, (k, n) = w.shape[:-2], w.shape[-2:]
    w = w.reshape(lead + (k // P, P, n // cols, cols))
    m = len(lead)
    w = w.transpose(tuple(range(m)) + (m + 2, m + 1, m, m + 3))
    return np.ascontiguousarray(w).reshape(lead + (n // cols, P, k // P * cols))


def shape_constants():
    f4 = np.float32
    s = np.arange(P)
    head, tok = s // C, s % C
    same = head[:, None] == head[None, :]
    strict = (same & (tok[:, None] < tok[None, :])).astype(f4)
    upto = (tok[:, None] <= np.arange(C)[None, :]).astype(f4)
    masks = [np.tile(strict, (1, PAIRS)), np.tile(upto, (1, 2 * PAIRS))]
    for size in [1 << n for n in range(LEVELS + 1)]:
        m = same & (tok[:, None] // (2 * size) == tok[None, :] // (2 * size)) & \
            (tok[:, None] // size % 2 == 0) & (tok[None, :] // size % 2 == 1)
        masks.append(np.tile(m.astype(f4), (1, PAIRS)))
        if size == 1:
            first = m.astype(f4)
    masks.append(np.tile(first.T, (1, PAIRS)))
    return {
        "ident4": np.tile(np.eye(P, dtype=f4), (1, 4)),
        "head_ones": same.astype(f4),
        "chunk_start": np.tile((np.arange(S) % C != 0).astype(f4), (P, 1)),
        "scalars": np.tile(np.array([[EPS, GN_EPS, LN_EPS, 8.5 * np.log(2.0)]], f4), (P, 1)),
        "rmask": np.stack(masks, 1).astype(f4),
    }


def ret_tables():
    f4 = np.float32
    inv = 1.0 / (f4(10000.0) ** np.linspace(0.0, 1.0, 32, dtype=f4))
    ang = (np.arange(S, dtype=f4)[:, None] * inv[None, :]).astype(f4)
    rep = lambda t: np.tile(t.T, (4, 1))
    rot = np.zeros((P, P), f4)
    for q in range(P):
        if q % 64 < 32:
            rot[q + 32, q] = -1.0
        else:
            rot[q - 32, q] = 1.0
    gamma = np.log(f4(1.0) - f4(2.0) ** (f4(-5.0) - np.arange(RET_HEADS, dtype=f4))).astype(np.float64)
    diff = np.arange(S)[None, :] - np.arange(P)[:, None]
    decay = np.where(diff[:, None, :] >= 0, np.exp(np.maximum(diff, 0)[:, None, :] * gamma[None, :, None]), 0.0)
    return {"ret_cossin": np.stack([rep(np.cos(ang)), rep(np.sin(ang))], 1).astype(f4), "rot": rot,
            "ret_decay": (decay * 64 ** -0.5).astype(f4)}


def layout(a):
    a = {k: np.asarray(v) for k, v in a.items()}
    L = DEPTH
    flat2 = lambda n: a[n].reshape(L, -1)
    out = shape_constants()
    out["layer_cols"] = np.concatenate(
        [by_feature(flat2(n)) for n in ("norm1_g", "rw_mu", "rw_w0", "rw_a0", "rw_k_k", "rw_k_a", "rw_r_k",
                                        "rw_lnx_g", "rw_lnx_b", "norm2_g")], axis=-1)
    low = np.concatenate([a["rw_w_up"], a["rw_a_up"]], axis=1)
    out.update(ret_tables())
    x = a["x"][0]
    out["xT"] = np.ascontiguousarray(x.reshape(S, KD, P).transpose(2, 1, 0))
    w_in = weight_chunks(a["w_in"], 256)
    first_gate = (RW_T * P + 1536 + 1024) // 256
    gates = w_in[:, first_gate:]
    out["w_in"] = w_in[:, :first_gate]
    out["w_merge"] = np.concatenate([gates, weight_chunks(a["w_branch"], 256).reshape(L, 12, P, -1)], axis=-1)
    out["w_out"] = weight_chunks(a["w_out"], P)
    up = a["ffn_w_up"]
    gate, val = (weight_chunks(up[:, :, o:o + D_FF], P).reshape(L, FT, P, KD, P) for o in (0, D_FF))
    out["ffn_up"] = np.concatenate([gate, val], axis=-1).reshape(L, FT, P, KD * 256)
    out["ffn_down"] = weight_chunks(a["ffn_w_down"], P)
    taps = np.concatenate([a["ffn_conv_w"], a["ffn_conv_b"][:, None]], axis=1)
    taps = taps.reshape(L, 4, 2, FT, P).transpose(0, 4, 3, 2, 1)
    out["ffn_conv"] = np.ascontiguousarray(taps).reshape(L, P, FT, 8)
    out["sg_wT"] = np.ascontiguousarray(a["sg_w_s"].transpose(0, 3, 1, 2)).reshape(L, P, S)
    out["sg_rows"] = np.concatenate([a["sg_ln_g"], a["sg_ln_b"], a["sg_b"].reshape(L, -1)], axis=-1)
    out["causal"] = np.tile((np.arange(P)[:, None] <= np.arange(P)[None, :]).astype(np.float32), (1, 4))
    out["gains2"] = np.concatenate([by_feature(a[n].reshape(-1)) for n in GCOLS], axis=-1)
    out["w_in_2"] = weight_chunks(a["w_in_2"][0], 256)
    for n in ("w_xq_2", "w_xk_2", "w_xv_2"):
        out[n] = weight_chunks(a[n][0], 256)
    for n in ("w_out_2", "w_xo_2"):
        out[n] = weight_chunks(a[n][0], P)
    par = np.concatenate([a["conv_dw_w_2"][0], a["conv_dw_b_2"], a["conv_ln_g_2"], a["conv_ln_b_2"]], axis=0)
    out["conv_par"] = np.ascontiguousarray(par.reshape(CONV_KERNEL + 3, 2, P).transpose(2, 1, 0))
    out["positions"] = a["positions_2"].reshape(1, S)
    out["memT"] = np.ascontiguousarray(a["mem_2"][0].reshape(MEM_LEN, KD, P).transpose(2, 1, 0))
    inv = 1.0 / (np.float32(10000.0) ** (np.arange(32, dtype=np.float32) * np.float32(2.0 / 64)))
    out["rope_inv"] = np.tile(inv.astype(np.float32), 4)[:, None]
    off = np.abs(np.arange(S)[:, None] - np.arange(S)[None, :])
    seen = (off <= 64).astype(int) + ((off <= 256) & (off % 4 == 0)) + (off % 16 == 0)
    mask = np.where(seen > 0, np.log(np.maximum(seen, 1)), -1e30).astype(np.float32)
    out["att_mask"] = np.ascontiguousarray(mask.reshape(4, P, S).transpose(1, 0, 2))
    out["router_w"] = np.ascontiguousarray(np.concatenate([a["w_group_2"][0], a["w_router_2"][0]], axis=-1).reshape(
        KD, P, -1).transpose(1, 0, 2))
    out["router_b"] = np.concatenate([a["b_group_2"], a["b_router_2"]], axis=-1)
    out["iota"] = np.tile(np.arange(SLOTS, dtype=np.float32), (P, 1))
    out["before"] = (np.arange(P)[:, None] < np.arange(P)[None, :]).astype(np.float32)
    for n in ("w1_2", "w3_2", "w2_2"):
        w = a[n][0]
        out["moe_" + n[:2]] = np.ascontiguousarray(w.reshape(N_EXPERTS, -1, P, w.shape[-1]).transpose(
            0, 2, 1, 3)).reshape(N_EXPERTS, P, -1)
    out["rw_up"] = np.stack([low, a["rw_g_up"]], axis=2)
    return out


def kernel(**inputs):
    import concourse.bacc as bacc
    from concourse.bass_utils import run_bass_kernel_spmd

    nc = bacc.Bacc("TRN2", target_bir_lowering=False, num_devices=1)
    arrays = {f"in_{name}": a for name, a in layout(inputs).items()}
    dram = {name[3:]: nc.dram_tensor(name, a.shape, mybir.dt.from_np(a.dtype), kind="ExternalInput").ap()
            for name, a in arrays.items()}
    out = nc.dram_tensor("out", (P, KD, S), F32, kind="ExternalOutput").ap()
    two_blocks(nc, dram, out)
    got = run_bass_kernel_spmd(nc, [arrays], core_ids=[0]).results[0]["out"]
    return np.ascontiguousarray(got.transpose(2, 1, 0)).reshape(1, S, D)
```
